# Optimizing a Trainium2 kernel written in Bass

```python
import math
import jax
import jax.numpy as jnp
from jax import lax

D_MODEL = 1024
BATCH = 1
SEQ = 256
DEPTH = 2
DEC_BATCH = 8
DEC_SEQ = 4
PAST_LEN = 1024
PAGE_SIZE = 128

HEAD_DIM = 64
H_SB = 4
H_GDN = 4
H_MOBA = 4
H_DIL_G = 2
DIL_PATTERN = ((128, 1), (512, 4), (2048, 16))
N_DIL_GROUPS = 3
H_DIL = H_DIL_G * N_DIL_GROUPS
W_SB = H_SB * HEAD_DIM
W_GDN = H_GDN * HEAD_DIM
W_MOBA = H_MOBA * HEAD_DIM
W_DIL = H_DIL * HEAD_DIM
W_DIL_OUT = H_DIL_G * HEAD_DIM
N_BRANCH = 4
IN_COLS = 3 * W_SB + 4 * W_GDN + 2 * H_GDN + 3 * W_MOBA + 3 * W_DIL + N_BRANCH * D_MODEL
CONV_W = 4
GDN_CHUNK = 64
MOBA_BLOCK = 256
MOBA_TOPK = 3
MOBA_QCHUNK = 32
SB_QBLOCK = 128
DIL_QBLOCK = 64
REL_BUCKETS = 32
REL_MAX_DIST = 2048
N_REL_HEADS = H_MOBA + H_DIL
D_FF = 2816
N_EXPERTS = 8
TOP_K = 2
D_EXPERT = 3584
N_DENSE = (DEPTH + 1) // 2
N_MOE = DEPTH // 2
EPS = 1e-6

kernel_name = 'hybrid_gated_parallel_decoder_step'

def _rmsnorm(x, g):
    xf = x.astype(jnp.float32)
    y = xf * lax.rsqrt(jnp.mean(xf * xf, axis=-1, keepdims=True) + EPS)
    return (y * g.astype(jnp.float32)).astype(x.dtype)

def _l2norm(x):
    xf = x.astype(jnp.float32)
    return xf * lax.rsqrt(jnp.sum(xf * xf, axis=-1, keepdims=True) + EPS)

def _in_offsets():
    sizes = (3 * W_SB, 3 * W_GDN, W_GDN, H_GDN, H_GDN, 3 * W_MOBA, 3 * W_DIL)
    offs, acc = [], 0
    for s in sizes:
        acc += s
        offs.append(acc)
    return offs

def _t5_bucket(dist):
    dist = jnp.maximum(dist, 0)
    exact = REL_BUCKETS // 2
    d = jnp.maximum(dist, exact).astype(jnp.float32)
    log_b = exact + (jnp.log(d / exact) / math.log(REL_MAX_DIST / exact) * (REL_BUCKETS - exact)).astype(jnp.int32)
    return jnp.where(dist < exact, dist, jnp.minimum(log_b, REL_BUCKETS - 1))

def _sweep(fn, q, q_pos, block):
    B, T = q.shape[0], q.shape[1]
    n = T // block
    qb = jnp.moveaxis(q.reshape((B, n, block) + q.shape[2:]), 1, 0)
    pb = q_pos.reshape(n, block)
    out = lax.map(lambda a: fn(a[0], a[1]), (qb, pb))
    return jnp.moveaxis(out, 0, 1).reshape((B, T) + out.shape[3:])

def _gather_pages(pool, page_table):
    g = pool[page_table]
    return g.reshape((g.shape[0], g.shape[1] * g.shape[2]) + g.shape[3:])

def _sb_attend(q, k, v, q_pos):
    z = jnp.einsum('bqhd,bkhd->bhqk', q, k).astype(jnp.float32) * (HEAD_DIM ** -0.5)
    k_pos = jnp.arange(k.shape[1], dtype=jnp.int32)
    past = k_pos[None, :] < q_pos[:, None]
    log_keep = jnp.where(past, jax.nn.log_sigmoid(-z), 0.0)
    tail = lax.cumsum(log_keep, axis=3, reverse=True) - log_keep
    w = jnp.where(past, jnp.exp(jax.nn.log_sigmoid(z) + tail), 0.0)
    return jnp.einsum('bhqk,bkhd->bqhd', w.astype(v.dtype), v)

def _causal_conv(x, state, w):
    T = x.shape[1]
    xx = jnp.concatenate([state.astype(x.dtype), x], axis=1)
    y = xx[:, 0:T] * w[0]
    for i in range(1, CONV_W):
        y = y + xx[:, i:i + T] * w[i]
    return y, xx[:, T:]

def _gated_delta(q, k, v, g, beta, s0, chunk):
    f32 = jnp.float32
    B, T, H, _ = q.shape
    dv = v.shape[-1]
    n = T // chunk

    def chunks(a):
        a = a.astype(f32).reshape((B, n, chunk, H) + a.shape[3:])
        return jnp.moveaxis(a, (1, 3), (0, 2))

    qc, kc, vc, gc, bc = chunks(q), chunks(k), chunks(v), chunks(g), chunks(beta)
    G = jnp.cumsum(gc, axis=-1)
    i = jnp.arange(chunk)
    causal = i[:, None] >= i[None, :]
    strict = i[:, None] > i[None, :]
    gamma = jnp.exp(jnp.where(causal, G[..., :, None] - G[..., None, :], -jnp.inf))
    kb = kc * bc[..., None]
    m = jnp.where(strict, jnp.einsum('nbhid,nbhjd->nbhij', kb, kc) * gamma, 0.0)
    eye = jnp.eye(chunk, dtype=f32)
    tinv = lax.linalg.triangular_solve(eye + m, jnp.broadcast_to(eye, m.shape), left_side=True,
                                       lower=True, unit_diagonal=True)
    u = tinv @ (vc * bc[..., None])
    w = tinv @ (kb * jnp.exp(G)[..., None])
    qk = jnp.where(causal, jnp.einsum('nbhid,nbhjd->nbhij', qc, kc) * gamma, 0.0)
    qg = qc * jnp.exp(G)[..., None]
    kt = kc * jnp.exp(G[..., -1:] - G)[..., None]
    glast = jnp.exp(G[..., -1])

    def step(s, xs):
        u_i, w_i, qk_i, qg_i, kt_i, gl_i = xs
        v_new = u_i - w_i @ s
        o_i = qg_i @ s + qk_i @ v_new
        s = s * gl_i[..., None, None] + jnp.swapaxes(kt_i, -1, -2) @ v_new
        return s, o_i

    s, o = lax.scan(step, s0.astype(f32), (u, w, qk, qg, kt, glast))
    o = jnp.moveaxis(o, (0, 2), (1, 3)).reshape(B, T, H, dv)
    return o, s

def _moba_attend(q, kbh, vbh, kmean, q_pos, bias_tab):
    f32 = jnp.float32
    B, Tq, H, dh = q.shape
    nb = kmean.shape[1]
    K, BLK = MOBA_TOPK, MOBA_BLOCK
    own = q_pos[0] // BLK
    gate = jnp.einsum('bqhd,bnhd->bqhn', q, kmean).astype(f32)
    gate = jnp.where(jnp.arange(nb) < own, gate, -jnp.inf)
    _, sel = lax.top_k(gate, K)
    valid = jnp.arange(K) < own
    sel = jnp.moveaxis(sel, 2, 1)
    flat = sel.reshape(B, H, Tq * K, 1, 1)
    k_sel = jnp.take_along_axis(kbh, flat, axis=2).reshape(B, H, Tq, K, BLK, dh)
    v_sel = jnp.take_along_axis(vbh, flat, axis=2).reshape(B, H, Tq, K, BLK, dh)
    k_own = lax.dynamic_index_in_dim(kbh, own, axis=2, keepdims=False)
    v_own = lax.dynamic_index_in_dim(vbh, own, axis=2, keepdims=False)
    qh = jnp.moveaxis(q, 2, 1)
    scale = dh ** -0.5
    off = jnp.arange(BLK, dtype=jnp.int32)
    dist_sel = q_pos[None, None, :, None, None] - (sel[..., None] * BLK + off)
    dist_own = q_pos[:, None] - (own * BLK + off)[None, :]
    bt = bias_tab.T.astype(f32)
    b_sel = bt[jnp.arange(H)[None, :, None, None, None], _t5_bucket(dist_sel)]
    b_own = bt[:, _t5_bucket(dist_own)]
    s_sel = jnp.einsum('bhqd,bhqikd->bhqik', qh, k_sel).astype(f32) * scale + b_sel
    s_sel = jnp.where(valid[:, None], s_sel, -jnp.inf).reshape(B, H, Tq, K * BLK)
    s_own = jnp.einsum('bhqd,bhkd->bhqk', qh, k_own).astype(f32) * scale + b_own[None]
    s_own = jnp.where(dist_own >= 0, s_own, -jnp.inf)
    p = jax.nn.softmax(jnp.concatenate([s_sel, s_own], axis=-1), axis=-1).astype(vbh.dtype)
    o = (jnp.einsum('bhqik,bhqikd->bhqd', p[..., :K * BLK].reshape(B, H, Tq, K, BLK), v_sel)
         + jnp.einsum('bhqk,bhkd->bhqd', p[..., K * BLK:], v_own))
    return jnp.moveaxis(o, 1, 2)

def _dil_group(q, k_src, v_src, q_pos, k_pos0, window, dil, bias_tab):
    f32 = jnp.float32
    n_keys = window // dil + 1
    dist = jnp.arange(n_keys, dtype=jnp.int32) * dil
    kpos = q_pos[:, None] - dist[None, :]
    valid = kpos >= 0
    idx = jnp.clip(kpos - k_pos0, 0, k_src.shape[1] - 1)
    kg = jnp.take(k_src, idx, axis=1)
    vg = jnp.take(v_src, idx, axis=1)
    bias = bias_tab.astype(f32)[_t5_bucket(dist)].T
    s = jnp.einsum('bqhd,bqmhd->bqhm', q, kg).astype(f32) * (HEAD_DIM ** -0.5) + bias
    s = jnp.where(valid[None, :, None, :], s, -jnp.inf)
    mx = jnp.max(s, axis=-1, keepdims=True)
    p = jnp.exp(s - mx)
    den = jnp.sum(p, axis=-1, keepdims=True)
    o = jnp.einsum('bqhm,bqmhd->bqhd', (p / den).astype(vg.dtype), vg).astype(f32)
    return o, (mx + jnp.log(den))[..., 0]

def _dil_attend(q, srcs, q_pos, bias_tab):
    outs, lses = [], []
    for g in range(N_DIL_GROUPS):
        win, dil = DIL_PATTERN[g]
        ks, vs, p0 = srcs[g]
        hs = slice(g * H_DIL_G, (g + 1) * H_DIL_G)
        o, lse = _dil_group(q[:, :, hs], ks, vs, q_pos, p0, win, dil, bias_tab[:, hs])
        outs.append(o)
        lses.append(lse)
    w = jax.nn.softmax(jnp.stack(lses), axis=0)
    o = outs[0] * w[0][..., None]
    for g in range(1, N_DIL_GROUPS):
        o = o + outs[g] * w[g][..., None]
    return o.astype(q.dtype)

def _mixer(h, l, q_pos, past, W):
    f32 = jnp.float32
    B, T, _ = h.shape
    dt = h.dtype
    proj = h @ W['w_in'][l]
    sb_qkv, gdn_qkv, gdn_z, gdn_a, gdn_b, moba_qkv, dil_qkv, gate_in = jnp.split(proj, _in_offsets(), axis=-1)

    def heads(a, n):
        return a.reshape(B, T, n, HEAD_DIM)

    sq, sk, sv = (heads(a, H_SB) for a in jnp.split(sb_qkv, 3, axis=-1))
    sb_new = jnp.stack([sk, sv], axis=2)
    if past is None:
        o_sb = _sweep(lambda qb, pb: _sb_attend(qb, sk, sv, pb), sq, q_pos, SB_QBLOCK)
    else:
        pkv = past['sb']
        o_sb = _sb_attend(sq, jnp.concatenate([pkv[:, :, 0], sk], axis=1),
                          jnp.concatenate([pkv[:, :, 1], sv], axis=1), q_pos)
    o_sb = o_sb.reshape(B, T, W_SB)

    conv_state = jnp.zeros((B, CONV_W - 1, 3 * W_GDN), dt) if past is None else past['conv']
    c, conv_new = _causal_conv(gdn_qkv, conv_state, W['gdn_conv_w'][l])
    c = jax.nn.silu(c)
    gq, gk, gv = (heads(a, H_GDN) for a in jnp.split(c, 3, axis=-1))
    gq = _l2norm(gq) * (HEAD_DIM ** -0.5)
    gk = _l2norm(gk)
    beta = jax.nn.sigmoid(gdn_b.astype(f32))
    log_decay = -jnp.exp(W['gdn_a_log'][l].astype(f32)) * jax.nn.softplus(
        gdn_a.astype(f32) + W['gdn_dt_bias'][l].astype(f32))
    s0 = jnp.zeros((B, H_GDN, HEAD_DIM, HEAD_DIM), f32) if past is None else past['S']
    o, s_new = _gated_delta(gq, gk, gv, log_decay, beta, s0, GDN_CHUNK if past is None else T)
    o = _rmsnorm(o, W['gdn_norm_w'][l]) * jax.nn.silu(heads(gdn_z, H_GDN).astype(f32))
    o_gdn = o.astype(dt).reshape(B, T, W_GDN)

    mq, mk, mv = (heads(a, H_MOBA) for a in jnp.split(moba_qkv, 3, axis=-1))
    moba_new = jnp.stack([mk, mv], axis=2)
    if past is None:
        mka, mva = mk, mv
    else:
        pkv = past['moba']
        mka = jnp.concatenate([pkv[:, :, 0], mk], axis=1)
        mva = jnp.concatenate([pkv[:, :, 1], mv], axis=1)
    tk = mka.shape[1]
    nb = max(-(-tk // MOBA_BLOCK), MOBA_TOPK)
    pad = ((0, 0), (0, nb * MOBA_BLOCK - tk), (0, 0), (0, 0))
    kblk = jnp.pad(mka, pad).reshape(B, nb, MOBA_BLOCK, H_MOBA, HEAD_DIM)
    vblk = jnp.pad(mva, pad).reshape(B, nb, MOBA_BLOCK, H_MOBA, HEAD_DIM)
    kmean = jnp.mean(kblk.astype(f32), axis=2).astype(dt)
    kbh = jnp.moveaxis(kblk, 3, 1)
    vbh = jnp.moveaxis(vblk, 3, 1)
    mbias = W['rel_bias'][:, :H_MOBA]
    moba_fn = lambda qb, pb: _moba_attend(qb, kbh, vbh, kmean, pb, mbias)
    o_moba = _sweep(moba_fn, mq, q_pos, MOBA_QCHUNK) if past is None else moba_fn(mq, q_pos)
    o_moba = o_moba.reshape(B, T, W_MOBA)

    dil_q, dil_k, dil_v = (heads(a, H_DIL) for a in jnp.split(dil_qkv, 3, axis=-1))
    srcs, dil_new = [], []
    for g in range(N_DIL_GROUPS):
        win = DIL_PATTERN[g][0]
        hs = slice(g * H_DIL_G, (g + 1) * H_DIL_G)
        kg, vg = dil_k[:, :, hs], dil_v[:, :, hs]
        if past is None:
            keep = min(win, T)
            p0 = 0
        else:
            buf = past['dil'][g]
            keep = buf.shape[1]
            kg = jnp.concatenate([buf[:, :, 0], kg], axis=1)
            vg = jnp.concatenate([buf[:, :, 1], vg], axis=1)
            p0 = PAST_LEN - keep
        srcs.append((kg, vg, p0))
        dil_new.append(jnp.stack([kg[:, -keep:], vg[:, -keep:]], axis=2))
    dbias = W['rel_bias'][:, H_MOBA:]
    dil_fn = lambda qb, pb: _dil_attend(qb, srcs, pb, dbias)
    o_dil = _sweep(dil_fn, dil_q, q_pos, DIL_QBLOCK) if past is None else dil_fn(dil_q, q_pos)
    o_dil = o_dil.reshape(B, T, W_DIL_OUT)

    gate = jax.nn.sigmoid(gate_in.astype(f32)).astype(dt).reshape(B, T, N_BRANCH, D_MODEL)
    merged = (gate[:, :, 0] * (o_sb @ W['w_br_sb'][l])
              + gate[:, :, 1] * (o_gdn @ W['w_br_gdn'][l])
              + gate[:, :, 2] * (o_moba @ W['w_br_moba'][l])
              + gate[:, :, 3] * (o_dil @ W['w_br_dil'][l]))
    out = merged @ W['w_out'][l]
    return out, (sb_new, moba_new, conv_new, s_new.astype(dt), dil_new[0], dil_new[1], dil_new[2])

def _swiglu(h, wg, wu, wd):
    return (jax.nn.silu(h @ wg) * (h @ wu)) @ wd

def _moe(h, router, wg, wu, wd):
    logits = (h @ router).astype(jnp.float32)
    top_v, top_i = lax.top_k(logits, TOP_K)
    gates = jax.nn.softmax(top_v, axis=-1)
    comb = jnp.sum(jax.nn.one_hot(top_i, N_EXPERTS, dtype=jnp.float32) * gates[..., None], axis=-2)
    comb = comb.astype(h.dtype)
    out = jnp.zeros_like(h)
    for e in range(N_EXPERTS):
        out = out + comb[..., e:e + 1] * _swiglu(h, wg[e], wu[e], wd[e])
    return out

def _trunk(x, q_pos, past, W):
    outs = [[] for _ in range(7)]
    for l in range(DEPTH):
        pl = None
        if past is not None:
            pt = past['page_table']
            pl = dict(sb=_gather_pages(past['sb'][l], pt), moba=_gather_pages(past['moba'][l], pt),
                      conv=past['conv'][l], S=past['S'][l], dil=[d[l] for d in past['dil']])
        h = _rmsnorm(x, W['norm_mix'][l])
        mix, st = _mixer(h, l, q_pos, pl, W)
        x = x + mix
        h = _rmsnorm(x, W['norm_ffn'][l])
        j = l // 2
        if l % 2 == 0:
            x = x + _swiglu(h, W['ffn_w_gate'][j], W['ffn_w_up'][j], W['ffn_w_down'][j])
        else:
            x = x + _moe(h, W['moe_router'][j], W['moe_w_gate'][j], W['moe_w_up'][j], W['moe_w_down'][j])
        for i in range(7):
            outs[i].append(st[i])
    y = _rmsnorm(x, W['final_norm'])
    return (y, jnp.stack(outs[0]), jnp.stack(outs[1]), jnp.stack(outs[2]), jnp.stack(outs[3]),
            jnp.stack(outs[4]), jnp.stack(outs[5]), jnp.stack(outs[6]))

def setup_inputs(seed: int = 0) -> dict:
    key = jax.random.key(seed)
    keys = jax.random.split(key, 40)
    f32 = jnp.float32

    def nrm(i, shape, scale):
        return jax.random.normal(keys[i], shape, f32) * scale

    n_pages = PAST_LEN // PAGE_SIZE
    n_used = DEC_BATCH * n_pages
    n_phys = n_used + max(1, n_used // 4)
    page_table = jax.random.permutation(keys[0], n_phys)[:n_used].reshape(DEC_BATCH, n_pages).astype(jnp.int32)
    dt0 = jnp.exp(jax.random.uniform(keys[13], (DEPTH, H_GDN), f32, math.log(1e-3), math.log(1e-1)))
    return {
        'x_prompt': nrm(1, (BATCH, SEQ, D_MODEL), 1.0),
        'x_sample': nrm(2, (DEC_BATCH, DEC_SEQ, D_MODEL), 1.0),
        'cache_sb_kv': nrm(3, (DEPTH, n_phys, PAGE_SIZE, 2, H_SB, HEAD_DIM), 1.0),
        'cache_moba_kv': nrm(4, (DEPTH, n_phys, PAGE_SIZE, 2, H_MOBA, HEAD_DIM), 1.0),
        'state_gdn_conv': nrm(5, (DEPTH, DEC_BATCH, CONV_W - 1, 3 * W_GDN), 1.0),
        'state_gdn_S': nrm(6, (DEPTH, DEC_BATCH, H_GDN, HEAD_DIM, HEAD_DIM), 0.05),
        'cache_dil_kv_0': nrm(7, (DEPTH, DEC_BATCH, min(DIL_PATTERN[0][0], PAST_LEN), 2, H_DIL_G, HEAD_DIM), 1.0),
        'cache_dil_kv_1': nrm(8, (DEPTH, DEC_BATCH, min(DIL_PATTERN[1][0], PAST_LEN), 2, H_DIL_G, HEAD_DIM), 1.0),
        'cache_dil_kv_2': nrm(9, (DEPTH, DEC_BATCH, min(DIL_PATTERN[2][0], PAST_LEN), 2, H_DIL_G, HEAD_DIM), 1.0),
        'page_table': page_table,
        'w_in': nrm(10, (DEPTH, D_MODEL, IN_COLS), D_MODEL ** -0.5),
        'w_br_sb': nrm(11, (DEPTH, W_SB, D_MODEL), W_SB ** -0.5),
        'w_br_gdn': nrm(12, (DEPTH, W_GDN, D_MODEL), W_GDN ** -0.5),
        'w_br_moba': nrm(14, (DEPTH, W_MOBA, D_MODEL), W_MOBA ** -0.5),
        'w_br_dil': nrm(15, (DEPTH, W_DIL_OUT, D_MODEL), W_DIL_OUT ** -0.5),
        'w_out': nrm(16, (DEPTH, D_MODEL, D_MODEL), D_MODEL ** -0.5),
        'norm_mix': 1.0 + nrm(17, (DEPTH, D_MODEL), 0.02),
        'norm_ffn': 1.0 + nrm(18, (DEPTH, D_MODEL), 0.02),
        'gdn_conv_w': nrm(19, (DEPTH, CONV_W, 3 * W_GDN), CONV_W ** -0.5),
        'gdn_a_log': jnp.log(jax.random.uniform(keys[20], (DEPTH, H_GDN), f32, 1.0, 16.0)),
        'gdn_dt_bias': dt0 + jnp.log(-jnp.expm1(-dt0)),
        'gdn_norm_w': 1.0 + nrm(21, (DEPTH, HEAD_DIM), 0.02),
        'rel_bias': nrm(22, (REL_BUCKETS, N_REL_HEADS), 0.2),
        'ffn_w_gate': nrm(23, (N_DENSE, D_MODEL, D_FF), D_MODEL ** -0.5),
        'ffn_w_up': nrm(24, (N_DENSE, D_MODEL, D_FF), D_MODEL ** -0.5),
        'ffn_w_down': nrm(25, (N_DENSE, D_FF, D_MODEL), D_FF ** -0.5),
        'moe_router': nrm(26, (N_MOE, D_MODEL, N_EXPERTS), D_MODEL ** -0.5),
        'moe_w_gate': nrm(27, (N_MOE, N_EXPERTS, D_MODEL, D_EXPERT), D_MODEL ** -0.5),
        'moe_w_up': nrm(28, (N_MOE, N_EXPERTS, D_MODEL, D_EXPERT), D_MODEL ** -0.5),
        'moe_w_down': nrm(29, (N_MOE, N_EXPERTS, D_EXPERT, D_MODEL), D_EXPERT ** -0.5),
        'final_norm': 1.0 + nrm(30, (D_MODEL,), 0.02),
    }

def reference(x_prompt, x_sample, cache_sb_kv, cache_moba_kv, state_gdn_conv, state_gdn_S,
              cache_dil_kv_0, cache_dil_kv_1, cache_dil_kv_2, page_table,
              w_in, w_br_sb, w_br_gdn, w_br_moba, w_br_dil, w_out, norm_mix, norm_ffn,
              gdn_conv_w, gdn_a_log, gdn_dt_bias, gdn_norm_w, rel_bias,
              ffn_w_gate, ffn_w_up, ffn_w_down, moe_router, moe_w_gate, moe_w_up, moe_w_down,
              final_norm):
    W = dict(w_in=w_in, w_br_sb=w_br_sb, w_br_gdn=w_br_gdn, w_br_moba=w_br_moba, w_br_dil=w_br_dil,
             w_out=w_out, norm_mix=norm_mix, norm_ffn=norm_ffn, gdn_conv_w=gdn_conv_w,
             gdn_a_log=gdn_a_log, gdn_dt_bias=gdn_dt_bias, gdn_norm_w=gdn_norm_w, rel_bias=rel_bias,
             ffn_w_gate=ffn_w_gate, ffn_w_up=ffn_w_up, ffn_w_down=ffn_w_down, moe_router=moe_router,
             moe_w_gate=moe_w_gate, moe_w_up=moe_w_up, moe_w_down=moe_w_down, final_norm=final_norm)
    past = dict(sb=cache_sb_kv, moba=cache_moba_kv, conv=state_gdn_conv, S=state_gdn_S,
                dil=(cache_dil_kv_0, cache_dil_kv_1, cache_dil_kv_2), page_table=page_table)
    pos_p = jnp.arange(x_prompt.shape[1], dtype=jnp.int32)
    pos_s = PAST_LEN + jnp.arange(x_sample.shape[1], dtype=jnp.int32)
    y_prompt, p_sb, p_moba, p_conv, p_S, p_d0, p_d1, p_d2 = _trunk(x_prompt, pos_p, None, W)
    y_sample, s_sb, s_moba, s_conv, s_S, s_d0, s_d1, s_d2 = _trunk(x_sample, pos_s, past, W)
    return (y_prompt, y_sample, p_sb, s_sb, p_moba, s_moba, p_conv, s_conv, p_S, s_S,
            p_d0, s_d0, p_d1, s_d1, p_d2, s_d2)


_drawn_inputs = setup_inputs


def setup_inputs(seed=0):
    import zlib

    import numpy as np

    out = dict(_drawn_inputs(seed))
    spreads = {}
    factors = {}
    for name, (base, spread) in spreads.items():
        noise = np.random.default_rng([zlib.crc32(name.encode()), seed]).standard_normal(out[name].shape)
        drawn = base * np.exp(spread * noise) if base else spread * noise
        out[name] = jnp.asarray(drawn.astype(out[name].dtype))
    for name, factor in factors.items():
        out[name] = (out[name] * factor).astype(out[name].dtype)
    return out
```

```python
import math
from contextlib import ExitStack

import numpy as np
import concourse.bass as bass
from concourse import mybir

F32 = mybir.dt.float32
I32 = mybir.dt.int32
ALU = mybir.AluOpType
ACT = mybir.ActivationFunctionType
AX = mybir.AxisListType

P = 128
D = 1024
KD = D // P
TP = 256
NS, TQ = 8, 4
TS = NS * TQ
T = TP + TS
L = 2
PAST = 1024
PAGE = 128
NPG = PAST // PAGE
HD = 64
SCALE = HD ** -0.5
EPS = 1e-6
NEG = -1e30
DFF, DEXP, NEXP = 2816, 3584, 8
FB, EB = DFF // P, DEXP // P
DIL = ((128, 1), (512, 4), (2048, 16))
BUCKETS, MAXDIST = 32, 2048
SLOTS = 6
SLOT = 2048
GRP = 6

SBQ, SBK, SBV, GQ, GK, GV, GZ, MQ, MK, MV, DQ, DK, DV, AB, NBLK = 0, 2, 4, 6, 8, 10, 12, 14, 16, 18, 20, 23, 26, 29, 30
OSB, OGD, OMO, ODI, NOB = 0, 2, 4, 6, 7
DCOL = {1: 0, 0: 512, 2: 640}
DNEW = 896
DW = DNEW + 3 * TS
SW = PAST + TS
PMIX, PFFN, PCONV, PGN, PALOG, PDTB, PFIN, NPAR = 0, 8, 16, 40, 41, 42, 43, 51


def bucket(dist):
    dist = np.maximum(dist, 0)
    exact = BUCKETS // 2
    d = np.maximum(dist, exact).astype(np.float32)
    big = exact + (np.log(d / np.float32(exact)) / np.float32(math.log(MAXDIST / exact))
                   * np.float32(BUCKETS - exact)).astype(np.int32)
    return np.where(dist < exact, dist, np.minimum(big, BUCKETS - 1))


def tables():
    c = {}
    j, i = np.arange(P)[:, None], np.arange(P)[None, :]
    c["ident"] = (j == i)
    c["ones"] = np.ones((P, P))
    c["head_ones"] = (j // HD == i // HD)
    c["upto"] = (j <= i)
    c["later"] = np.where(i >= j, 0.0, NEG)
    same = (j // TQ == i // TQ)
    c["seq_ones"] = same[:, :TS]
    c["seq_upto"] = (same & (j <= i))[:, :TS]
    c["seq_later"] = np.where(same & (i >= j), 0.0, NEG)[:, :TS]
    for s in range(7):
        b = 1 << s
        c[f"lvl{s}"] = (j // (2 * b) == i // (2 * b)) & ((j // b) % 2 == 0) & ((i // b) % 2 == 1)
    c["seq_of"] = (j // TQ == np.arange(NS)[None, :])
    c["rank"] = np.broadcast_to(np.arange(1, 5)[None, :], (P, 4))
    c["down"] = np.broadcast_to(np.arange(NEXP, 0, -1)[None, :], (P, NEXP))
    q = np.arange(P)[:, None]
    k = np.arange(TP)[None, :]
    c["sb_prompt"] = np.concatenate([np.where(k < q + t * P, 0.0, NEG) for t in range(2)], 1)
    r = np.arange(P)
    rb, rq = r // 16, r % 4
    kb, kt = np.arange(TS) // TQ, np.arange(TS) % TQ
    mine = rb[:, None] == kb[None, :]
    c["sb_new"] = np.where(mine & (kt[None] < rq[:, None]), 0.0, NEG)
    c["mo_new"] = np.where(mine & (kt[None] <= rq[:, None]), 0.0, NEG)
    r = np.arange(64)
    rb, rq = r // 8, r % 4
    mask = np.full((P, DW), NEG)
    hot = np.zeros((P, DW))
    pos = {1: 512 + np.arange(512), 0: 896 + np.arange(128),
           2: (16 * np.arange(64)[None, :] + np.arange(4)[:, None]).reshape(-1)}
    for g, (win, dil) in enumerate(DIL):
        for kpos, col, own in ((pos[g], DCOL[g], None), (PAST + kt, DNEW + g * TS, kb)):
            n = len(kpos)
            dist = PAST + rq[:, None] - kpos[None, :]
            ok = (dist >= 0) & (dist % dil == 0) & (dist <= win)
            if own is not None:
                ok &= rb[:, None] == own[None, :]
            mask[:64, col:col + n] = np.where(ok, 0.0, NEG)
            for t in range(TQ):
                bk = bucket(PAST + t - kpos)
                hot[t * BUCKETS + bk, col + np.arange(n)] = 1
    c["di_sample"], c["di_hot"] = mask, hot
    hot = np.zeros((P, SW))
    kpos = np.concatenate([np.arange(PAST), PAST + kt])
    for t in range(TQ):
        hot[t * BUCKETS + bucket(PAST + t - kpos), np.arange(SW)] = 1
    c["mo_hot"] = hot
    dist = TP - 1 - np.arange(2 * TP)
    hot = np.zeros((P, 2 * TP))
    hot[bucket(dist), np.arange(2 * TP)] = 1
    c["pr_hot"] = hot
    masks = [np.where((dist >= 0) & (dist % dil == 0) & (dist <= win), 0.0, NEG) for win, dil in ((TP, 1),) + DIL]
    c["pr_mask"] = np.broadcast_to(np.concatenate(masks)[None, :], (P, 8 * TP))
    return {n: np.ascontiguousarray(v, dtype=np.float32) for n, v in c.items()}


RESIDENT = (["ident", "ones", "head_ones", "upto", "later", "seq_ones", "seq_upto", "seq_later"]
            + [f"lvl{s}" for s in range(7)] + ["seq_of", "rank", "down", "sb_prompt", "sb_new"])
SETUP = ["mo_new", "mo_hot", "di_sample", "di_hot", "pr_hot", "pr_mask"]


def columns(names, c):
    at, n = {}, 0
    for name in names:
        at[name] = (n, n + c[name].shape[1])
        n += c[name].shape[1]
    return at, n


class Signals:

    def __init__(self, nc, ctx, per):
        self.nc, self.ctx, self.per = nc, ctx, per
        self.sems, self.count, self.times, self.layer = {}, {}, 1, 0

    def sem(self, name):
        if name not in self.sems:
            self.sems[name] = self.ctx.enter_context(self.nc.semaphore(name))
        return self.sems[name]

    def post(self, ins, name, n=1):
        ins.then_inc(self.sem(name), n)
        c = self.count.setdefault(name, [0] * L)
        c[self.layer] += n * self.times
        return ins

    def wait(self, eng, name, k, layer=None):
        layer = self.layer if layer is None else layer
        base = layer * self.per.get(name, 0)
        if isinstance(k, int) and base + k <= 0:
            return
        eng.wait_ge(self.sem(name), base + k)


class Chain:

    def __init__(self, eng, sem):
        self.eng, self.sem, self.n = eng, sem, 0

    def step(self, ins):
        ins.then_inc(self.sem, 1)
        self.n += 1
        self.eng.wait_ge(self.sem, self.n)


def plan():
    u = []
    for l in range(L):
        u += [("in", l, i, 1, "in_mm", 2 * i + 2) for i in range(NBLK // 2)]
        for kind in ("sb", "mo"):
            u += [(kind + "k", l, b, NPG, f"s{kind}_k", b + 1) for b in range(NS)]
            u += [(kind + "v", l, b, NPG, f"s{kind}_v", b + 1) for b in range(NS)]
        u += [("dk1", l, 0, 1, "sdi_k", 1), ("dk1", l, 1, 1, "sdi_k", 2), ("dk2", l, 0, 1, "sdi_k", 3),
              ("d0", l, 0, 2, "sdi_v", 1), ("dv1", l, 0, 1, "sdi_v", 1), ("dv1", l, 1, 1, "sdi_v", 1),
              ("dv2", l, 0, 4, "sdi_v", 1)]
        for m2 in range(KD // 2):
            u += [("gate", l, 4 * m2 + i, 1, "gate_mm", 8 * m2 + 2 * i + 2) for i in range(4)]
            u += [("br", l, m2, 1, "br_mm", 8 * m2 + 8)]
        u += [("out", l, i, 1, "out_mm", 2 * i + 2) for i in range(KD // 2)]
        if l == 0:
            u += [("fgu", l, i, 1, "fgu_mm", 2 * i + 2) for i in range(FB)]
            u += [("fdn", l, i, 1, "fdn_mm", (16 * i + 15) // FB + 1) for i in range(KD * FB // 16)]
    base = len(u)
    u += [("egu", 1, i, 1, "egu_mm", 2 * i + 2) for i in range(EB)]
    u += [("edn", 1, i, 1, "edn_mm", (16 * i + 15) // EB + 1) for i in range(KD * EB // 16)]
    land, total = [], [0] * SLOTS
    for n, x in enumerate(u):
        total[n % SLOTS] += 16 * x[3]
        land.append(total[n % SLOTS])
    return u, land, base


def attention_units():
    u = [("sb", h, [(SBQ + h // 2, SBK + h // 2, h % 2, h // 2, None)], OSB + h // 2) for h in range(4)]
    u += [("mo", h, [(MQ + h // 2, MK + h // 2, h % 2, 2 + h // 2, h)], OMO + h // 2) for h in range(4)]
    u += [("di", h, [(DQ + g, DK + g, h, 4 + g, 4 + 2 * g + h) for g in range(3)], ODI) for h in range(2)]
    return u


def score_banks(u):
    return [2, 3, 4] if attention_units()[u][0] == "di" else [2 + u % 2]


VB = [SBV, SBV + 1, MV, MV + 1, DV, DV + 1, DV + 2]
NORM = {"mix": 1, "ffn": 2, "fin": 3}
VGROUPS = [(t, a, b) for t in range(3) for a, b in ((0, 4), (4, 7))]


def gdn_rows(c):
    return TS if c == 2 else P


def gdn_levels(c):
    return 2 if c == 2 else 7


def half(h):
    return slice(64 * h, 64 * h + 64)


def program(nc, A, per):
    units, landing, moe_base = plan()
    C = tables()
    cat, cn = columns(RESIDENT, C)
    sat, sn = columns(SETUP, C)

    with ExitStack() as ctx:
        def sb(name, *shape, dt=F32):
            return ctx.enter_context(nc.sbuf_tensor(name, list(shape), dt))

        xT = sb("xT", P, KD, T)
        hT = sb("hT", P, KD, T)
        projT = sb("projT", P, NBLK, T)
        gate = projT[:, 0:8, :]
        mergedT = projT[:, DQ:DQ + KD, :]
        squares = mergedT
        actT = projT
        oT = sb("oT", P, NOB, T)
        rstd = sb("rstd", P, T)
        ring = sb("ring", P, SLOTS, SLOT)
        const = sb("const", P, cn)
        par = sb("par", P, L, NPAR)
        router = sb("router", P, KD, NEXP)
        pages = sb("pages", 1, NS * NPG, dt=I32)
        wk = sb("wk", P, 2, 3584)
        wkA = [wk[:, i, 0:1536] for i in range(2)]
        wkB = [wk[:, i, 1536:2048] for i in range(2)]
        wkR = [wk[:, i, 2048:2560] for i in range(2)]
        pt = [wk[:, i, 2560:2944] for i in range(2)]
        sA, sB, sR = (wk[:, 0, i * SW:(i + 1) * SW] for i in range(3))
        qbd = wk[:, 1, 0:8 * 272]
        dqbd = wk[:, 1, 0:8 * 200]
        spt = wk[:, 1, 2176:2176 + 9 * P].rearrange("p (g n) -> p g n", g=9)
        setup = wk[:, :, :].rearrange("p a b -> p (a b)")
        rel = setup[0:BUCKETS, sn:sn + 10]
        rel_mo, rel_di = setup[:, sn + 10:sn + 138], setup[:, sn + 138:sn + 330]
        region = sb("region", P, 5120)
        prompt_bias = region[:, :].rearrange("p (h n) -> p h n", h=10)
        gtok = region[:, 0:3840].rearrange("p (c i n) -> p c i n", c=3, i=5)
        sS = region[:, 3840:4864].rearrange("p (a b d) -> p a b d", a=2, b=NS)
        mo_bias = sb("mo_bias", P, SW)
        di_bias = sb("di_bias", 64, DW)
        vtok = sb("vtok", P, 3, NOB, P)
        qall = sb("qall", P, 2, P)
        dqall = sb("dqall", P, 3, 64)
        small = sb("small", P, 64)
        comb = wk[:, 1, 1024:1024 + NEXP * T].rearrange("p (e n) -> p e n", e=NEXP)
        cT = vtok[:, :, :, :].rearrange("p a b c -> p (a b c)")[:, 0:6 * T].rearrange("p (f n) -> p f n", f=6)
        sconv = sb("sconv", P, 6, NS, 7)
        conv_out = sb("conv_out", P, 6, 3 * (NS + 1))
        abT = sb("abT", P, T)
        abw = sb("abw", P, T)
        negA = sb("negA", P, 1)
        gwork = [wk[:, c, :].rearrange("p (s n) -> p s n", s=7) for c in range(2)] + [sb("gwork2", P, 7, 4 * TS)]
        gsc = sb("gsc", P, 3, 32)
        glast = sb("glast", P, 3, 4 * NS)
        nwm = sb("nwm", P, 2, NS * 36)
        pS = sb("pS", P, 2, HD)
        rlog = sb("rlog", P, 3, 4, NEXP)
        toks = sb("toks", P, 3, 16)
        PS = ctx.enter_context(nc.psum_tensor("PS", [P, 8, 512], F32))

        S = Signals(nc, ctx, per)
        post, wait = S.post, S.wait
        dma_sems = {n: ctx.enter_context(nc.semaphore(n)) for n in
                    ("const_loaded", "x_loaded", "setup_loaded", "bias_stored", "bias_loaded", "state_loaded",
                     "outputs_stored", "rows_stored", "windows_stored", "pages_loaded")}
        landed = [ctx.enter_context(nc.semaphore(f"slot{i}_landed")) for i in range(SLOTS)]
        steps = {e: ctx.enter_context(nc.semaphore(f"{e}_step")) for e in ("dve", "act", "pool")}
        counts = {"stored": 0, "state": 0}

        def cc(name, rows=P, cols=None):
            a, b = cat[name]
            return const[0:rows, a:(b if cols is None else a + cols)]

        ident = cc("ident")
        block = ctx.enter_context(nc.Block())

        @block.sync
        def _(sp):
            S.layer = 0
            sp.dma_start(const[:, :], A["const"]).then_inc(dma_sems["const_loaded"], 16)
            sp.dma_start(setup[:, 0:sn + 330], A["setup"]).then_inc(dma_sems["setup_loaded"], 16)
            sp.dma_start(pages[:, :], A["pages"]).then_inc(dma_sems["pages_loaded"], 16)
            sp.dma_start(xT[:, :, :], A["x"]).then_inc(dma_sems["x_loaded"], 16)
            sp.dma_start(par[:, :, :], A["par"]).then_inc(dma_sems["x_loaded"], 16)
            sp.dma_start(router[:, :, :], A["router"]).then_inc(dma_sems["x_loaded"], 16)
            sp.wait_ge(dma_sems["pages_loaded"], 16)

            def free(n):
                if n >= SLOTS:
                    _, l, _, _, name, k = units[n - SLOTS]
                    wait(sp, name, k, 0 if name[0] in "fe" else l)

            def cache_unit(n):
                kind, l, b, _, _, _ = units[n]
                free(n)
                s = ring[:, n % SLOTS, :]
                sem = landed[n % SLOTS]
                if kind in ("sbk", "sbv", "mok", "mov"):
                    src = A[kind]
                    for pg in range(NPG):
                        page = sp.value_load(pages[0:1, b * NPG + pg:b * NPG + pg + 1], min_val=0,
                                             max_val=A["n_phys"] - 1)
                        sp.dma_start(s[:, pg * 256:(pg + 1) * 256], src[page + l * A["n_phys"], :, :]).then_inc(sem, 16)
                elif kind == "dk1":
                    sp.dma_start(s.rearrange("p (b k) -> p b k", b=4), A["dk1"][l, :, 4 * b:4 * b + 4, :]).then_inc(sem, 16)
                elif kind == "dk2":
                    sp.dma_start(s.rearrange("p (b k) -> p b k", b=8),
                                 A["dk2"][l].rearrange("p b r n -> p b (r n)")[:, :, 0:256]).then_inc(sem, 16)
                elif kind == "d0":
                    sp.dma_start(s[:, 0:1024].rearrange("p (b k) -> p b k", b=8), A["dk0"][l]).then_inc(sem, 16)
                    sp.dma_start(s[:, 1024:2048], A["dv0"][l].rearrange("t b d -> t (b d)")).then_inc(sem, 16)
                elif kind == "dv1":
                    sp.dma_start(s.rearrange("p (k n) -> p k n", k=2),
                                 A["dv1"][l, 256 * b:256 * b + 256].rearrange("(k p) b d -> p k (b d)", p=P)
                                 ).then_inc(sem, 16)
                elif kind == "dv2":
                    rows = A["dv2"][l].rearrange("(n r) b d -> r n (b d)", r=16)
                    for r in range(4):
                        sp.dma_start(s[64 * (r % 2):64 * (r % 2) + 64, 1024 * (r // 2):1024 * (r // 2) + 1024],
                                     rows[r]).then_inc(sem, 16)

            def weight_unit(n):
                kind, l, i, _, _, _ = units[n]
                free(n)
                width = 1792 if kind == "br" else SLOT
                src = A[kind][i] if kind in ("fgu", "fdn") else A[kind][l, i]
                sp.dma_start(ring[:, n % SLOTS, 0:width], src).then_inc(landed[n % SLOTS], 16)

            for n in range(moe_base):
                (cache_unit if units[n][0] in ("sbk", "sbv", "mok", "mov", "dk1", "dk2", "d0", "dv1", "dv2")
                 else weight_unit)(n)

            nd = KD * EB // 16
            for j in range(SLOTS):
                free(moe_base + j)
            with sp.Fori(0, NEXP) as e:
                for i in range(EB + nd):
                    n = moe_base + i
                    if i < SLOTS:
                        sp.wait_ge(S.sem("edn_mm"), e * KD)
                    elif i < EB + SLOTS:
                        sp.wait_ge(S.sem("egu_mm"), e * (2 * EB) + units[n - SLOTS][5])
                    else:
                        sp.wait_ge(S.sem("edn_mm"), e * KD + units[n - SLOTS][5])
                    src = A["egu"][e * EB + i, :, :] if i < EB else A["edn"][e * nd + (i - EB), :, :]
                    sp.dma_start(ring[:, n % SLOTS, :], src).then_inc(landed[n % SLOTS], 16)

        @block.tensor
        def _(pe):
            S.layer = 0
            at = [0]

            def take(kind, extra=0, slot_turns=0):
                n = at[0]
                at[0] += 1
                assert units[n][0] == kind, (units[n], kind)
                pe.wait_ge(landed[n % SLOTS], landing[n] + slot_turns)
                return ring[:, n % SLOTS, :]

            def mm(out, lhsT, rhs, first, last):
                return pe.matmul(out, lhsT, rhs, start=first, stop=last)

            def norm_sum(tag):
                wait(pe, "norm_squares", NORM[tag])
                for k in range(KD):
                    ins = mm(PS[:, 7, 0:T], cc("ones"), squares[:, k, :], k == 0, k == KD - 1)
                post(ins, "norm_sum")

            def bias_tables():
                pe.wait_ge(dma_sems["const_loaded"], 16)
                pe.wait_ge(dma_sems["setup_loaded"], 16)
                def t(name, a=0, b=None):
                    return setup[:, sat[name][0] + a:sat[name][1] if b is None else sat[name][0] + b]
                for i, (a, b) in enumerate(((0, 512), (512, 1024), (1024, SW))):
                    mm(PS[:, 2 + i, 0:b - a], rel_mo, t("mo_hot", a, b), True, True)
                for g in range(3):
                    for a, n in ((DCOL[g], (128, 512, 256)[g]), (DNEW + g * TS, TS)):
                        ins = mm(PS[0:64, 5 + a // 512, a % 512:a % 512 + n], rel_di[:, g * 64:g * 64 + 64],
                                 t("di_hot", a, a + n), True, True)
                post(ins, "tables_mm")
                for h in range(10):
                    if h >= 3:
                        wait(pe, "table_sum", h - 2)
                    ins = mm(PS[:, (0, 1, 7)[h % 3], :], rel[:, h:h + 1].to_broadcast([BUCKETS, P]),
                             setup[0:BUCKETS, sat["pr_hot"][0]:sat["pr_hot"][1]], True, True)
                    post(ins, "table_mm")

            def in_projection(l):
                wait(pe, "norm_h", NORM["mix"])
                for i in range(NBLK // 2):
                    w = take("in").rearrange("p (h k c) -> p h k c", h=2, k=KD)
                    for h in range(2):
                        n = 2 * i + h
                        if n >= 2:
                            wait(pe, "in_evac", n - 1)
                        for k in range(KD):
                            ins = mm(PS[:, n % 2, 0:T], w[:, h, k, :], hT[:, k, :], k == 0, k == KD - 1)
                        post(ins, "in_mm")

            def value_transposes(l):
                wait(pe, "in_evac", NBLK)
                for i, (t, a, b) in enumerate(VGROUPS):
                    if i >= 2:
                        wait(pe, "vtok_copied", i - 1)
                    cols = (P, P, TS)[t]
                    for v in range(a, b):
                        ins = pe.transpose(PS[0:cols, 5 + i % 2, (v - a) * P:(v - a) * P + P],
                                           projT[:, VB[v], t * P:t * P + cols], ident)
                    post(ins, "vtok_mm")

            AUNITS = attention_units()

            def scores(u):
                kind, h, subs, _ = AUNITS[u]
                banks = score_banks(u)
                if u >= 1:
                    wait(pe, "at_s", u)
                for (qb, kb, hf, _, _), bank in zip(subs, banks):
                    for t in range(2):
                        ins = mm(PS[:, bank, t * TP:(t + 1) * TP], projT[half(hf), qb, t * P:(t + 1) * P],
                                 projT[half(hf), kb, 0:TP], True, True)
                post(ins, "at_qk")

            def prompt_attention(l):
                wait(pe, "vtok_copied", len(VGROUPS))
                scores(0)
                s = 0
                for u, (kind, h, subs, _) in enumerate(AUNITS):
                    if u + 1 < len(AUNITS):
                        scores(u + 1)
                    wait(pe, "sb_p", u + 1) if kind == "sb" else wait(pe, "md_p", u - 3)
                    if u >= 2:
                        wait(pe, "at_o", u - 1)
                    for g, (_, _, hf, vb, _) in enumerate(subs):
                        if s >= 2:
                            wait(pe, "pt_copied", s - 1)
                        p = wkA[u % 2].rearrange("p (g n) -> p g n", g=3)[:, g, :]
                        for i, a in enumerate((0, TP, TP + P)):
                            ins = pe.transpose(PS[:, 5 + s % 2, i * P:i * P + P], p[:, a:a + P], ident)
                        post(ins, "pt_mm")
                        wait(pe, "pt_copied", s + 1)
                        mm(PS[half(hf), u % 2, 0:TP], vtok[:, 0, vb, half(hf)], pt[s % 2][:, 0:TP], g == 0, False)
                        ins = mm(PS[half(hf), u % 2, P:TP], vtok[:, 1, vb, half(hf)], pt[s % 2][:, TP:TP + P],
                                 False, g == len(subs) - 1)
                        post(ins, "at_pv_sub")
                        s += 1

            def sample_attention(l, kind):
                kb, ob = {"sb": (SBK, 0), "mo": (MK, 2)}[kind]
                wait(pe, f"s{kind}_q", 1)
                for b in range(NS):
                    w = take(kind + "k").rearrange("p (g h t) -> p g h t", g=NPG, h=2)
                    for hp in range(2):
                        q = qbd[:, b * 256 + hp * P:b * 256 + hp * P + P]
                        for c in range(2):
                            ins = mm(PS[:, 2 + c, :], q, w[:, 4 * c:4 * c + 4, hp, :], b == 0 and hp == 0,
                                     b == NS - 1 and hp == 1)
                    post(ins, f"s{kind}_k")
                for hp in range(2):
                    ins = mm(PS[:, 4, 0:TS], qall[:, hp, :], projT[:, kb + hp, TP:T], hp == 0, hp == 1)
                post(ins, f"s{kind}_qk")
                wait(pe, f"s{kind}_p", 1)
                for g in range(NPG):
                    ins = pe.transpose(PS[:, 5 + g // 4, (g % 4) * P:(g % 4) * P + P], sA[:, g * P:g * P + P], ident)
                    if g == 3:
                        post(ins, f"s{kind}_pt")
                post(ins, f"s{kind}_pt")
                post(pe.transpose(PS[0:TS, 7, 0:P], sA[:, PAST:SW], ident), f"s{kind}_pt")
                wait(pe, f"s{kind}_ptcopied", 3)
                for b in range(NS):
                    w = take(kind + "v").rearrange("p (g n) -> p g n", g=NPG)
                    for hp in range(2):
                        out = PS[:, 1, (b * 2 + hp) * 8:(b * 2 + hp) * 8 + 8]
                        rows = slice(b * 16 + hp * 8, b * 16 + hp * 8 + 8)
                        mm(out, vtok[0:TS, 2, ob + hp, :], spt[0:TS, NPG, rows], True, False)
                        for g in range(NPG):
                            ins = mm(out, w[:, g, hp * P:hp * P + P], spt[:, g, rows], False, g == NPG - 1)
                    post(ins, f"s{kind}_v")

            def dilated_sample(l):
                wait(pe, "sdi_q", 1)

                def q(b, g):
                    return dqbd[:, b * 192 + g * 64:b * 192 + g * 64 + 64]
                for a in range(2):
                    w = take("dk1").rearrange("p (b k) -> p b k", b=4)
                    for b in range(4):
                        ins = mm(PS[0:64, 2, :], q(4 * a + b, 1), w[:, b, :], a == 0 and b == 0, a == 1 and b == 3)
                    post(ins, "sdi_k")
                w = take("dk2").rearrange("p (b k) -> p b k", b=8)
                for b in range(NS):
                    ins = mm(PS[0:64, 3, 128:384], q(b, 2), w[:, b, :], b == 0, b == NS - 1)
                post(ins, "sdi_k")
                d0 = take("d0")
                w = d0[:, 0:1024].rearrange("p (b k) -> p b k", b=8)
                for b in range(NS):
                    mm(PS[0:64, 3, 0:128], q(b, 0), w[:, b, :], b == 0, b == NS - 1)
                for g in range(3):
                    ins = mm(PS[0:64, 3, 384 + g * TS:384 + (g + 1) * TS], dqall[:, g, :], projT[:, DK + g, TP:T],
                             True, True)
                post(ins, "sdi_qk")
                wait(pe, "sdi_p", 1)
                for k in range(7):
                    pe.transpose(PS[:, 5, k * 64:k * 64 + 64], sA[0:64, k * P:k * P + P], ident[0:64, 0:64])
                for g in range(3):
                    ins = pe.transpose(PS[0:TS, 6, g * 64:g * 64 + 64], sA[0:64, DNEW + g * TS:DNEW + (g + 1) * TS],
                                       ident[0:64, 0:64])
                post(ins, "sdi_pt")
                v0 = d0[:, 1024:2048].rearrange("p (b n) -> p b n", b=8)
                v1 = [take("dv1").rearrange("p (k b n) -> p k b n", k=2, b=8) for _ in range(2)]
                v2 = take("dv2").rearrange("p (k b n) -> p k b n", k=2, b=8)
                wait(pe, "sdi_ptcopied", 2)
                flat = spt.rearrange("p g n -> p (g n)")
                for b in range(NS):
                    out = PS[:, 1, b * 8:b * 8 + 8]
                    vs = [v1[0][:, 0, b], v1[0][:, 1, b], v1[1][:, 0, b], v1[1][:, 1, b], v0[:, b], v2[:, 0, b],
                          v2[:, 1, b]]
                    for k, v in enumerate(vs):
                        mm(out, v, flat[:, k * 64 + b * 8:k * 64 + b * 8 + 8], k == 0, False)
                    for g in range(3):
                        ins = mm(out, vtok[0:TS, 2, 4 + g, :],
                                 flat[0:TS, 7 * P + g * 64 + b * 8:7 * P + g * 64 + b * 8 + 8], False, g == 2)
                post(ins, "sdi_v")

            def heads_view(ap, n):
                return ap[:, 0:4 * n].rearrange("p (h n) -> p h n", h=4)

            def delta(l):
                wait(pe, "conv_sq", 1)
                for i in range(4):
                    ins = mm(PS[:, i, 0:T], cc("head_ones"), wk[:, 0, i * T:(i + 1) * T],
                             True, True)
                post(ins, "conv_sum")
                wait(pe, "conv_done", 1)
                wait(pe, "ab_done", 1)
                for c in range(3):
                    n = gdn_rows(c)
                    for i in range(2):
                        pe.transpose(PS[0:n, 2 * c, i * P:i * P + P], cT[:, 2 + i, c * P:c * P + n], ident)
                        pe.transpose(PS[0:n, 2 * c, TP + i * P:TP + i * P + P], cT[:, 4 + i, c * P:c * P + n], ident)
                    post(pe.transpose(PS[0:n, 2 * c + 1, 0:P], abT[:, c * P:c * P + n], ident), "gtok_mm")
                for c in range(3):
                    n = gdn_rows(c)
                    wait(pe, "gsc_g", c + 1)
                    g = gsc[0:n, c, 0:4]
                    mm(PS[0:n, 6, c * 32:c * 32 + 4], cc("seq_upto" if c == 2 else "upto", n, n), g, True, True)
                    ins = mm(PS[0:n, 6, c * 32 + 8:c * 32 + 12], cc("seq_ones" if c == 2 else "ones", n, n), g, True, True)
                    post(ins, "gcum_mm")
                for c in range(3):
                    n = gdn_rows(c)
                    wait(pe, "gtok_copied", c + 1)
                    wait(pe, "gbc_rhs", c + 1)
                    mm(PS[:, 2 * c, 0:4 * n], cc("ones", n), gwork[c][0:n, 0, 0:4 * n], True, True)
                    ins = mm(PS[:, 2 * c + 1, 0:4 * n], cc("ones", n), gwork[c][0:n, 1, 0:4 * n], True, True)
                    post(ins, "gbc_mm")
                for c in range(3):
                    n = gdn_rows(c)
                    wait(pe, "gkq", c + 1)
                    kb = gwork[c][:, 6, 0:2 * n].rearrange("p (a n) -> p a n", a=2)
                    for h in range(4):
                        k = cT[half(h % 2), 2 + h // 2, c * P:c * P + n]
                        bank, a = 2 * c + h % 2, h // 2
                        mm(PS[0:n, bank, a * n:(a + 1) * n], k, kb[half(h % 2), a, :], True, True)
                        ins = mm(PS[0:n, bank, (2 + a) * n:(3 + a) * n], k, cT[half(h % 2), a, c * P:c * P + n],
                                 True, True)
                    post(ins, "gm_mm")
                x = [0, 0, 0]
                for s in range(7):
                    for c in range(3):
                        n = gdn_rows(c)
                        if s >= gdn_levels(c):
                            continue
                        wait(pe, f"g{c}_bt", s + 1)
                        B, Tm = heads_view(gwork[c][:, 0, :], n), heads_view(gwork[c][:, 3, :], n)
                        for h in range(4):
                            ins = mm(PS[0:n, 2 * c, h * n:(h + 1) * n], B[0:n, h], Tm[0:n, h], True, True)
                        post(ins, f"g{c}_x")
                    for c in range(3):
                        n = gdn_rows(c)
                        if s >= gdn_levels(c):
                            continue
                        wait(pe, f"g{c}_xcopied", s + 1)
                        X, Tm, TT = (heads_view(gwork[c][:, i, :], n) for i in (5, 3, 4))
                        for h in range(4):
                            mm(PS[0:n, 2 * c, h * n:(h + 1) * n], TT[0:n, h], X[0:n, h], True, True)
                            ins = mm(PS[0:n, 2 * c + 1, h * n:(h + 1) * n], X[0:n, h], TT[0:n, h], True, True)
                        post(ins, f"g{c}_y")
                for c in range(3):
                    n = gdn_rows(c)
                    wait(pe, f"g{c}_t", gdn_levels(c))
                    wait(pe, "gscaled", c + 1)
                    TT = heads_view(gwork[c][:, 4, :], n)
                    for h in range(4):
                        ins = mm(PS[half(h % 2), 2 * c, (h // 2) * n:(h // 2 + 1) * n], gtok[0:n, c, 2, h * HD:(h + 1) * HD],
                                 TT[0:n, h], True, True)
                    post(ins, "gw_mm")
                for c in range(3):
                    n = gdn_rows(c)
                    TT = heads_view(gwork[c][:, 4, :], n)
                    QK = heads_view(gwork[c][:, 2, :], n)
                    qg = gwork[c][:, 6, 2 * n:4 * n].rearrange("p (a n) -> p a n", a=2)
                    wait(pe, "gnw", c + 1)
                    if c == 1:
                        wait(pe, "pstate", 1)
                    for h in range(4):
                        hf, hp = half(h % 2), h // 2
                        out = PS[0:n, 2 * c + h % 2, hp * HD:(hp + 1) * HD]
                        ins = mm(out, TT[0:n, h], gtok[0:n, c, 1, h * HD:(h + 1) * HD], True, c == 0)
                        if c == 1:
                            ins = mm(out, gtok[hf, c, 4, hp * P:hp * P + P], pS[hf, hp, :], False, True)
                        if c == 2:
                            for b in range(NS):
                                ins = mm(out, nwm[hf, hp, b * TS:(b + 1) * TS], sS[hf, hp, b, :], False, b == NS - 1)
                    post(ins, "gu_mm")
                    wait(pe, "gvnew", c + 1)
                    for h in range(4):
                        hf, hp = half(h % 2), h // 2
                        out = PS[hf, 2 * c, hp * n:(hp + 1) * n]
                        ins = mm(out, gtok[0:n, c, 3, h * HD:(h + 1) * HD], QK[0:n, h], True, c == 0)
                        if c == 1:
                            ins = mm(out, pS[hf, hp, :], qg[hf, hp, :], False, True)
                        if c == 2:
                            for b in range(NS):
                                ins = mm(PS[hf, 2 * c, hp * n + b * TQ:hp * n + (b + 1) * TQ], sS[hf, hp, b, :],
                                         qg[hf, hp, b * TQ:(b + 1) * TQ], False, b == NS - 1)
                    post(ins, "go_mm")
                    if c < 2:
                        for h in range(4):
                            ins = mm(PS[half(h % 2), 6 + c, (h // 2) * HD:(h // 2 + 1) * HD],
                                     gtok[0:n, c, 0, h * HD:(h + 1) * HD], gtok[0:n, c, 3, h * HD:(h + 1) * HD], True, True)
                        post(ins, "gs_mm")
                wait(pe, "gvm", 1)
                wait(pe, "pstate", 2)
                for h in range(4):
                    ins = mm(PS[half(h % 2), 6 + h // 2, :], gtok[0:TS, 2, 0, h * HD:(h + 1) * HD],
                             mergedT.rearrange("p a b -> p (a b)")[0:TS, h * 512:(h + 1) * 512], True, True)
                post(ins, "gss_mm")
                wait(pe, "go_sq", 1)
                for i in range(2):
                    ins = mm(PS[:, i, 0:T], cc("head_ones"), squares[:, i, :], True, True)
                post(ins, "go_sum")

            def merge(l):
                g = 0
                wait(pe, "go_rs", 1)
                for m2 in range(KD // 2):
                    for u in range(4):
                        w = take("gate").rearrange("p (h k c) -> p h k c", h=2, k=KD)
                        for h in range(2):
                            if g >= 2:
                                wait(pe, "gate_evac", g - 1)
                            for k in range(KD):
                                ins = mm(PS[:, g % 2, 0:T], w[:, h, k, :], hT[:, k, :], k == 0, k == KD - 1)
                            post(ins, "gate_mm")
                            g += 1
                    if m2 == 0:
                        wait(pe, "o_done", 1)
                    w = take("br")[:, 0:1792].rearrange("p (m k c) -> p m k c", m=2, k=7)
                    for m in range(2):
                        for br, (k0, k1) in enumerate(((OSB, 2), (OGD, 4), (OMO, 6), (ODI, 7))):
                            n = (2 * m2 + m) * 4 + br
                            if n >= 4:
                                wait(pe, "br_evac", n - 3)
                            for k in range(k0, k1):
                                ins = mm(PS[:, 2 + n % 4, 0:T], w[:, m, k, :], oT[:, k, :], k == k0, k == k1 - 1)
                            post(ins, "br_mm")
                wait(pe, "merged", KD)
                for i in range(KD // 2):
                    w = take("out").rearrange("p (h k c) -> p h k c", h=2, k=KD)
                    for h in range(2):
                        n = 2 * i + h
                        if n >= 2:
                            wait(pe, "out_evac", n - 1)
                        for k in range(KD):
                            ins = mm(PS[:, n % 2, 0:T], w[:, h, k, :], mergedT[:, k, :], k == 0, k == KD - 1)
                        post(ins, "out_mm")

            def feed_forward(t, nblk, e=0, turns=0):
                for i in range(nblk):
                    w = take(t + "gu", slot_turns=turns).rearrange("p (h k c) -> p h k c", h=2, k=KD)
                    for h in range(2):
                        n = 2 * i + h
                        if isinstance(e, int):
                            if n >= 4:
                                pe.wait_ge(S.sem(t + "act"), i - 1)
                        elif n % 2 == 0:
                            pe.wait_ge(S.sem(t + "act"), e * nblk + max(i - 1, 0))
                        for k in range(KD):
                            ins = mm(PS[:, n % 4, 0:T], w[:, h, k, :], hT[:, k, :], k == 0, k == KD - 1)
                        post(ins, t + "gu_mm")
                pe.wait_ge(S.sem(t + "act"), nblk + e * nblk)
                w = None
                for m in range(KD):
                    if not isinstance(e, int) or m >= 2:
                        pe.wait_ge(S.sem(t + "dn_evac"), e * KD + max(m - 1, 0))
                    for k in range(nblk):
                        b = m * nblk + k
                        if b % 16 == 0:
                            w = take(t + "dn", slot_turns=turns).rearrange("p (k c) -> p k c", k=16)
                        ins = mm(PS[:, 4 + m % 2, 0:T], w[:, b % 16, :], actT[:, k, :], k == 0, k == nblk - 1)
                    post(ins, t + "dn_mm")

            def routing():
                wait(pe, "norm_h", NORM["ffn"])
                for t in range(3):
                    n = gdn_rows(t)
                    for k in range(KD):
                        ins = mm(PS[0:n, 6, t * 8:t * 8 + 8], hT[:, k, t * P:t * P + n], router[:, k, :], k == 0, k == KD - 1)
                post(ins, "router_mm")
                for t in range(3):
                    n = gdn_rows(t)
                    for c in range(2):
                        i = 2 * t + c
                        pe.wait_ge(S.sem("comb_rhs"), i + 1)
                        ins = mm(PS[:, 2 + i % 2, 0:4 * n], cc("ones", n), wk[0:n, i % 2, 0:4 * n], True, True)
                        post(ins, "comb_mm")
                        pe.wait_ge(S.sem("comb_copied"), i + 1)

            bias_tables()
            for l in range(L):
                S.layer = l
                norm_sum("mix")
                in_projection(l)
                value_transposes(l)
                prompt_attention(l)
                sample_attention(l, "sb")
                sample_attention(l, "mo")
                dilated_sample(l)
                delta(l)
                merge(l)
                norm_sum("ffn")
                if l == 0:
                    wait(pe, "norm_h", NORM["ffn"])
                    feed_forward("f", FB)
            routing()
            with pe.Fori(0, NEXP) as e:
                S.times = NEXP
                at[0] = moe_base
                per_expert = 16 * ((EB + KD * EB // 16) // SLOTS)
                feed_forward("e", EB, e, e * per_expert)
                S.times = 1
            norm_sum("fin")

        @block.scalar
        def _(act):
            chain = Chain(act, steps["act"])
            step = chain.step
            AUNITS = attention_units()

            def copy(out, in_, scale=1.0):
                return act.activation(out, in_, ACT.Copy, scale=scale)

            def softplus_rest(A, B):
                step(act.activation(B, A, ACT.Abs))
                step(act.activation(B, B, ACT.Exp, scale=-1.0))
                return act.activation(B, B, ACT.Ln, bias=1.0)

            def norm_root(tag):
                wait(act, "norm_mean", NORM[tag])
                post(act.activation(rstd[:, :], rstd[:, :], ACT.Sqrt), "norm_root")

            def in_evacuation(l):
                if l:
                    wait(act, "norm_squares", NORM["mix"])
                    wait(act, "fdn_evac", KD, 0)
                for n in range(NBLK):
                    wait(act, "in_mm", n + 1)
                    post(copy(projT[:, n, :], PS[:, n % 2, 0:T]), "in_evac")

            def value_copies(l):
                for i, (t, a, b) in enumerate(VGROUPS):
                    n = (P, P, TS)[t]
                    wait(act, "vtok_mm", i + 1)
                    post(copy(vtok[0:n, t, a:b, :], PS[0:n, 5 + i % 2, 0:(b - a) * P].rearrange("p (v d) -> p v d", d=P)),
                         "vtok_copied")

            def prompt_attention(l):
                s = 0
                for v in range(len(AUNITS) + 1):
                    if v < len(AUNITS):
                        A, B = wkA[v % 2], wkB[v % 2]
                        if AUNITS[v][0] == "sb":
                            wait(act, "at_s", v + 1)
                            post(softplus_rest(A[:, 0:512], B[:, 0:512]), "sb_soft")
                        else:
                            wait(act, "at_nm", v - 3)
                            w = A.rearrange("p (g t k) -> p t g k", g=3, t=2)[:, :, 0:len(AUNITS[v][2]), :]
                            for t in range(2):
                                ins = act.activation(w[:, t], w[:, t], ACT.Exp, bias=small[:, 6 * v + t:6 * v + t + 1],
                                                     accum_out=small[:, 6 * v + 2 + t:6 * v + 3 + t])
                            post(ins, "at_e")
                    if v >= 1:
                        u = v - 1
                        if AUNITS[u][0] == "sb":
                            wait(act, "sb_r", u + 1)
                            A = wkA[u % 2][:, 0:512]
                            post(act.activation(A, A, ACT.Exp), "sb_p")
                        for _ in AUNITS[u][2]:
                            wait(act, "pt_mm", s + 1)
                            if s >= 2:
                                wait(act, "at_pv_sub", s - 1)
                            post(copy(pt[s % 2], PS[:, 5 + s % 2, 0:384]), "pt_copied")
                            s += 1

            def sample_attention(l, kind):
                A, B = sA, sB
                if kind == "sb":
                    wait(act, "ssb_s", 1)
                    post(softplus_rest(A, B), "ssb_soft")
                    wait(act, "ssb_r", 1)
                    post(act.activation(A, A, ACT.Exp), "ssb_p")
                else:
                    wait(act, "smo_nm", 1)
                    post(act.activation(A, A, ACT.Exp, bias=small[:, 60:61], accum_out=small[:, 61:62]), "smo_e")
                for i in range(2):
                    wait(act, f"s{kind}_pt", i + 1)
                    post(copy(spt[:, 4 * i:4 * i + 4, :], PS[:, 5 + i, :].rearrange("p (g n) -> p g n", g=4)),
                         f"s{kind}_ptcopied")
                wait(act, f"s{kind}_pt", 3)
                post(copy(spt[0:TS, NPG, :], PS[0:TS, 7, 0:P]), f"s{kind}_ptcopied")

            def dilated_sample(l):
                A = sA[0:64, 0:DW]
                wait(act, "sdi_nm", 1)
                post(act.activation(A, A, ACT.Exp, bias=small[0:64, 60:61], accum_out=small[0:64, 61:62]), "sdi_e")
                flat = spt.rearrange("p g n -> p (g n)")
                wait(act, "sdi_pt", 1)
                post(copy(flat[:, 0:448], PS[:, 5, 0:448]), "sdi_ptcopied")
                post(copy(flat[0:TS, 7 * P:7 * P + 192], PS[0:TS, 6, 0:192]), "sdi_ptcopied")

            def delta(l):
                wait(act, "conv_y", 1)
                post(act.activation(cT[:, :, :], cT[:, :, :], ACT.Silu), "conv_silu")
                wait(act, "ab_in", 1)
                post(act.activation(abT[32:36, :], projT[32:36, AB, :], ACT.Sigmoid), "beta_done")
                step(act.activation(negA[0:4, :], par[0:4, l, PALOG:PALOG + 1], ACT.Exp))
                post(softplus_rest(abw[0:4, :], abT[0:4, :]), "ab_soft")
                wait(act, "conv_ms", 1)
                post(act.activation(wk[:, 1, 0:4 * T], wk[:, 1, 0:4 * T], ACT.Sqrt), "conv_root")
                for c in range(3):
                    n = gdn_rows(c)
                    wait(act, "gtok_mm", c + 1)
                    post(copy(gtok[0:n, c, 0:2, :], PS[0:n, 2 * c, :].rearrange("p (a n) -> p a n", a=2)), "gtok_copied")
                for c in range(3):
                    n = gdn_rows(c)
                    wait(act, "gbc_mm", c + 1)
                    G = PS[:, 2 * c, 0:4 * n]
                    post(act.activation(gwork[c][:, 5, 0:4 * n], G, ACT.Exp), "g_eg")
                    gv = G.rearrange("p (h n) -> p h n", h=4)
                    if c < 2:
                        ins = act.activation(glast[:, c, 0:4], gv[:, :, n - 1], ACT.Exp)
                    else:
                        ins = act.activation(glast[:, c, :].rearrange("p (h b) -> p h b", h=4), gv[:, :, TQ - 1::TQ], ACT.Exp)
                    post(ins, "g_last")
                    wait(act, "gsc_in", c + 1)
                    act.activation(gsc[0:n, c, 16:20], gsc[0:n, c, 8:12], ACT.Exp)
                    post(act.activation(gsc[0:n, c, 28:32], gsc[0:n, c, 24:28], ACT.Exp), "gsc_exp")
                    wait(act, "gam_in", c + 1)
                    post(act.activation(gwork[c][0:n, 0, 0:4 * n], gwork[c][0:n, 0, 0:4 * n], ACT.Exp), "gam")
                for s in range(7):
                    for c in range(3):
                        n = gdn_rows(c)
                        if s < gdn_levels(c):
                            wait(act, f"g{c}_x", s + 1)
                            post(copy(gwork[c][0:n, 5, 0:4 * n], PS[0:n, 2 * c, 0:4 * n]), f"g{c}_xcopied")
                wait(act, "gtok_mm", 3)
                post(act.activation(cT[:, 4:6, :], projT[:, GZ:GZ + 2, :], ACT.Silu), "z_silu")
                for c in range(3):
                    n = gdn_rows(c)
                    wait(act, "gw_mm", c + 1)
                    if c < 2:
                        post(copy(gtok[:, c, 4, :], PS[:, 2 * c, 0:2 * n], -1.0), "gnw")
                    else:
                        for a in range(2):
                            ins = copy(nwm[:, a, :].rearrange("p (b x) -> p b x", x=36)[:, :, 0:TQ],
                                       PS[:, 4, a * TS:(a + 1) * TS].rearrange("p (b q) -> p b q", q=TQ), -1.0)
                        post(ins, "gnw")
                for c in range(3):
                    n = gdn_rows(c)
                    wait(act, "gu_mm", c + 1)
                    new = gtok[0:n, c, 3, :].rearrange("p (a t d) -> p a t d", a=2, t=2)
                    for hf in range(2):
                        ins = copy(new[:, :, hf, :], PS[0:n, 2 * c + hf, 0:P].rearrange("p (a d) -> p a d", a=2))
                    post(ins, "gvnew")

            def gates(l):
                act.wait_ge(dma_sems["rows_stored"], 16 * 3 * (l + 1))
                wait(act, "go_rs", 1)
                post(act.activation(squares[:, 2:4, :], squares[:, 2:4, :], ACT.Sqrt), "go_root")
                wait(act, "o_done", 1)
                for g in range(4 * KD):
                    if g % 8 == 0 and g:
                        wait(act, "merged", g // 4)
                    wait(act, "gate_mm", g + 1)
                    post(act.activation(gate[:, g % 8, :], PS[:, g % 2, 0:T], ACT.Sigmoid), "gate_evac")

            def feed_forward(t, nblk, e=0):
                for i in range(nblk):
                    act.wait_ge(S.sem(t + "gu_mm"), e * (2 * nblk) + (2 * i + 1))
                    if not isinstance(e, int) or i >= 2:
                        act.wait_ge(S.sem(t + "act"), e * nblk + max(i - 1, 0))
                    post(act.activation(wk[:, 1, (i % 2) * T:(i % 2 + 1) * T], PS[:, (2 * i) % 4, 0:T], ACT.Silu),
                         t + "silu")

            act.wait_ge(dma_sems["const_loaded"], 16)
            act.wait_ge(dma_sems["x_loaded"], 48)
            for l in range(L):
                S.layer = l
                norm_root("mix")
                in_evacuation(l)
                value_copies(l)
                prompt_attention(l)
                sample_attention(l, "sb")
                sample_attention(l, "mo")
                dilated_sample(l)
                delta(l)
                gates(l)
                norm_root("ffn")
                if l == 0:
                    feed_forward("f", FB)
            for t in range(3):
                n = gdn_rows(t)
                act.wait_ge(S.sem("route_in"), t + 1)
                post(act.activation(toks[0:n, t, 5:6], toks[0:n, t, 4:5], ACT.Exp), "route_exp")
            for i in range(6):
                t, c = i // 2, i % 2
                n = gdn_rows(t)
                act.wait_ge(S.sem("comb_mm"), i + 1)
                post(copy(comb[:, 4 * c:4 * c + 4, t * P:t * P + n],
                          PS[:, 2 + i % 2, 0:4 * n].rearrange("p (e n) -> p e n", e=4)), "comb_copied")
            with act.Fori(0, NEXP) as e:
                S.times = NEXP
                feed_forward("e", EB, e)
                S.times = 1
            norm_root("fin")

        @block.vector
        def _(dve):
            chain = Chain(dve, steps["dve"])
            step = chain.step
            AUNITS = attention_units()

            def tt(out, a, b, op):
                return dve.tensor_tensor(out, a, b, op)

            def ts(out, a, s1, s2, op0, op1=ALU.bypass):
                if s2 is None:
                    return dve.tensor_scalar(out, a, s1, None, op0)
                return dve.tensor_scalar(out, a, s1, s2, op0, op1)

            def stt(out, a, s, b, op0, op1):
                return dve.scalar_tensor_tensor(out=out, in0=a, scalar=s, in1=b, op0=op0, op1=op1)

            def norm(tag, col, l):
                post(tt(squares[:, :, :], xT[:, :, :], xT[:, :, :], ALU.mult), "norm_squares")
                wait(dve, "norm_sum", NORM[tag])
                post(ts(rstd[:, :], PS[:, 7, 0:T], 1.0 / D, EPS, ALU.mult, ALU.add), "norm_mean")
                wait(dve, "norm_root", NORM[tag])
                step(dve.reciprocal(rstd[:, :], rstd[:, :]))
                for k in range(KD):
                    ins = stt(hT[:, k, :], xT[:, k, :], par[:, l, col + k:col + k + 1], rstd[:, :], ALU.mult, ALU.mult)
                post(ins, "norm_h")

            def bias_tables():
                dve.wait_ge(dma_sems["const_loaded"], 16)
                dve.wait_ge(dma_sems["setup_loaded"], 16)
                wait(dve, "tables_mm", 1)

                def t(name, rows=P):
                    return setup[0:rows, sat[name][0]:sat[name][1]]
                masks = t("pr_mask").rearrange("p (m n) -> p m n", m=4)
                for h in range(10):
                    wait(dve, "table_mm", h + 1)
                    post(tt(prompt_bias[:, h, :], PS[:, (0, 1, 7)[h % 3], :], masks[:, 0 if h < 4 else 1 + (h - 4) // 2, :],
                            ALU.add), "table_sum")
                hot = PS[:, 2:5, :].rearrange("p a b -> p (a b)")
                dve.tensor_copy(mo_bias[:, 0:PAST], hot[:, 0:PAST])
                tt(mo_bias[:, PAST:SW], hot[:, PAST:SW], t("mo_new"), ALU.add)
                step(tt(di_bias[:, :], PS[0:64, 5:7, :].rearrange("p a b -> p (a b)")[:, 0:DW], t("di_sample", 64), ALU.add))

            def prompt_attention(l):
                dve.wait_ge(dma_sems["bias_loaded"], 32 * (l + 1))
                subs = 0
                done = []
                for u in AUNITS:
                    subs += len(u[2])
                    done.append(subs)

                def sc(u, c):
                    return small[:, 6 * u + c:6 * u + c + 2]

                def first(u):
                    kind, h, parts, _ = AUNITS[u]
                    A = wkA[u % 2]
                    n = len(parts)
                    if u >= 2:
                        wait(dve, "at_pv_sub", done[u - 2])
                    wait(dve, "at_qk", u + 1)
                    b0 = score_banks(u)[0]
                    if kind == "sb":
                        post(stt(A[:, 0:512], PS[:, b0, :], SCALE, cc("sb_prompt"), ALU.mult, ALU.add), "at_s")
                        return
                    bias = prompt_bias[:, h:h + 1, :] if kind == "mo" else prompt_bias[:, 4 + h:9 + h:2, :]
                    post(stt(A.rearrange("p (g n) -> p g n", g=3)[:, 0:n, :], PS[:, b0:b0 + n, :], SCALE, bias,
                             ALU.mult, ALU.add), "at_s")
                    wait(dve, "at_s", u + 1)
                    w = A.rearrange("p (g t k) -> p t g k", g=3, t=2)[:, :, 0:n, :]
                    step(dve.tensor_reduce(sc(u, 4), w, AX.XY, ALU.max))
                    post(ts(sc(u, 0), sc(u, 4), -1.0, None, ALU.mult), "at_nm")

                def second(u):
                    kind, h, parts, _ = AUNITS[u]
                    A, B, R = wkA[u % 2], wkB[u % 2], wkR[u % 2]
                    if kind == "sb":
                        wait(dve, "sb_soft", u + 1)
                        step(stt(B[:, 0:512], A[:, 0:512], 0.0, B[:, 0:512], ALU.max, ALU.add))
                        suffix_sums(R, B, ((0, TP), (TP, 2 * TP)), P)
                        post(tt(A[:, 0:512], A[:, 0:512], R[:, 0:512], ALU.subtract), "sb_r")
                        return
                    wait(dve, "at_e", u - 3)
                    step(dve.reciprocal(sc(u, 4), sc(u, 2)))
                    w = A.rearrange("p (g t k) -> p t g k", g=3, t=2)[:, :, 0:len(parts), :]
                    for t in range(2):
                        ins = ts(w[:, t], w[:, t], small[:, 6 * u + 4 + t:6 * u + 5 + t], None, ALU.mult)
                    post(ins, "md_p")

                def third(u):
                    _, h, parts, ob = AUNITS[u]
                    hf = half(parts[0][2])
                    wait(dve, "at_pv_sub", done[u])
                    post(dve.tensor_copy(oT[hf, ob, 0:TP], PS[hf, u % 2, 0:TP]), "at_o")

                n = len(AUNITS)
                for v in range(n + 2):
                    if v < n:
                        first(v)
                    if 1 <= v <= n:
                        second(v - 1)
                    if v >= 2:
                        third(v - 2)

            def suffix_sums(out, a, spans, rows):
                for lo, hi in spans:
                    o, x = (y[:, lo:hi][:, ::-1] for y in (out, a))
                    ins = dve.tensor_tensor_scan(o, cc("ones", rows, 1).to_broadcast([rows, hi - lo]), x, 0.0,
                                                 ALU.mult, ALU.add)
                step(ins)

            def sample_queries(l, kind):
                if kind == "sb":
                    wait(dve, "q_zeroed", 1)
                qb = {"sb": SBQ, "mo": MQ}[kind]
                for hp in range(2):
                    for hf in range(2):
                        q = projT[half(hf), qb + hp, TP:T].rearrange("p (b q) -> p b q", q=TQ)
                        dve.tensor_copy(qbd.rearrange("p (b x) -> p b x", x=272)[
                            half(hf), :, hp * 136 + hf * 4:hp * 136 + hf * 4 + TQ], q)
                        c = (2 * hp + hf) * 4
                        ins = dve.tensor_copy(qall[half(hf), hp, :].rearrange("p (b x) -> p b x", x=16)[:, :, c:c + TQ], q)
                post(ins, f"s{kind}_q")

            def sample_output(kind, ob):
                wait(dve, f"s{kind}_v", NS)
                for hf in range(2):
                    src = PS[half(hf), 1, 0:P].rearrange("p (b a x) -> p a b x", b=NS, a=2)[:, :, :, hf * 4:hf * 4 + TQ]
                    step(dve.tensor_copy(oT[half(hf), ob:ob + 2, TP:T].rearrange("p a (b q) -> p a b q", q=TQ), src))

            def softmax(A, rows, kind):
                step(dve.tensor_reduce(small[0:rows, 62:63], A, AX.X, ALU.max))
                post(ts(small[0:rows, 60:61], small[0:rows, 62:63], -1.0, None, ALU.mult), f"s{kind}_nm")
                wait(dve, f"s{kind}_e", 1)
                step(dve.reciprocal(small[0:rows, 62:63], small[0:rows, 61:62]))
                post(ts(A, A, small[0:rows, 62:63], None, ALU.mult), f"s{kind}_p")

            def sample_attention(l, kind):
                sample_queries(l, kind)
                A, B, R = sA, sB, sR
                scores = PS[:, 2:5, :].rearrange("p a b -> p (a b)")[:, 0:SW]
                wait(dve, f"s{kind}_qk", 1)
                if kind == "sb":
                    ts(A[:, 0:PAST], scores[:, 0:PAST], SCALE, None, ALU.mult)
                    post(stt(A[:, PAST:SW], scores[:, PAST:SW], SCALE, cc("sb_new"), ALU.mult, ALU.add), "ssb_s")
                    wait(dve, "ssb_soft", 1)
                    step(stt(B, A, 0.0, B, ALU.max, ALU.add))
                    suffix_sums(R, B, ((0, SW),), P)
                    post(tt(A, A, R, ALU.subtract), "ssb_r")
                    sample_output("sb", OSB)
                    return
                step(ts(A, scores, SCALE, None, ALU.mult))
                g = A[:, 0:PAST].rearrange("p (n k) -> p n k", n=4)
                step(dve.tensor_reduce(small[:, 0:4], g, AX.X, ALU.add))
                step(dve.tensor_reduce(small[:, 4:5], small[:, 0:4], AX.X, ALU.min))
                step(ts(small[:, 8:12], small[:, 0:4], small[:, 4:5], None, ALU.is_le))
                step(tt(small[:, 8:12], small[:, 8:12], cc("rank"), ALU.mult))
                step(dve.tensor_reduce(small[:, 5:6], small[:, 8:12], AX.X, ALU.max))
                step(ts(small[:, 8:12], small[:, 8:12], small[:, 5:6], NEG, ALU.is_equal, ALU.mult))
                step(tt(A, A, mo_bias[:, :], ALU.add))
                step(tt(g, g, small[:, 8:12].unsqueeze(2).to_broadcast([P, 4, 256]), ALU.add))
                softmax(A, P, "mo")
                sample_output("mo", OMO)

            def dilated_sample(l):
                wait(dve, "dq_zeroed", 1)
                for g in range(3):
                    for hf in range(2):
                        q = projT[half(hf), DQ + g, TP:T].rearrange("p (b q) -> p b q", q=TQ)
                        dve.tensor_copy(dqbd.rearrange("p (b x) -> p b x", x=200)[
                            half(hf), :, g * 64 + hf * 4:g * 64 + hf * 4 + TQ], q)
                        ins = dve.tensor_copy(dqall[half(hf), g, :].rearrange("p (b x) -> p b x", x=8)[:, :, hf * 4:hf * 4 + TQ], q)
                post(ins, "sdi_q")
                A = sA[0:64, 0:DW]
                wait(dve, "sdi_qk", 1)
                step(stt(A, PS[0:64, 2:4, :].rearrange("p a b -> p (a b)")[:, 0:DW], SCALE, di_bias[:, :], ALU.mult, ALU.add))
                softmax(A, 64, "di")
                wait(dve, "sdi_v", 1)
                for hf in range(2):
                    src = PS[half(hf), 1, 0:64].rearrange("p (b x) -> p b x", b=NS)[:, :, hf * 4:hf * 4 + TQ]
                    step(dve.tensor_copy(oT[half(hf), ODI, TP:T].rearrange("p (b q) -> p b q", q=TQ), src))

            def convolution(l):
                def w(f, i):
                    return par[:, l, PCONV + 4 * f + i:PCONV + 4 * f + i + 1]
                dve.wait_ge(dma_sems["state_loaded"], 32 * (l + 1))
                dve.tensor_copy(conv_out[:, :, 0:3], projT[:, GQ:GQ + 6, TP - 3:TP])
                step(dve.tensor_copy(sconv[:, :, :, 3:7], projT[:, GQ:GQ + 6, TP:T].rearrange("p f (b q) -> p f b q", q=TQ)))
                post(dve.tensor_copy(conv_out[:, :, 3:].rearrange("p f (b q) -> p f b q", q=3), sconv[:, :, :, 4:7]),
                     "conv_state")
                for i in (3, 2, 1, 0):
                    d = 3 - i
                    for f in range(6):
                        y, x = cT[:, f, 0:TP], projT[:, GQ + f, 0:TP]
                        ys = cT[:, f, TP:T].rearrange("p (b q) -> p b q", q=TQ)
                        xs = sconv[:, f, :, i:i + TQ]
                        if i == 3:
                            ts(y, x, w(f, i), None, ALU.mult)
                            ins = ts(ys, xs, w(f, i), None, ALU.mult)
                        else:
                            stt(y[:, d:], x[:, 0:TP - d], w(f, i), y[:, d:], ALU.mult, ALU.add)
                            ins = stt(ys, xs, w(f, i), ys, ALU.mult, ALU.add)
                    if i:
                        step(ins)
                    else:
                        post(ins, "conv_y")

            def delta(l):
                convolution(l)
                post(ts(abw[0:4, :], projT[0:4, AB, :], par[0:4, l, PDTB:PDTB + 1], None, ALU.add), "ab_in")
                sq = wk[:, 0, 0:4 * T].rearrange("p (a n) -> p a n", a=4)
                rs = wk[:, 1, 0:4 * T].rearrange("p (a n) -> p a n", a=4)
                wait(dve, "conv_silu", 1)
                post(tt(sq, cT[:, 0:4, :], cT[:, 0:4, :], ALU.mult), "conv_sq")
                wait(dve, "ab_soft", 1)
                step(stt(abT[0:4, :], abw[0:4, :], 0.0, abT[0:4, :], ALU.max, ALU.add))
                post(ts(abT[0:4, :], abT[0:4, :], negA[0:4, :], -1.0, ALU.mult, ALU.mult), "ab_done")
                wait(dve, "conv_sum", 1)
                post(ts(rs, PS[:, 0:4, 0:T], EPS, None, ALU.add), "conv_ms")
                wait(dve, "conv_root", 1)
                step(dve.reciprocal(rs, rs))
                stt(cT[:, 0:2, :], cT[:, 0:2, :], SCALE, rs[:, 0:2, :], ALU.mult, ALU.mult)
                post(tt(cT[:, 2:4, :], cT[:, 2:4, :], rs[:, 2:4, :], ALU.mult), "conv_done")
                for c in range(3):
                    n = gdn_rows(c)
                    wait(dve, "gtok_mm", c + 1)
                    dve.tensor_copy(gsc[0:n, c, 0:4], PS[0:n, 2 * c + 1, 0:4])
                    post(dve.tensor_copy(gsc[0:n, c, 4:8], PS[0:n, 2 * c + 1, 32:36]), "gsc_g")
                for c in range(3):
                    n = gdn_rows(c)
                    wait(dve, "gsc_g", c + 1)
                    for slot, table, col in ((0, "seq_upto" if c == 2 else "upto", 0), (1, "ident", 4)):
                        ins = tt(gwork[c][0:n, slot, 0:4 * n].rearrange("p (h n) -> p h n", h=4),
                                 cc(table, n, n).unsqueeze(1).to_broadcast([n, 4, n]),
                                 gsc[0:n, c, col:col + 4].unsqueeze(2).to_broadcast([n, 4, n]), ALU.mult)
                    post(ins, "gbc_rhs")
                for c in range(3):
                    n = gdn_rows(c)
                    wait(dve, "gcum_mm", 3)
                    dve.tensor_copy(gsc[0:n, c, 8:12], PS[0:n, 6, c * 32:c * 32 + 4])
                    step(dve.tensor_copy(gsc[0:n, c, 12:16], PS[0:n, 6, c * 32 + 8:c * 32 + 12]))
                    post(tt(gsc[0:n, c, 24:28], gsc[0:n, c, 12:16], gsc[0:n, c, 8:12], ALU.subtract), "gsc_in")
                for c in range(3):
                    n = gdn_rows(c)
                    wait(dve, "gbc_mm", c + 1)
                    wait(dve, "g_last", c + 1)
                    gam = gwork[c][0:n, 0, 0:4 * n].rearrange("p (h n) -> p h n", h=4)
                    step(tt(gam, PS[0:n, 2 * c, 0:4 * n].rearrange("p (h n) -> p h n", h=4),
                            gsc[0:n, c, 8:12].unsqueeze(2).to_broadcast([n, 4, n]), ALU.subtract))
                    post(tt(gam, gam, cc("seq_later" if c == 2 else "later", n, n).unsqueeze(1).to_broadcast([n, 4, n]),
                            ALU.add), "gam_in")
                    wait(dve, "g_eg", c + 1)
                    kq = gwork[c][:, 6, 0:4 * n].rearrange("p (a n) -> p a n", a=4)
                    for hf in range(2):
                        def pick(ap):
                            return ap.rearrange("p (a t n) -> p a t n", a=2, t=2)[half(hf), :, hf, :]
                        tt(kq[half(hf), 2:4], cT[half(hf), 0:2, c * P:c * P + n], pick(gwork[c][:, 5, 0:4 * n]), ALU.mult)
                        ins = tt(kq[half(hf), 0:2], cT[half(hf), 2:4, c * P:c * P + n], pick(PS[:, 2 * c + 1, 0:4 * n]), ALU.mult)
                    post(ins, "gkq")
                    wait(dve, "gsc_exp", c + 1)
                    step(tt(gsc[0:n, c, 20:24], gsc[0:n, c, 16:20], gsc[0:n, c, 4:8], ALU.mult))
                    wait(dve, "gtok_copied", c + 1)
                    for dst, src, col in ((1, 1, 4), (2, 0, 20), (0, 0, 28)):
                        ins = tt(gtok[0:n, c, dst, :].rearrange("p (h d) -> p h d", h=4),
                                 gtok[0:n, c, src, :].rearrange("p (h d) -> p h d", h=4),
                                 gsc[0:n, c, col:col + 4].unsqueeze(2).to_broadcast([n, 4, HD]), ALU.mult)
                    post(ins, "gscaled")
                for c in range(3):
                    n = gdn_rows(c)
                    wait(dve, "gm_mm", c + 1)
                    wait(dve, "gam", c + 1)
                    for hf in range(2):
                        def own(slot):
                            return gwork[c][0:n, slot, 0:4 * n].rearrange("p (a t n) -> p a t n", a=2, t=2)[:, :, hf, :]
                        ps = PS[0:n, 2 * c + hf, 0:4 * n].rearrange("p (w a n) -> p w a n", w=2, a=2)
                        tt(own(1), ps[:, 0], own(0), ALU.mult)
                        tt(own(2), ps[:, 1], own(0), ALU.mult)
                    for slot in (3, 4):
                        ins = dve.tensor_copy(gwork[c][0:n, slot, 0:4 * n].rearrange("p (h n) -> p h n", h=4),
                                              cc("ident", n, n).unsqueeze(1).to_broadcast([n, 4, n]))
                    step(ins)
                for s in range(7):
                    for c in range(3):
                        n = gdn_rows(c)
                        if s < gdn_levels(c):
                            if s:
                                wait(dve, f"g{c}_t", s)
                            post(tt(gwork[c][0:n, 0, 0:4 * n].rearrange("p (h n) -> p h n", h=4),
                                    gwork[c][0:n, 1, 0:4 * n].rearrange("p (h n) -> p h n", h=4),
                                    cc(f"lvl{s}", n, n).unsqueeze(1).to_broadcast([n, 4, n]), ALU.mult), f"g{c}_bt")
                    for c in range(3):
                        n = gdn_rows(c)
                        if s < gdn_levels(c):
                            wait(dve, f"g{c}_y", s + 1)
                            tt(gwork[c][0:n, 3, 0:4 * n], gwork[c][0:n, 3, 0:4 * n], PS[0:n, 2 * c, 0:4 * n], ALU.subtract)
                            post(tt(gwork[c][0:n, 4, 0:4 * n], gwork[c][0:n, 4, 0:4 * n], PS[0:n, 2 * c + 1, 0:4 * n],
                                    ALU.subtract), f"g{c}_t")
                for c in range(3):
                    n = gdn_rows(c)
                    wait(dve, "go_mm", c + 1)
                    step(dve.tensor_copy(oT[:, OGD:OGD + 2, c * P:c * P + n],
                                         PS[:, 2 * c, 0:2 * n].rearrange("p (a n) -> p a n", a=2)))
                    if c == 0:
                        wait(dve, "gs_mm", 1)
                        post(dve.tensor_copy(pS[:, :, :], PS[:, 6, 0:P].rearrange("p (a n) -> p a n", a=2)), "pstate")
                        wait(dve, "pstate", 1)
                    if c == 1:
                        wait(dve, "gs_mm", 2)
                        for h in range(4):
                            hf, hp = half(h % 2), h // 2
                            ins = stt(pS[hf, hp, :], pS[hf, hp, :], glast[hf, 1, h:h + 1], PS[hf, 7, hp * HD:(hp + 1) * HD],
                                      ALU.mult, ALU.add)
                        post(ins, "pstate")
                wait(dve, "gvnew", 3)
                dve.wait_ge(dma_sems["rows_stored"], 16 * 3 * (l + 1))
                vm = mergedT.rearrange("p a b -> p (a b)")
                for h in range(4):
                    ins = tt(vm[0:TS, h * 512:(h + 1) * 512].rearrange("p (b d) -> p b d", b=NS),
                             gtok[0:TS, 2, 3, h * HD:(h + 1) * HD].unsqueeze(1).to_broadcast([TS, NS, HD]),
                             cc("seq_of", TS).unsqueeze(2).to_broadcast([TS, NS, HD]), ALU.mult)
                post(ins, "gvm")
                for hf in range(2):
                    gl = glast[half(hf), 2, :].rearrange("p (a t b) -> p a t b", a=2, t=2)[:, :, hf, :]
                    ins = tt(sS[half(hf)], sS[half(hf)], gl.unsqueeze(3).to_broadcast([64, 2, NS, HD]), ALU.mult)
                step(ins)
                wait(dve, "gss_mm", 1)
                post(tt(sS[:, :, :, :], sS[:, :, :, :], PS[:, 6:8, :].rearrange("p a (b d) -> p a b d", b=NS), ALU.add),
                     "sstate")
                post(tt(squares[:, 0:2, :], oT[:, OGD:OGD + 2, :], oT[:, OGD:OGD + 2, :], ALU.mult), "go_sq")
                wait(dve, "go_sum", 1)
                post(ts(squares[:, 2:4, :], PS[:, 0:2, 0:T], 1.0 / HD, EPS, ALU.mult, ALU.add), "go_rs")
                wait(dve, "go_root", 1)
                step(dve.reciprocal(squares[:, 2:4, :], squares[:, 2:4, :]))
                step(stt(oT[:, OGD:OGD + 2, :], oT[:, OGD:OGD + 2, :], par[:, l, PGN:PGN + 1], squares[:, 2:4, :],
                         ALU.mult, ALU.mult))
                wait(dve, "z_silu", 1)
                post(tt(oT[:, OGD:OGD + 2, :], oT[:, OGD:OGD + 2, :], cT[:, 4:6, :], ALU.mult), "o_done")
                wait(dve, "o_done", 1)

            def merge(l):
                for m in range(KD):
                    t = wk[:, m % 2, 0:4 * T].rearrange("p (b n) -> p b n", b=4)
                    for br in range(4):
                        n = 4 * m + br
                        wait(dve, "gate_evac", n + 1)
                        wait(dve, "br_mm", n + 1)
                        post(tt(t[:, br, :], PS[:, 2 + n % 4, 0:T], gate[:, n % 8, :], ALU.mult), "br_evac")
                    wait(dve, "br_evac", 4 * m + 4)
                    step(tt(t[:, 0:2, :], t[:, 0:2, :], t[:, 2:4, :], ALU.add))
                    post(tt(mergedT[:, m, :], t[:, 0, :], t[:, 1, :], ALU.add), "merged")
                for m in range(KD):
                    wait(dve, "out_mm", m + 1)
                    post(tt(xT[:, m, :], xT[:, m, :], PS[:, m % 2, 0:T], ALU.add), "out_evac")
                wait(dve, "out_evac", KD)

            def feed_forward(t, nblk, e=0):
                looped = not isinstance(e, int)
                for i in range(nblk):
                    dve.wait_ge(S.sem(t + "gu_mm"), e * (2 * nblk) + (2 * i + 2))
                    dve.wait_ge(S.sem(t + "silu"), e * nblk + (i + 1))
                    post(tt(actT[:, i, :], wk[:, 1, (i % 2) * T:(i % 2 + 1) * T], PS[:, (2 * i + 1) % 4, 0:T], ALU.mult),
                         t + "act")
                for m in range(KD):
                    dve.wait_ge(S.sem(t + "dn_mm"), e * KD + (m + 1))
                    if looped:
                        tmp = wk[:, 0, (m % 2) * T:(m % 2 + 1) * T]
                        post(tt(tmp, PS[:, 4 + m % 2, 0:T], comb[:, bass.ds(e, 1), :].rearrange("p a n -> p (a n)"), ALU.mult),
                             t + "dn_evac")
                        dve.wait_ge(S.sem(t + "dn_evac"), e * KD + (m + 1))
                        post(tt(xT[:, m, :], xT[:, m, :], tmp, ALU.add), "moe_added")
                    else:
                        post(tt(xT[:, m, :], xT[:, m, :], PS[:, 4 + m % 2, 0:T], ALU.add), t + "dn_evac")

            def routing():
                wait(dve, "router_mm", 1)
                for t in range(3):
                    n = gdn_rows(t)
                    lg, one, two, c = (rlog[0:n, t, i, :] for i in range(4))

                    def col(i):
                        return toks[0:n, t, i:i + 1]
                    step(dve.tensor_copy(lg, PS[0:n, 6, t * 8:t * 8 + 8]))

                    def pick(out, top, rank):
                        step(dve.tensor_reduce(top, lg, AX.X, ALU.max))
                        step(ts(out, lg, top, None, ALU.is_ge))
                        step(tt(out, out, cc("down", n), ALU.mult))
                        step(dve.tensor_reduce(rank, out, AX.X, ALU.max))
                        step(ts(out, out, rank, None, ALU.is_equal))
                    pick(one, col(0), col(2))
                    step(stt(lg, one, NEG, lg, ALU.mult, ALU.add))
                    pick(two, col(1), col(3))
                    post(tt(col(4), col(1), col(0), ALU.subtract), "route_in")
                    dve.wait_ge(S.sem("route_exp"), t + 1)
                    step(ts(col(6), col(5), 1.0, None, ALU.add))
                    step(dve.reciprocal(col(7), col(6)))
                    step(tt(col(8), col(7), col(5), ALU.mult))
                    step(ts(one, one, col(7), None, ALU.mult))
                    step(stt(c, two, col(8), one, ALU.mult, ALU.add))
                for i in range(6):
                    t, h = i // 2, i % 2
                    n = gdn_rows(t)
                    if i >= 2:
                        dve.wait_ge(S.sem("comb_mm"), i - 1)
                    post(tt(wk[0:n, i % 2, 0:4 * n].rearrange("p (e n) -> p e n", e=4),
                            cc("ident", n, n).unsqueeze(1).to_broadcast([n, 4, n]),
                            rlog[0:n, t, 3, 4 * h:4 * h + 4].unsqueeze(2).to_broadcast([n, 4, n]), ALU.mult), "comb_rhs")
                dve.wait_ge(S.sem("comb_mm"), 6)
                dve.wait_ge(S.sem("comb_copied"), 6)

            bias_tables()
            dve.wait_ge(dma_sems["x_loaded"], 48)
            for l in range(L):
                S.layer = l
                norm("mix", PMIX, l)
                prompt_attention(l)
                sample_attention(l, "sb")
                sample_attention(l, "mo")
                dilated_sample(l)
                delta(l)
                merge(l)
                norm("ffn", PFFN, l)
                if l == 0:
                    feed_forward("f", FB)
                    wait(dve, "fdn_evac", KD, 0)
            routing()
            with dve.Fori(0, NEXP) as e:
                S.times = NEXP
                feed_forward("e", EB, e)
                S.times = 1
            dve.wait_ge(S.sem("moe_added"), NEXP * KD)
            norm("fin", PFIN, 0)

        @block.gpsimd
        def _(pool):
            step = Chain(pool, steps["pool"]).step
            S.layer = 0
            out = dma_sems["outputs_stored"]
            rows_out = dma_sems["rows_stored"]
            windows = dma_sems["windows_stored"]
            pool.memset(abT[:, :], 0.0)
            pool.memset(nwm[:, :, :], 0.0)
            pool.memset(qall[:, :, :], 0.0)
            pool.memset(dqall[:, :, :], 0.0)
            scratch = A["scratch"]
            wait(pool, "table_sum", 10)
            pool.dma_start(scratch, region[:, :]).then_inc(dma_sems["bias_stored"], 16)
            pool.wait_ge(dma_sems["bias_stored"], 16)
            for l in range(L):
                S.layer = l
                if l:
                    wait(pool, "o_done", 1, l - 1)
                    pool.wait_ge(out, stored_after(l - 1))
                for t in range(2):
                    pool.dma_start(prompt_bias[:, :, t * TP:(t + 1) * TP],
                                   bass.AP(scratch.tensor, TP - 1 - t * P, [[5120 - 1, P], [2 * TP, 10], [1, TP]])
                                   ).then_inc(dma_sems["bias_loaded"], 16)
                pool.dma_start(sconv[:, :, :, 0:3], A["conv"][l]).then_inc(dma_sems["state_loaded"], 16)
                wait(pool, "in_evac", NBLK)
                for i, (a, b) in enumerate(((SBK, GZ), (MK, DQ), (DK, AB))):
                    pool.dma_start(A["rows"][l, :, (0, 10, 14)[i]:(0, 10, 14)[i] + b - a, :], projT[:, a:b, :]
                                   ).then_inc(rows_out, 16)
                for name, keep in (("dk0", 128), ("dk1", 512)):
                    pool.dma_start(A[name + "_out"][l], A[name][l, :, :, TQ:keep]).then_inc(windows, 16)
                pool.dma_start(A["dk2a_out"][l], A["dk2"][l, :, :, 4:16, :]).then_inc(windows, 16)
                pool.dma_start(A["dk2b_out"][l], A["dk2"][l, :, :, 0:4, 1:64]).then_inc(windows, 16)
                for name, keep in (("dv0", 128), ("dv1", 512), ("dv2", 1024)):
                    pool.dma_start(A[name + "_out"][l].rearrange("t b d -> t (b d)"),
                                   A[name][l, TQ:keep].rearrange("t b d -> t (b d)")).then_inc(windows, 16)
                wait(pool, "at_o", 10)
                post(pool.memset(qbd, 0.0), "q_zeroed")
                pool.dma_start(sS, A["S"][l]).then_inc(dma_sems["state_loaded"], 16)
                wait(pool, "smo_qk", 1)
                post(pool.memset(dqbd, 0.0), "dq_zeroed")
                wait(pool, "conv_state", 1)
                pool.dma_start(A["conv_out"][l], conv_out[:, :, :]).then_inc(out, 16)
                wait(pool, "pstate", 2)
                pool.dma_start(A["pS_out"][l], pS[:, :, :]).then_inc(out, 16)
                wait(pool, "sstate", 1)
                pool.dma_start(A["sS_out"][l], sS).then_inc(out, 16)
            wait(pool, "norm_h", NORM["fin"])
            pool.dma_start(A["y_out"], hT[:, :, :]).then_inc(out, 16)
            pool.wait_ge(out, stored_after(L - 1) + 16)
            pool.wait_ge(rows_out, 16 * 3 * L)
            pool.wait_ge(windows, 16 * 7 * L)

        return {k: (v[0] if v[1] else 0) for k, v in S.count.items()}


def stored_after(l):
    return 16 * 3 * (l + 1)


def laid_out(x):
    f = {k: np.asarray(v) for k, v in x.items()}

    def tr(a, *axes):
        return np.ascontiguousarray(np.transpose(a, axes))

    def feature_blocks(v):
        return np.swapaxes(v.reshape(v.shape[:-1] + (-1, P)), -1, -2)

    o = {}
    tok = np.concatenate([f["x_prompt"].reshape(TP, D), f["x_sample"].reshape(TS, D)])
    o["x"] = tr(tok.reshape(T, KD, P), 2, 1, 0)
    w = f["w_in"]
    zero = np.zeros((L, D, 28), np.float32)
    cols = np.concatenate([w[:, :, 0:1536], w[:, :, 1536:1792], w[:, :, 1800:2568], w[:, :, 2568:3720],
                           w[:, :, 1792:1796], zero, w[:, :, 1796:1800], zero, np.zeros((L, D, 64), np.float32)], 2)
    o["in"] = tr(cols.reshape(L, KD, P, NBLK // 2, 2, P), 0, 3, 2, 4, 1, 5).reshape(L, NBLK // 2, P, SLOT)
    g = w[:, :, 3720:].reshape(L, KD, P, 2, 2, KD, P)
    o["gate"] = tr(g, 0, 5, 3, 2, 4, 1, 6).reshape(L, 2 * KD, P, SLOT)
    br = np.concatenate([f["w_br_sb"], f["w_br_gdn"], f["w_br_moba"], f["w_br_dil"]], 1)
    o["br"] = tr(br.reshape(L, 7, P, KD // 2, 2, P), 0, 3, 2, 4, 1, 5).reshape(L, KD // 2, P, 14 * P)
    o["out"] = tr(f["w_out"].reshape(L, KD, P, KD // 2, 2, P), 0, 3, 2, 4, 1, 5).reshape(L, KD // 2, P, SLOT)

    def gate_up(wg, wu):
        both = np.stack([wg, wu], -3).reshape((-1, 2, KD, P, wg.shape[-1] // P, P))
        return tr(both, 0, 4, 3, 1, 2, 5).reshape(-1, P, SLOT)

    def down(wd):
        nb = wd.shape[-2] // P
        blocks = wd.reshape(-1, nb, P, KD, P).transpose(0, 3, 1, 2, 4).reshape(-1, 16, P, P)
        return tr(blocks, 0, 2, 1, 3).reshape(-1, P, SLOT)
    o["fgu"], o["fdn"] = gate_up(f["ffn_w_gate"], f["ffn_w_up"]), down(f["ffn_w_down"])
    o["egu"], o["edn"] = gate_up(f["moe_w_gate"][0], f["moe_w_up"][0]), down(f["moe_w_down"][0])
    o["router"] = tr(f["moe_router"][0].reshape(KD, P, NEXP), 1, 0, 2)
    for kind, name in (("sb", "cache_sb_kv"), ("mo", "cache_moba_kv")):
        c = f[name].reshape(-1, PAGE, 2, 256)
        o[kind + "k"] = tr(c[:, :, 0].reshape(-1, PAGE, 2, P), 0, 3, 2, 1).reshape(-1, P, 256)
        o[kind + "v"] = np.ascontiguousarray(c[:, :, 1])
    for g in range(3):
        c = f[f"cache_dil_kv_{g}"].reshape(L, NS, -1, 2, P)
        o[f"dk{g}"] = tr(c[:, :, :, 0], 0, 3, 1, 2)
        o[f"dv{g}"] = tr(c[:, :, :, 1], 0, 2, 1, 3)
    o["dk2"] = tr(o["dk2"].reshape(L, P, NS, 64, 16), 0, 1, 2, 4, 3)
    o["conv"] = tr(f["state_gdn_conv"].reshape(L, NS, 3, 6, P), 0, 4, 3, 1, 2)
    o["S"] = tr(f["state_gdn_S"].reshape(L, NS, 2, 2, HD, HD), 0, 3, 4, 2, 1, 5).reshape(L, P, 2, NS, HD)
    par = np.zeros((P, L, NPAR), np.float32)
    par[:, :, PMIX:PMIX + 8] = feature_blocks(f["norm_mix"]).transpose(1, 0, 2)
    par[:, :, PFFN:PFFN + 8] = feature_blocks(f["norm_ffn"]).transpose(1, 0, 2)
    par[:, :, PCONV:PCONV + 24] = f["gdn_conv_w"].reshape(L, 4, 6, P).transpose(3, 0, 2, 1).reshape(P, L, 24)
    par[:, :, PGN] = np.concatenate([f["gdn_norm_w"]] * 2, 1).T
    par[0:4, :, PALOG] = f["gdn_a_log"].T
    par[0:4, :, PDTB] = f["gdn_dt_bias"].T
    par[:, :, PFIN:PFIN + 8] = feature_blocks(f["final_norm"])[:, None, :]
    o["par"] = par
    rel = f["rel_bias"]
    mo = np.zeros((TQ, BUCKETS, NS, 4, TQ), np.float32)
    di = np.zeros((TQ, BUCKETS, 3, NS, 2, TQ), np.float32)
    for t in range(TQ):
        mo[t, :, :, :, t] = rel[:, None, 0:4]
        di[t, :, :, :, :, t] = rel[:, 4:10].reshape(BUCKETS, 3, 1, 2)
    o["pages"] = f["page_table"].astype(np.int32).reshape(1, NS * NPG)
    C = tables()
    o["const"] = np.concatenate([C[n] for n in RESIDENT], 1)
    o["setup"] = np.concatenate([C[n] for n in SETUP] + [np.pad(rel, ((0, P - BUCKETS), (0, 0))), mo.reshape(P, P),
                                                         di.reshape(P, 3 * 64)], 1)
    return o


OUTPUTS = {
    "y_out": (P, KD, T), "rows": (L, P, 20, T), "dk0_out": (L, P, NS, 124), "dk1_out": (L, P, NS, 508),
    "dk2a_out": (L, P, NS, 12, 64), "dk2b_out": (L, P, NS, 4, 63), "dv0_out": (L, 124, NS, P),
    "dv1_out": (L, 508, NS, P), "dv2_out": (L, 1020, NS, P), "conv_out": (L, P, 6, 27), "pS_out": (L, P, 2, HD),
    "sS_out": (L, P, 2, NS, HD),
}


def given_back(r):
    y = r["y_out"].transpose(2, 1, 0).reshape(T, D)
    rows = r["rows"].transpose(0, 3, 2, 1)

    def kv(first, n, heads):
        a = rows[:, :, first:first + 2 * n].reshape(L, T, 2, heads, HD)
        return a[:, None, :TP], a[:, TP:].reshape(L, NS, TQ, 2, heads, HD)
    p_sb, s_sb = kv(0, 2, 4)
    p_mo, s_mo = kv(10, 2, 4)
    dil = rows[:, :, 14:20].reshape(L, T, 2, 3, 2, HD)
    conv = r["conv_out"].transpose(0, 3, 2, 1).reshape(L, 27, 768)
    p_conv, s_conv = conv[:, None, 0:3], conv[:, 3:].reshape(L, NS, 3, 768)
    pS = r["pS_out"].reshape(L, 2, HD, 2, HD).transpose(0, 3, 1, 2, 4).reshape(L, 1, 4, HD, HD)
    sS = r["sS_out"].reshape(L, 2, HD, 2, NS, HD).transpose(0, 4, 3, 1, 2, 5).reshape(L, NS, 4, HD, HD)
    out = [y[:TP].reshape(1, TP, D), y[TP:].reshape(NS, TQ, D), p_sb, s_sb, p_mo, s_mo, p_conv, s_conv, pS, sS]
    k2 = np.zeros((L, P, NS, 64, 16), np.float32)
    k2[..., 0:12] = r["dk2a_out"].transpose(0, 1, 2, 4, 3)
    k2[:, :, :, 0:63, 12:16] = r["dk2b_out"].transpose(0, 1, 2, 4, 3)
    ks = [r["dk0_out"], r["dk1_out"], k2.reshape(L, P, NS, PAST)[..., 0:PAST - TQ]]
    for g in range(3):
        keep = min(DIL[g][0], TP)
        out.append(dil[:, None, TP - keep:TP, :, g])
        old = np.stack([ks[g].transpose(0, 2, 3, 1), r[f"dv{g}_out"].transpose(0, 2, 1, 3)], 3)
        old = old.reshape(L, NS, -1, 2, 2, HD)
        out.append(np.concatenate([old, dil[:, TP:, :, g].reshape(L, NS, TQ, 2, 2, HD)], 2))
    return tuple(np.ascontiguousarray(a) for a in out)


def declare(nc, arrays):
    A = {}
    for n, a in arrays.items():
        A[n] = nc.dram_tensor("in_" + n, a.shape, mybir.dt.from_np(a.dtype), kind="ExternalInput").ap()
    for n, shape in OUTPUTS.items():
        A[n] = nc.dram_tensor("out_" + n, shape, F32, kind="ExternalOutput").ap()
    A["scratch"] = nc.dram_tensor("bias_scratch", (P, 5120), F32, kind="Internal").ap()
    A["n_phys"] = arrays["sbk"].shape[0] // L
    return A


def kernel(**inputs):
    import concourse.bacc as bacc
    from concourse.bass_utils import run_bass_kernel_spmd as run

    arrays = laid_out(inputs)
    count = bacc.Bacc("TRN2", target_bir_lowering=False, num_devices=1)
    per = program(count, declare(count, arrays), {})
    nc = bacc.Bacc("TRN2", target_bir_lowering=False, num_devices=1)
    program(nc, declare(nc, arrays), per)
    r = run(nc, [{"in_" + n: a for n, a in arrays.items()}], core_ids=[0]).results[0]
    return given_back({n: np.asarray(r["out_" + n]) for n in OUTPUTS})
```

```python
import math
from contextlib import ExitStack

import numpy as np
import concourse.bass as bass
from concourse import mybir

F32 = mybir.dt.float32
I32 = mybir.dt.int32
ALU = mybir.AluOpType
ACT = mybir.ActivationFunctionType
AX = mybir.AxisListType

P = 128
D = 1024
KD = D // P
TP = 256
NS, TQ = 8, 4
TS = NS * TQ
T = TP + TS
L = 2
PAST = 1024
PAGE = 128
NPG = PAST // PAGE
HD = 64
SCALE = HD ** -0.5
EPS = 1e-6
NEG = -1e30
DFF, DEXP, NEXP = 2816, 3584, 8
FB, EB = DFF // P, DEXP // P
DIL = ((128, 1), (512, 4), (2048, 16))
BUCKETS, MAXDIST = 32, 2048
SLOTS = 6
SLOT = 2048
EARLY = 16
CAP = P
EXTRA = 4
EC = DEXP // 512
EU = 4 * EC + EB // 2

SBQ, SBK, SBV, GQ, GK, GV, GZ, MQ, MK, MV, DQ, DK, DV, AB, NBLK = 0, 2, 4, 6, 8, 10, 12, 14, 16, 18, 20, 23, 26, 29, 30
IN_ORDER = [0, 1, 2] + list(range(MQ // 2, NBLK // 2)) + list(range(GQ // 2, MQ // 2))
IN_BLOCKS = [2 * u + h for u in IN_ORDER for h in range(2)]
IN_FIRST = NBLK - (MQ - GQ)
OSB, OGD, OMO, ODI, NOB = 0, 2, 4, 6, 7
DCOL = {1: 0, 0: 512, 2: 640}
DNEW = 896
DW = DNEW + 3 * TS
SW = PAST + TS
PMIX, PFFN, PCONV, PGN, PALOG, PDTB, PFIN, NPAR = 0, 8, 16, 40, 41, 42, 43, 51


def bucket(dist):
    dist = np.maximum(dist, 0)
    exact = BUCKETS // 2
    d = np.maximum(dist, exact).astype(np.float32)
    big = exact + (np.log(d / np.float32(exact)) / np.float32(math.log(MAXDIST / exact))
                   * np.float32(BUCKETS - exact)).astype(np.int32)
    return np.where(dist < exact, dist, np.minimum(big, BUCKETS - 1))


def tables():
    c = {}
    j, i = np.arange(P)[:, None], np.arange(P)[None, :]
    c["ident"] = (j == i)
    c["ones"] = np.ones((P, P))
    c["head_ones"] = (j // HD == i // HD)
    c["upto"] = (j <= i)
    c["later"] = np.where(i >= j, 0.0, NEG)
    same = (j // TQ == i // TQ)
    c["seq_ones"] = same[:, :TS]
    c["seq_upto"] = (same & (j <= i))[:, :TS]
    c["seq_later"] = np.where(same & (i >= j), 0.0, NEG)[:, :TS]
    for s in range(7):
        b = 1 << s
        c[f"lvl{s}"] = (j // (2 * b) == i // (2 * b)) & ((j // b) % 2 == 0) & ((i // b) % 2 == 1)
    c["seq_of"] = (j // TQ == np.arange(NS)[None, :])
    c["rank"] = np.broadcast_to(np.arange(1, 5)[None, :], (P, 4))
    c["slot_no"] = np.broadcast_to(np.where(np.arange(P) < CAP, np.arange(P), -1000)[None, :], (P, P))
    c["down"] = np.broadcast_to(np.arange(NEXP, 0, -1)[None, :], (P, NEXP))
    q = np.arange(P)[:, None]
    k = np.arange(TP)[None, :]
    c["sb_prompt"] = np.concatenate([np.where(k < q + t * P, 0.0, NEG) for t in range(2)], 1)
    r = np.arange(P)
    rb, rq = r // 16, r % 4
    kb, kt = np.arange(TS) // TQ, np.arange(TS) % TQ
    mine = rb[:, None] == kb[None, :]
    c["sb_new"] = np.where(mine & (kt[None] < rq[:, None]), 0.0, NEG)
    c["mo_new"] = np.where(mine & (kt[None] <= rq[:, None]), 0.0, NEG)
    r = np.arange(64)
    rb, rq = r // 8, r % 4
    mask = np.full((P, DW), NEG)
    hot = np.zeros((P, DW))
    pos = {1: 512 + np.arange(512), 0: 896 + np.arange(128),
           2: (16 * np.arange(64)[None, :] + np.arange(4)[:, None]).reshape(-1)}
    for g, (win, dil) in enumerate(DIL):
        for kpos, col, own in ((pos[g], DCOL[g], None), (PAST + kt, DNEW + g * TS, kb)):
            n = len(kpos)
            dist = PAST + rq[:, None] - kpos[None, :]
            ok = (dist >= 0) & (dist % dil == 0) & (dist <= win)
            if own is not None:
                ok &= rb[:, None] == own[None, :]
            mask[:64, col:col + n] = np.where(ok, 0.0, NEG)
            for t in range(TQ):
                bk = bucket(PAST + t - kpos)
                hot[t * BUCKETS + bk, col + np.arange(n)] = 1
    c["di_sample"], c["di_hot"] = mask, hot
    hot = np.zeros((P, SW))
    kpos = np.concatenate([np.arange(PAST), PAST + kt])
    for t in range(TQ):
        hot[t * BUCKETS + bucket(PAST + t - kpos), np.arange(SW)] = 1
    c["mo_hot"] = hot
    dist = TP - 1 - np.arange(2 * TP)
    hot = np.zeros((P, 2 * TP))
    hot[bucket(dist), np.arange(2 * TP)] = 1
    c["pr_hot"] = hot
    masks = [np.where((dist >= 0) & (dist % dil == 0) & (dist <= win), 0.0, NEG) for win, dil in ((TP, 1),) + DIL]
    c["pr_mask"] = np.broadcast_to(np.concatenate(masks)[None, :], (P, 8 * TP))
    return {n: np.ascontiguousarray(v, dtype=np.float32) for n, v in c.items()}


RESIDENT = (["ident", "ones", "head_ones", "upto", "later", "seq_ones", "seq_upto", "seq_later"]
            + [f"lvl{s}" for s in range(7)] + ["seq_of", "rank", "down", "slot_no", "sb_prompt", "sb_new"])
SETUP = ["mo_new", "mo_hot", "di_sample", "di_hot", "pr_hot", "pr_mask"]


def columns(names, c):
    at, n = {}, 0
    for name in names:
        at[name] = (n, n + c[name].shape[1])
        n += c[name].shape[1]
    return at, n


SHARED = {}
for _sem, _turns in (
        ("sample_q", (("ssb_q", 1), ("smo_q", 1), ("sdi_q", 1))), ("sample_k", (("ssb_k", NS), ("smo_k", NS))),
        ("sample_qk", (("ssb_qk", 1), ("smo_qk", 1), ("sdi_qk", 1))), ("sample_v", (("ssb_v", NS), ("smo_v", NS))),
        ("sample_pt", (("ssb_pt", 3), ("smo_pt", 3), ("sdi_pt", 1))), ("sample_ptcopied", (("ssb_ptcopied", 3), ("smo_ptcopied", 3), ("sdi_ptcopied", 2))),
        ("sample_out", (("ssb_out", 4), ("smo_out", 4), ("sdi_out", 1))),
        ("sample_outT", (("ssb_outT", 1), ("smo_outT", 1), ("sdi_outT", 1))),
        ("sample_p", (("smo_p", 1), ("sdi_p", 1))), ("ssb_vector", (("ssb_s", 1), ("ssb_r", 1))),
        ("ssb_scalar", (("ssb_soft", 1), ("ssb_p", 1))), ("queries_zeroed", (("q_zeroed", 1), ("dq_zeroed", 1))),
        ("sample_nm", (("smo_nm", 1), ("sdi_nm", 1))), ("sample_e", (("smo_e", 1), ("sdi_e", 1))),
        ("conv_vector", (("conv_y", 1), ("ab_in", 1), ("conv_sq", 1), ("ab_done", 1), ("conv_ms", 1), ("conv_done", 1))),
        ("conv_scalar", (("conv_silu", 1), ("beta_done", 1), ("ab_soft", 1), ("conv_root", 1))),
        ("go_vector", (("go_sq", 1), ("go_rs", 1)))):
    _n = 0
    for _name, _k in _turns:
        SHARED[_name] = (_sem, _n)
        _n += _k


class Signals:

    def __init__(self, nc, ctx, per):
        self.nc, self.ctx, self.per = nc, ctx, per
        self.sems, self.count, self.times, self.layer = {}, {}, 1, 0

    def sem(self, name):
        if name not in self.sems:
            self.sems[name] = self.ctx.enter_context(self.nc.semaphore(name))
        return self.sems[name]

    def post(self, ins, name, n=1):
        name = SHARED.get(name, (name, 0))[0]
        ins.then_inc(self.sem(name), n)
        c = self.count.setdefault(name, [0] * L)
        c[self.layer] += n * self.times
        return ins

    def wait(self, eng, name, k, layer=None):
        layer = self.layer if layer is None else layer
        if name in SHARED:
            name, k = SHARED[name][0], SHARED[name][1] + k
        base = layer * self.per.get(name, 0)
        if isinstance(k, int) and base + k <= 0:
            return
        eng.wait_ge(self.sem(name), base + k)


class Chain:

    def __init__(self, eng, sem):
        self.eng, self.sem, self.n = eng, sem, 0

    def step(self, ins):
        ins.then_inc(self.sem, 1)
        self.n += 1
        self.eng.wait_ge(self.sem, self.n)


PAGED = ("sbk", "sbv", "mok", "mov")


def plan():
    u = []
    for l in range(L):
        u += [("in", l, unit, 1, "in_mm", 2 * i + 2) for i, unit in enumerate(IN_ORDER)]
        gates = [("gate", l, i, 1, "gate_mm", 2 * i + 2) for i in range(2 * KD)]
        for kind, early in (("sb", gates[0:1]), ("mo", gates[1:3])):
            u += [(kind + "k", l, b, NPG, f"s{kind}_k", b + 1) for b in range(NS)]
            u += early
            u += [(kind + "v", l, b, NPG, f"s{kind}_v", b + 1) for b in range(NS)]
        u += [("dk1", l, 0, 1, "sdi_k", 1), ("dk1", l, 1, 1, "sdi_k", 2), ("dk2", l, 0, 1, "sdi_k", 3),
              ("d0", l, 0, 2, "sdi_v", 1), gates[3], ("dv1", l, 0, 1, "sdi_v", 1), ("dv1", l, 1, 1, "sdi_v", 1),
              ("dv2", l, 0, 4, "sdi_v", 1)]
        u += gates[4:EARLY // 2]
        for m2 in range(KD // 2):
            u += [("br", l, m2, 1, "br_mm", 8 * m2 + 8)]
            u += gates[EARLY // 2 + 4 * m2:EARLY // 2 + 4 * m2 + 4]
        u += [("out", l, i, 1, "out_mm", 2 * i + 2) for i in range(KD // 2)]
        if l == 0:
            u += [("fgu", l, i, 1, "fgu_mm", 2 * i + 2) for i in range(FB)]
            u += [("fdn", l, i, 1, "fdn_mm", (16 * i + 15) // FB + 1) for i in range(KD * FB // 16)]
    base = len(u)
    u += [("moe", 1, i, 1, "moe_unit", i + 1) for i in range(EU)]
    land, total, half_total = [], [0] * SLOTS, [0] * SLOTS
    for n, x in enumerate(u):
        by_pool = NPG // 2 if x[0] in PAGED else 0
        total[n % SLOTS] += 16 * (x[3] - by_pool)
        half_total[n % SLOTS] += 16 * by_pool
        land.append((total[n % SLOTS], half_total[n % SLOTS]))
    return u, land, base


def attention_units():
    u = [("sb", h, [(SBQ + h // 2, SBK + h // 2, h % 2, h // 2, None)], OSB + h // 2) for h in range(4)]
    u += [("mo", h, [(MQ + h // 2, MK + h // 2, h % 2, 2 + h // 2, h)], OMO + h // 2) for h in range(4)]
    u += [("di", h, [(DQ + g, DK + g, h, 4 + g, 4 + 2 * g + h) for g in range(3)], ODI) for h in range(2)]
    return u


def late_blocks(u):
    return range(IN_FIRST, IN_FIRST + 2) if u == 0 else range(IN_FIRST + u + 1, min(IN_FIRST + u + 2, NBLK))


def late_bank(n):
    return 1 if n == IN_FIRST + 1 else 7


def score_banks(u):
    return [2, 3, 4] if attention_units()[u][0] == "di" else [2 + u % 2]


VB = [SBV, SBV + 1, MV, MV + 1, DV, DV + 1, DV + 2]
NORM = {"mix": 1, "ffn": 2, "fin": 3}
VGROUPS = [(t, a, b) for t in range(3) for a, b in ((0, 4), (4, 7))]


def gdn_rows(c):
    return TS if c == 2 else P


def gdn_levels(c):
    return 2 if c == 2 else 7


def half(h):
    return slice(64 * h, 64 * h + 64)


def program(nc, A, per):
    units, landing, moe_base = plan()
    C = tables()
    cat, cn = columns(RESIDENT, C)
    sat, sn = columns(SETUP, C)

    with ExitStack() as ctx:
        def sb(name, *shape, dt=F32):
            return ctx.enter_context(nc.sbuf_tensor(name, list(shape), dt))

        xT = sb("xT", P, KD, T)
        hT = sb("hT", P, KD, T)
        projT = sb("projT", P, NBLK, T)

        def gate(g):
            i = g % EARLY
            return projT[:, i if i < MQ else NBLK - EARLY + i, :]

        mergedT = projT[:, DQ:DQ + KD, :]
        gosq = mergedT
        actT = projT
        oT = sb("oT", P, NOB, T)
        rstd = sb("rstd", P, T)
        ring = sb("ring", P, SLOTS, SLOT)
        const = sb("const", P, cn)
        par = sb("par", P, L, NPAR)
        router = sb("router", P, KD, NEXP)
        pages = sb("pages", 1, NS * NPG, dt=I32)
        wk = sb("wk", P, 2, 3584)
        wkA = [wk[:, i, 0:1536] for i in range(2)]
        wkB = [wk[:, i, 1536:2048] for i in range(2)]
        wkR = [wk[:, i, 2048:2560] for i in range(2)]
        pt = [wk[:, i, 2560:2944] for i in range(2)]
        sA, sB, sR = (wk[:, 0, i * SW:(i + 1) * SW] for i in range(3))
        qbd = wk[:, 1, 0:8 * 272]
        dqbd = wk[:, 1, 0:8 * 200]
        spt = wk[:, 1, 2176:2176 + 9 * P].rearrange("p (g n) -> p g n", g=9)
        so = wk[0:16, 0, 4 * T:4 * T + 2048]
        setup = wk[:, :, :].rearrange("p a b -> p (a b)")
        rel = setup[0:BUCKETS, sn:sn + 10]
        rel_mo, rel_di = setup[:, sn + 10:sn + 138], setup[:, sn + 138:sn + 330]
        region = sb("region", P, 5120)
        prompt_bias = region[:, :].rearrange("p (h n) -> p h n", h=10)
        gtok = region[:, 0:3840].rearrange("p (c i n) -> p c i n", c=3, i=5)
        sS = region[:, 3840:4864].rearrange("p (a b d) -> p a b d", a=2, b=NS)
        mo_bias = sb("mo_bias", P, SW)
        di_bias = sb("di_bias", 64, DW)
        vtok = sb("vtok", P, 3, NOB, P)
        qall = sb("qall", P, 2, P)
        dqall = sb("dqall", P, 3, 64)
        small = sb("small", P, 64)
        htok = projT[:, :, :].rearrange("p a b -> p (a b)")[:, 0:3 * D].rearrange("p (t n) -> p t n", t=3)
        hgT = projT[:, :, :].rearrange("p a b -> p (a b)")[:, 3 * D:4 * D].rearrange("p (k n) -> p k n", k=KD)
        eactT = projT[:, :, :].rearrange("p a b -> p (a b)")[:, 4 * D:4 * D + DEXP].rearrange("p (k n) -> p k n", k=EB)
        eact = wk[:, 0, :]
        esilu = [wk[:, 1, i * 512:(i + 1) * 512] for i in range(2)]
        yg = wk[:, 1, 1024:2048]
        perm = wk[:, 1, 2048:2432].rearrange("p (t n) -> p t n", t=3)
        permw = wk[:, 1, 2432:2816].rearrange("p (t n) -> p t n", t=3)
        backT = wk[:, 1, 2816:2816 + T]
        cT = projT[:, MQ:MQ + 6, :]
        sconv = sb("sconv", P, 6, NS, 7)
        conv_out = sb("conv_out", P, 6, 3 * (NS + 1))
        abT = sb("abT", P, T)
        abw = sb("abw", P, T)
        negA = sb("negA", P, 1)
        gwork = [wk[:, c, :].rearrange("p (s n) -> p s n", s=7) for c in range(2)] + [sb("gwork2", P, 7, 4 * TS)]
        gsc = sb("gsc", P, 3, 32)
        glast = sb("glast", P, 3, 4 * NS)
        nwm = sb("nwm", P, 2, NS * 36)
        pS = sb("pS", P, 2, HD)
        rlog = sb("rlog", P, 3, 4, NEXP)
        toks = sb("toks", P, 3, 16)
        slot_of = sb("slot_of", P, 3, NEXP + EXTRA + 1)
        weight = sb("weight", P, 3, NEXP + EXTRA)
        tally = sb("tally", P, 8, NEXP)
        planf = sb("planf", 1, 8)
        plani = sb("plani", 1, 8, dt=I32)
        PS = ctx.enter_context(nc.psum_tensor("PS", [P, 8, 512], F32))

        S = Signals(nc, ctx, per)
        post, wait = S.post, S.wait
        dma_sems = {n: ctx.enter_context(nc.semaphore(n)) for n in
                    ("const_loaded", "x_loaded", "setup_loaded", "bias_stored", "bias_loaded", "state_loaded",
                     "outputs_stored", "rows_stored", "windows_stored", "pages_loaded")}
        landed = [ctx.enter_context(nc.semaphore(f"slot{i}_landed")) for i in range(SLOTS)]
        pages_landed = [ctx.enter_context(nc.semaphore(f"slot{i}_pages_landed")) for i in range(SLOTS)]
        steps = {e: ctx.enter_context(nc.semaphore(f"{e}_step")) for e in ("dve", "act", "pool")}
        counts = {"stored": 0, "state": 0}

        def cc(name, rows=P, cols=None):
            a, b = cat[name]
            return const[0:rows, a:(b if cols is None else a + cols)]

        ident = cc("ident")
        block = ctx.enter_context(nc.Block())

        def slot_free(eng, n):
            if n >= SLOTS:
                _, l, _, _, name, k = units[n - SLOTS]
                wait(eng, name, k, 0 if name[0] == "f" else l)

        def page_half(eng, n, part):
            kind, l, b, _, _, _ = units[n]
            some = range(part * NPG // 2, (part + 1) * NPG // 2)
            at = [eng.value_load(pages[0:1, b * NPG + pg:b * NPG + pg + 1], min_val=0, max_val=A["n_phys"] - 1)
                  for pg in some]
            slot_free(eng, n)
            for page, pg in zip(at, some):
                eng.dma_start(ring[:, n % SLOTS, pg * 256:(pg + 1) * 256], A[kind][page + l * A["n_phys"], :, :]
                              ).then_inc((pages_landed if part else landed)[n % SLOTS], 16)

        @block.sync
        def _(sp):
            S.layer = 0
            sp.dma_start(pages[:, :], A["pages"]).then_inc(dma_sems["pages_loaded"], 16)
            sp.dma_start(xT[:, :, :], A["x"]).then_inc(dma_sems["x_loaded"], 16)
            sp.dma_start(par[:, :, :], A["par"]).then_inc(dma_sems["x_loaded"], 16)
            sp.dma_start(router[:, :, :], A["router"]).then_inc(dma_sems["x_loaded"], 16)
            sp.dma_start(const[:, :], A["const"]).then_inc(dma_sems["const_loaded"], 16)
            sp.dma_start(setup[:, 0:sn + 330], A["setup"]).then_inc(dma_sems["setup_loaded"], 16)
            sp.wait_ge(dma_sems["pages_loaded"], 16)

            def free(n):
                slot_free(sp, n)

            def cache_unit(n):
                kind, l, b, _, _, _ = units[n]
                s = ring[:, n % SLOTS, :]
                sem = landed[n % SLOTS]
                if kind in PAGED:
                    page_half(sp, n, 0)
                    return
                free(n)
                if kind == "dk1":
                    sp.dma_start(s.rearrange("p (b k) -> p b k", b=4), A["dk1"][l, :, 4 * b:4 * b + 4, :]).then_inc(sem, 16)
                elif kind == "dk2":
                    sp.dma_start(s.rearrange("p (b k) -> p b k", b=8),
                                 A["dk2"][l].rearrange("p b r n -> p b (r n)")[:, :, 0:256]).then_inc(sem, 16)
                elif kind == "d0":
                    sp.dma_start(s[:, 0:1024].rearrange("p (b k) -> p b k", b=8), A["dk0"][l]).then_inc(sem, 16)
                    sp.dma_start(s[:, 1024:2048], A["dv0"][l].rearrange("t b d -> t (b d)")).then_inc(sem, 16)
                elif kind == "dv1":
                    sp.dma_start(s.rearrange("p (k n) -> p k n", k=2),
                                 A["dv1"][l, 256 * b:256 * b + 256].rearrange("(k p) b d -> p k (b d)", p=P)
                                 ).then_inc(sem, 16)
                elif kind == "dv2":
                    rows = A["dv2"][l].rearrange("(n r) b d -> r n (b d)", r=16)
                    for r in range(4):
                        sp.dma_start(s[64 * (r % 2):64 * (r % 2) + 64, 1024 * (r // 2):1024 * (r // 2) + 1024],
                                     rows[r]).then_inc(sem, 16)

            def weight_unit(n):
                kind, l, i, _, _, _ = units[n]
                free(n)
                width = 1792 if kind == "br" else SLOT
                src = A[kind][i] if kind in ("fgu", "fdn") else A[kind][l, i]
                sp.dma_start(ring[:, n % SLOTS, 0:width], src).then_inc(landed[n % SLOTS], 16)

            for n in range(moe_base):
                (cache_unit if units[n][0] in PAGED + ("dk1", "dk2", "d0", "dv1", "dv2")
                 else weight_unit)(n)

            def expert_units(q, e):
                for i in range(EU):
                    n = moe_base + i
                    sp.wait_ge(S.sem("moe_unit"), q * EU + (i + 1))
                    sp.dma_start(ring[:, n % SLOTS, :], A["moe"][e * EU + i, :, :]).then_inc(landed[n % SLOTS], 16)

            for j in range(SLOTS):
                free(moe_base + j)
            with sp.Fori(0, NEXP) as e:
                expert_units(e, e)
            sp.wait_ge(S.sem("plan_made"), 1)
            extra = sp.value_load(plani[0:1, EXTRA:EXTRA + 1], min_val=0, max_val=EXTRA)
            with sp.Fori(0, EXTRA) as x:
                with sp.If(x < extra):
                    expert = sp.value_load(plani[0:1, bass.ds(x, 1)], min_val=0, max_val=NEXP - 1)
                    expert_units(x + NEXP, expert)

        @block.tensor
        def _(pe):
            S.layer = 0
            at = [0]

            def take(kind, extra=0, slot_turns=0):
                n = at[0]
                at[0] += 1
                assert units[n][0] == kind, (units[n], kind)
                pe.wait_ge(landed[n % SLOTS], landing[n][0] + slot_turns)
                if kind in PAGED:
                    pe.wait_ge(pages_landed[n % SLOTS], landing[n][1])
                return ring[:, n % SLOTS, :]

            def mm(out, lhsT, rhs, first, last):
                return pe.matmul(out, lhsT, rhs, start=first, stop=last)

            def squared_before(tag):
                return KD * (2 * S.layer + NORM[tag] - 1)

            def pe_unit(ins):
                post(ins, "moe_unit")

            def norm_sum(tag):
                for k in range(KD):
                    pe.wait_ge(S.sem("norm_squares"), squared_before(tag) + k + 1)
                    ins = mm(PS[:, 7, 0:T], cc("ones"), hT[:, k, :], k == 0, k == KD - 1)
                    if tag == "ffn" and S.layer == L - 1 and k < SLOTS:
                        pe_unit(ins)
                post(ins, "norm_sum")

            def bias_tables():
                pe.wait_ge(dma_sems["setup_loaded"], 16)
                def t(name, a=0, b=None):
                    return setup[:, sat[name][0] + a:sat[name][1] if b is None else sat[name][0] + b]
                for i, (a, b) in enumerate(((0, 512), (512, 1024), (1024, SW))):
                    mm(PS[:, 2 + i, 0:b - a], rel_mo, t("mo_hot", a, b), True, True)
                for g in range(3):
                    for a, n in ((DCOL[g], (128, 512, 256)[g]), (DNEW + g * TS, TS)):
                        ins = mm(PS[0:64, 5 + a // 512, a % 512:a % 512 + n], rel_di[:, g * 64:g * 64 + 64],
                                 t("di_hot", a, a + n), True, True)
                post(ins, "tables_mm")
                for h in range(10):
                    if h == 2:
                        wait(pe, "norm_mean", 1)
                    if h >= 3:
                        wait(pe, "table_sum", h - 2)
                    ins = mm(PS[:, (0, 1, 7)[h % 3], :], rel[:, h:h + 1].to_broadcast([BUCKETS, P]),
                             setup[0:BUCKETS, sat["pr_hot"][0]:sat["pr_hot"][1]], True, True)
                    post(ins, "table_mm")

            def in_unit():
                return take("in").rearrange("p (h k c) -> p h k c", h=2, k=KD)

            def in_block(n, bank, w):
                for k in range(KD):
                    if n == 0:
                        wait(pe, "norm_h", (NORM["mix"] - 1) * KD + k + 1)
                    ins = mm(PS[:, bank, 0:T], w[:, n % 2, k, :], hT[:, k, :], k == 0, k == KD - 1)
                post(ins, "in_mm")

            def in_projection(l):
                if l == 0:
                    wait(pe, "table_sum", 10)
                for n in range(IN_FIRST):
                    if n % 2 == 0:
                        w = in_unit()
                    if n >= 2:
                        wait(pe, "in_evac", n - 1)
                    in_block(n, n % 2, w)

            def value_transposes(l):
                if l == 0:
                    pe.wait_ge(S.sem("tables_read"), 1)
                wait(pe, "in_evac", IN_FIRST)
                for i, (t, a, b) in enumerate(VGROUPS):
                    if i >= 2:
                        wait(pe, "vtok_copied", i - 1)
                    cols = (P, P, TS)[t]
                    for v in range(a, b):
                        ins = pe.transpose(PS[0:cols, 5 + i % 2, (v - a) * P:(v - a) * P + P],
                                           projT[:, VB[v], t * P:t * P + cols], ident)
                    post(ins, "vtok_mm")

            AUNITS = attention_units()

            def scores(u):
                kind, h, subs, _ = AUNITS[u]
                banks = score_banks(u)
                if u >= 1:
                    wait(pe, "at_s", u)
                for (qb, kb, hf, _, _), bank in zip(subs, banks):
                    for t in range(2):
                        ins = mm(PS[:, bank, t * TP:(t + 1) * TP], projT[half(hf), qb, t * P:(t + 1) * P],
                                 projT[half(hf), kb, 0:TP], True, True)
                post(ins, "at_qk")

            def prompt_attention(l):
                wait(pe, "vtok_copied", len(VGROUPS))
                scores(0)
                s = 0
                for u, (kind, h, subs, _) in enumerate(AUNITS):
                    if u + 1 < len(AUNITS):
                        scores(u + 1)
                    for n in late_blocks(u):
                        if n % 2 == 0:
                            w = in_unit()
                        if n != IN_FIRST + 1:
                            wait(pe, "in_evac", n)
                        in_block(n, late_bank(n), w)
                    wait(pe, "sb_p", u + 1) if kind == "sb" else wait(pe, "md_p", u - 3)
                    if u >= 2:
                        wait(pe, "at_o", u - 1)
                    for g, (_, _, hf, vb, _) in enumerate(subs):
                        if s >= 2:
                            wait(pe, "pt_copied", s - 1)
                        p = wkA[u % 2].rearrange("p (g n) -> p g n", g=3)[:, g, :]
                        for i, a in enumerate((0, TP, TP + P)):
                            ins = pe.transpose(PS[:, 5 + s % 2, i * P:i * P + P], p[:, a:a + P], ident)
                        post(ins, "pt_mm")
                        wait(pe, "pt_copied", s + 1)
                        mm(PS[half(hf), u % 2, 0:TP], vtok[:, 0, vb, half(hf)], pt[s % 2][:, 0:TP], g == 0, False)
                        ins = mm(PS[half(hf), u % 2, P:TP], vtok[:, 1, vb, half(hf)], pt[s % 2][:, TP:TP + P],
                                 False, g == len(subs) - 1)
                        post(ins, "at_pv_sub")
                        s += 1

            def gate_block(g, bank, w):
                for k in range(KD):
                    ins = mm(PS[:, bank, 0:T], w[:, g % 2, k, :], hT[:, k, :], k == 0, k == KD - 1)
                post(ins, "gate_mm")

            def gate_unit():
                return take("gate").rearrange("p (h k c) -> p h k c", h=2, k=KD)

            def sample_attention(l, kind):
                kb, ob = {"sb": (SBK, 0), "mo": (MK, 2)}[kind]
                wait(pe, "in_evac", NBLK)
                wait(pe, f"s{kind}_q", 1)
                for b in range(NS):
                    w = take(kind + "k").rearrange("p (g h t) -> p g h t", g=NPG, h=2)
                    for hp in range(2):
                        q = qbd[:, b * 256 + hp * P:b * 256 + hp * P + P]
                        for c in range(2):
                            ins = mm(PS[:, 2 + c, :], q, w[:, 4 * c:4 * c + 4, hp, :], b == 0 and hp == 0,
                                     b == NS - 1 and hp == 1)
                    post(ins, f"s{kind}_k")
                for hp in range(2):
                    ins = mm(PS[:, 4, 0:TS], qall[:, hp, :], projT[:, kb + hp, TP:T], hp == 0, hp == 1)
                post(ins, f"s{kind}_qk")
                for g in range(*((0, 2) if kind == "sb" else (2, 6))):
                    if g % 2 == 0:
                        gw = gate_unit()
                    if g >= 2:
                        wait(pe, "gate_evac", g - 1)
                    gate_block(g, (0, 7)[g % 2], gw)
                wait(pe, f"s{kind}_p", 1)
                for g in range(NPG):
                    ins = pe.transpose(PS[:, 5 + g // 4, (g % 4) * P:(g % 4) * P + P], sA[:, g * P:g * P + P], ident)
                    if g == 3:
                        post(ins, f"s{kind}_pt")
                post(ins, f"s{kind}_pt")
                wait(pe, "gate_evac", 2 if kind == "sb" else 6)
                post(pe.transpose(PS[0:TS, 7, 0:P], sA[:, PAST:SW], ident), f"s{kind}_pt")
                wait(pe, f"s{kind}_ptcopied", 3)
                for b in range(NS):
                    w = take(kind + "v").rearrange("p (g n) -> p g n", g=NPG)
                    out, rows = PS[0:16, 1 + b // 2, (b % 2) * 256:(b % 2) * 256 + 256], slice(b * 16, b * 16 + 16)
                    mm(out, spt[0:TS, NPG, rows], vtok[0:TS, 2, ob:ob + 2, :], True, False)
                    for g in range(NPG):
                        ins = mm(out, spt[:, g, rows], w[:, g, :], False, g == NPG - 1)
                    post(ins, f"s{kind}_v")
                for b in range(NS):
                    if b % 2 == 0:
                        wait(pe, f"s{kind}_out", b // 2 + 1)
                    for hp in range(2):
                        n = 2 * b + hp
                        ins = pe.transpose(PS[:, 1, n * 16:n * 16 + 16], so[:, n * P:n * P + P], ident[0:16, 0:16])
                post(ins, f"s{kind}_outT")

            def dilated_sample(l):
                wait(pe, "conv_sq", 1)
                for i in range(4):
                    ins = mm(PS[:, 4 + i, 0:T], cc("head_ones"), wk[:, 0, i * T:(i + 1) * T], True, True)
                post(ins, "conv_sum")
                wait(pe, "sdi_q", 1)

                def q(b, g):
                    return dqbd[:, b * 192 + g * 64:b * 192 + g * 64 + 64]
                for a in range(2):
                    w = take("dk1").rearrange("p (b k) -> p b k", b=4)
                    for b in range(4):
                        ins = mm(PS[0:64, 2, :], q(4 * a + b, 1), w[:, b, :], a == 0 and b == 0, a == 1 and b == 3)
                    post(ins, "sdi_k")
                w = take("dk2").rearrange("p (b k) -> p b k", b=8)
                for b in range(NS):
                    ins = mm(PS[0:64, 3, 128:384], q(b, 2), w[:, b, :], b == 0, b == NS - 1)
                post(ins, "sdi_k")
                d0 = take("d0")
                w = d0[:, 0:1024].rearrange("p (b k) -> p b k", b=8)
                for b in range(NS):
                    mm(PS[0:64, 3, 0:128], q(b, 0), w[:, b, :], b == 0, b == NS - 1)
                for g in range(3):
                    ins = mm(PS[0:64, 3, 384 + g * TS:384 + (g + 1) * TS], dqall[:, g, :], projT[:, DK + g, TP:T],
                             True, True)
                post(ins, "sdi_qk")
                gw = gate_unit()
                wait(pe, "conv_ms", 1)
                gate_block(6, 0, gw)
                gate_block(7, 7, gw)
                wait(pe, "sdi_p", 1)
                for k in range(7):
                    pe.transpose(PS[:, 5, k * 64:k * 64 + 64], sA[0:64, k * P:k * P + P], ident[0:64, 0:64])
                for g in range(3):
                    ins = pe.transpose(PS[0:TS, 6, g * 64:g * 64 + 64], sA[0:64, DNEW + g * TS:DNEW + (g + 1) * TS],
                                       ident[0:64, 0:64])
                post(ins, "sdi_pt")
                v0 = d0[:, 1024:2048].rearrange("p (b n) -> p b n", b=8)
                v1 = [take("dv1").rearrange("p (k b n) -> p k b n", k=2, b=8) for _ in range(2)]
                v2 = take("dv2").rearrange("p (k b n) -> p k b n", k=2, b=8)
                wait(pe, "sdi_ptcopied", 2)
                flat = spt.rearrange("p g n -> p (g n)")
                for b in range(NS):
                    out = PS[0:8, 1 + b // 4, (b % 4) * P:(b % 4) * P + P]
                    vs = [v1[0][:, 0, b], v1[0][:, 1, b], v1[1][:, 0, b], v1[1][:, 1, b], v0[:, b], v2[:, 0, b],
                          v2[:, 1, b]]
                    for k, v in enumerate(vs):
                        mm(out, flat[:, k * 64 + b * 8:k * 64 + b * 8 + 8], v, k == 0, False)
                    for g in range(3):
                        ins = mm(out, flat[0:TS, 7 * P + g * 64 + b * 8:7 * P + g * 64 + b * 8 + 8],
                                 vtok[0:TS, 2, 4 + g, :], False, g == 2)
                post(ins, "sdi_v")
                wait(pe, "sdi_out", 1)
                for b in range(NS):
                    ins = pe.transpose(PS[:, 1, b * 8:b * 8 + 8], so[0:8, b * P:b * P + P], ident[0:8, 0:8])
                post(ins, "sdi_outT")

            def heads_view(ap, n):
                return ap[:, 0:4 * n].rearrange("p (h n) -> p h n", h=4)

            def delta(l):
                wait(pe, "conv_done", 1)
                wait(pe, "sdi_read", 2)
                for c in range(3):
                    n = gdn_rows(c)
                    for i in range(2):
                        pe.transpose(PS[0:n, 2 * c, i * P:i * P + P], cT[:, 2 + i, c * P:c * P + n], ident)
                        pe.transpose(PS[0:n, 2 * c, TP + i * P:TP + i * P + P], cT[:, 4 + i, c * P:c * P + n], ident)
                    post(pe.transpose(PS[0:n, 2 * c + 1, 0:P], abT[:, c * P:c * P + n], ident), "gtok_mm")
                for c in range(3):
                    n = gdn_rows(c)
                    wait(pe, "gsc_g", c + 1)
                    g = gsc[0:n, c, 0:4]
                    mm(PS[0:n, 6, c * 32:c * 32 + 4], cc("seq_upto" if c == 2 else "upto", n, n), g, True, True)
                    ins = mm(PS[0:n, 6, c * 32 + 8:c * 32 + 12], cc("seq_ones" if c == 2 else "ones", n, n), g, True, True)
                    post(ins, "gcum_mm")
                for c in range(3):
                    n = gdn_rows(c)
                    wait(pe, "gtok_copied", c + 1)
                    wait(pe, "gbc_rhs", c + 1)
                    mm(PS[:, 2 * c, 0:4 * n], cc("ones", n), gwork[c][0:n, 0, 0:4 * n], True, True)
                    ins = mm(PS[:, 2 * c + 1, 0:4 * n], cc("ones", n), gwork[c][0:n, 1, 0:4 * n], True, True)
                    post(ins, "gbc_mm")
                for c in range(3):
                    n = gdn_rows(c)
                    wait(pe, "gkq", c + 1)
                    kb = gwork[c][:, 6, 0:2 * n].rearrange("p (a n) -> p a n", a=2)
                    for h in range(4):
                        k = cT[half(h % 2), 2 + h // 2, c * P:c * P + n]
                        bank, a = 2 * c + h % 2, h // 2
                        mm(PS[0:n, bank, a * n:(a + 1) * n], k, kb[half(h % 2), a, :], True, True)
                        ins = mm(PS[0:n, bank, (2 + a) * n:(3 + a) * n], k, cT[half(h % 2), a, c * P:c * P + n],
                                 True, True)
                    post(ins, "gm_mm")
                for s in range(7):
                    if s < 6:
                        g = 8 + s
                        if g % 2 == 0:
                            gw = gate_unit()
                        wait(pe, "gate_evac", g if s == 0 else g - 1)
                        gate_block(g, 7 - g % 2, gw)
                    for c in range(3):
                        n = gdn_rows(c)
                        if s >= gdn_levels(c):
                            continue
                        wait(pe, f"g{c}_bt", s + 1)
                        B, Tm = heads_view(gwork[c][:, 0, :], n), heads_view(gwork[c][:, 3, :], n)
                        for h in range(4):
                            ins = mm(PS[0:n, 2 * c, h * n:(h + 1) * n], B[0:n, h], Tm[0:n, h], True, True)
                        post(ins, f"g{c}_x")
                    for c in range(3):
                        n = gdn_rows(c)
                        if s >= gdn_levels(c):
                            continue
                        wait(pe, f"g{c}_xcopied", s + 1)
                        X, Tm, TT = (heads_view(gwork[c][:, i, :], n) for i in (5, 3, 4))
                        for h in range(4):
                            mm(PS[0:n, 2 * c, h * n:(h + 1) * n], TT[0:n, h], X[0:n, h], True, True)
                            ins = mm(PS[0:n, 2 * c + 1, h * n:(h + 1) * n], X[0:n, h], TT[0:n, h], True, True)
                        post(ins, f"g{c}_y")
                wait(pe, "gate_evac", 14)
                for c in range(3):
                    n = gdn_rows(c)
                    wait(pe, f"g{c}_t", gdn_levels(c))
                    wait(pe, "gscaled", c + 1)
                    TT = heads_view(gwork[c][:, 4, :], n)
                    for h in range(4):
                        ins = mm(PS[half(h % 2), 2 * c, (h // 2) * n:(h // 2 + 1) * n], gtok[0:n, c, 2, h * HD:(h + 1) * HD],
                                 TT[0:n, h], True, True)
                    post(ins, "gw_mm")
                for c in range(3):
                    n = gdn_rows(c)
                    TT = heads_view(gwork[c][:, 4, :], n)
                    QK = heads_view(gwork[c][:, 2, :], n)
                    qg = gwork[c][:, 6, 2 * n:4 * n].rearrange("p (a n) -> p a n", a=2)
                    wait(pe, "gnw", c + 1)
                    if c == 1:
                        wait(pe, "pstate", 1)
                    for h in range(4):
                        hf, hp = half(h % 2), h // 2
                        out = PS[0:n, 2 * c + h % 2, hp * HD:(hp + 1) * HD]
                        ins = mm(out, TT[0:n, h], gtok[0:n, c, 1, h * HD:(h + 1) * HD], True, c == 0)
                        if c == 1:
                            ins = mm(out, gtok[hf, c, 4, hp * P:hp * P + P], pS[hf, hp, :], False, True)
                        if c == 2:
                            for b in range(NS):
                                ins = mm(out, nwm[hf, hp, b * TS:(b + 1) * TS], sS[hf, hp, b, :], False, b == NS - 1)
                    post(ins, "gu_mm")
                    wait(pe, "gvnew", c + 1)
                    for h in range(4):
                        hf, hp = half(h % 2), h // 2
                        out = PS[hf, 2 * c, hp * n:(hp + 1) * n]
                        ins = mm(out, gtok[0:n, c, 3, h * HD:(h + 1) * HD], QK[0:n, h], True, c == 0)
                        if c == 1:
                            ins = mm(out, pS[hf, hp, :], qg[hf, hp, :], False, True)
                        if c == 2:
                            for b in range(NS):
                                ins = mm(PS[hf, 2 * c, hp * n + b * TQ:hp * n + (b + 1) * TQ], sS[hf, hp, b, :],
                                         qg[hf, hp, b * TQ:(b + 1) * TQ], False, b == NS - 1)
                    post(ins, "go_mm")
                    if c < 2:
                        for h in range(4):
                            ins = mm(PS[half(h % 2), 6 + c, (h // 2) * HD:(h // 2 + 1) * HD],
                                     gtok[0:n, c, 0, h * HD:(h + 1) * HD], gtok[0:n, c, 3, h * HD:(h + 1) * HD], True, True)
                        post(ins, "gs_mm")
                wait(pe, "gvm", 1)
                wait(pe, "pstate", 2)
                for h in range(4):
                    ins = mm(PS[half(h % 2), 6 + h // 2, :], gtok[0:TS, 2, 0, h * HD:(h + 1) * HD],
                             mergedT.rearrange("p a b -> p (a b)")[0:TS, h * 512:(h + 1) * 512], True, True)
                post(ins, "gss_mm")
                wait(pe, "go_sq", 1)
                for i in range(2):
                    ins = mm(PS[:, i, 0:T], cc("head_ones"), gosq[:, i, :], True, True)
                post(ins, "go_sum")
                gw = gate_unit()
                for g in (14, 15):
                    gate_block(g, 4 + g % 2, gw)

            def merge(l):
                wait(pe, "gate_evac", EARLY)
                wait(pe, "o_done", 1)
                for m2 in range(KD // 2):
                    w = take("br")[:, 0:1792].rearrange("p (m k c) -> p m k c", m=2, k=7)
                    for m in range(2):
                        for br, (k0, k1) in enumerate(((OSB, 2), (OGD, 4), (OMO, 6), (ODI, 7))):
                            n = (2 * m2 + m) * 4 + br
                            if n >= 4:
                                wait(pe, "br_evac", n - 3)
                            for k in range(k0, k1):
                                ins = mm(PS[:, 2 + n % 4, 0:T], w[:, m, k, :], oT[:, k, :], k == k0, k == k1 - 1)
                            post(ins, "br_mm")
                    for g in range(EARLY + 8 * m2, min(EARLY + 8 * m2 + 8, 4 * KD)):
                        if g % 2 == 0:
                            gw = gate_unit()
                        wait(pe, "gate_evac", g - 1)
                        gate_block(g, g % 2, gw)
                wait(pe, "merged", KD)
                for i in range(KD // 2):
                    w = take("out").rearrange("p (h k c) -> p h k c", h=2, k=KD)
                    for h in range(2):
                        n = 2 * i + h
                        if n >= 2:
                            wait(pe, "out_evac", n - 1)
                        for k in range(KD):
                            ins = mm(PS[:, n % 2, 0:T], w[:, h, k, :], mergedT[:, k, :], k == 0, k == KD - 1)
                        post(ins, "out_mm")

            def feed_forward(t, nblk):
                for i in range(nblk):
                    w = take(t + "gu").rearrange("p (h k c) -> p h k c", h=2, k=KD)
                    for h in range(2):
                        n = 2 * i + h
                        if n >= 4:
                            pe.wait_ge(S.sem(t + "act"), i - 1)
                        for k in range(KD):
                            ins = mm(PS[:, n % 4, 0:T], w[:, h, k, :], hT[:, k, :], k == 0, k == KD - 1)
                        post(ins, t + "gu_mm")
                pe.wait_ge(S.sem(t + "act"), nblk)
                w = None
                for m in range(KD):
                    if m >= 2:
                        pe.wait_ge(S.sem(t + "dn_evac"), m - 1)
                    for k in range(nblk):
                        b = m * nblk + k
                        if b % 16 == 0:
                            w = take(t + "dn").rearrange("p (k c) -> p k c", k=16)
                        ins = mm(PS[:, 4 + m % 2, 0:T], w[:, b % 16, :], actT[:, k, :], k == 0, k == nblk - 1)
                    post(ins, t + "dn_mm")

            def gather(q):
                pe.wait_ge(S.sem("perm_made"), q + 1)
                for half_k in range(2):
                    for k in range(4):
                        for t in range(3):
                            n = gdn_rows(t)
                            f = (4 * half_k + k) * P
                            ins = mm(PS[:, 2 + half_k, k * P:(k + 1) * P], htok[0:n, t, f:f + P], perm[0:n, t, :],
                                     t == 0, t == 2)
                    post(ins, "gather_mm")

            def act_transposes(q, c):
                pe.wait_ge(S.sem("eact"), q * EC + (c + 1))
                if c == 0:
                    pe.wait_ge(S.sem("moe_added"), q * KD)
                else:
                    pe.wait_ge(S.sem("eactT_copied"), q * EC + c)
                for j in range(4):
                    ins = pe.transpose(PS[:, 6, j * P:(j + 1) * P], eact[:, (4 * c + j) * P:(4 * c + j + 1) * P], ident)
                post(ins, "eactT_mm")

            def expert_pass(q):
                at[0] = moe_base
                turns = q * (16 * EU // SLOTS)
                pe.wait_ge(S.sem("gathered"), q * 2 + 2)
                for c in range(EC):
                    if c >= 2:
                        pe.wait_ge(S.sem("eact"), q * EC + (c - 1))
                    for b in range(2):
                        for u in range(2):
                            w = take("moe", slot_turns=turns).rearrange("p (k n) -> p k n", k=4)
                            for k in range(4):
                                ins = mm(PS[:, 2 * (c % 2) + b, :], hgT[:, 4 * u + k, :], w[:, k, :],
                                         u + k == 0, u + k == 4)
                            pe_unit(ins)
                    if c:
                        act_transposes(q, c - 1)
                gather(q + 1)
                act_transposes(q, EC - 1)
                for u in range(EB // 2):
                    w = take("moe", slot_turns=turns).rearrange("p (k n) -> p k n", k=2)
                    if u % 2 == 0:
                        pe.wait_ge(S.sem("eactT_copied"), q * EC + (u // 2 + 1))
                    for j in range(2):
                        k = 2 * u + j
                        for b in range(2):
                            ins = mm(PS[:, 4 + b, :], eactT[:, k, :], w[:, j, b * 512:(b + 1) * 512], k == 0, k == EB - 1)
                    pe_unit(ins)
                    if u == 4:
                        pe.wait_ge(S.sem("permw_made"), q + 1)
                        for t in range(3):
                            n = gdn_rows(t)
                            ins = pe.transpose(PS[:, 7, t * P:t * P + n], permw[0:n, t, :], ident[0:n, 0:n])
                        post(ins, "back_mm")
                pe.wait_ge(S.sem("back_copied"), q + 1)
                pe.wait_ge(S.sem("yg_high"), q + 1)
                pe.wait_ge(S.sem("yg_low"), q + 1)
                for m in range(KD):
                    if m >= 2:
                        pe.wait_ge(S.sem("moe_added"), q * KD + (m - 1))
                    ins = mm(PS[:, 6 + m % 2, 0:T], yg[:, m * P:(m + 1) * P], backT, True, True)
                    post(ins, "back_sum")

            def routing():
                wait(pe, "norm_h", KD * NORM["ffn"])
                for t in range(3):
                    n = gdn_rows(t)
                    for k in range(KD):
                        ins = mm(PS[0:n, 6, t * 8:t * 8 + 8], hT[:, k, t * P:t * P + n], router[:, k, :], k == 0, k == KD - 1)
                post(ins, "router_mm")
                for i in range(6):
                    t, a = i // 2, i % 2
                    n = gdn_rows(t)
                    for k in range(4):
                        ins = pe.transpose(PS[0:n, i, k * P:(k + 1) * P], hT[:, 4 * a + k, t * P:t * P + n], ident)
                    post(ins, "htok_mm")
                pe.wait_ge(S.sem("chosen"), 3)
                for t in range(3):
                    n = gdn_rows(t)
                    for s in range(t + 1):
                        r = gdn_rows(s)
                        ins = mm(PS[0:n, 6, 32 + t * 8:40 + t * 8], cc("upto" if s == t else "ones", r, n),
                                 rlog[0:r, s, 0, :], s == 0, s == t)
                for s in range(3):
                    r = gdn_rows(s)
                    ins = mm(PS[:, 6, 56:64], cc("ones", r), rlog[0:r, s, 0, :], s == 0, s == 2)
                post(ins, "counted")
                pe.wait_ge(S.sem("htok_copied"), 6)
                gather(0)

            pe.wait_ge(dma_sems["const_loaded"], 16)
            for l in range(L):
                S.layer = l
                norm_sum("mix")
                if l == 0:
                    bias_tables()
                in_projection(l)
                value_transposes(l)
                prompt_attention(l)
                sample_attention(l, "sb")
                sample_attention(l, "mo")
                dilated_sample(l)
                delta(l)
                merge(l)
                norm_sum("ffn")
                if l == 0:
                    wait(pe, "norm_h", KD * NORM["ffn"])
                    feed_forward("f", FB)
            routing()
            with pe.Fori(0, NEXP) as e:
                expert_pass(e)
            pe.wait_ge(S.sem("plan_made"), 1)
            extra = pe.value_load(plani[0:1, EXTRA:EXTRA + 1], min_val=0, max_val=EXTRA)
            with pe.Fori(0, EXTRA) as x:
                with pe.If(x < extra):
                    expert_pass(x + NEXP)
            norm_sum("fin")

        @block.scalar
        def _(act):
            chain = Chain(act, steps["act"])
            step = chain.step
            AUNITS = attention_units()

            def copy(out, in_, scale=1.0):
                return act.activation(out, in_, ACT.Copy, scale=scale)

            def softplus_rest(A, B):
                step(act.activation(B, A, ACT.Abs))
                step(act.activation(B, B, ACT.Exp, scale=-1.0))
                return act.activation(B, B, ACT.Ln, bias=1.0)

            def norm_root(tag):
                wait(act, "norm_mean", NORM[tag])
                post(act.activation(rstd[:, :], rstd[:, :], ACT.Sqrt), "norm_root")

            def in_evac(n, bank):
                wait(act, "in_mm", n + 1)
                post(copy(projT[:, IN_BLOCKS[n], :], PS[:, bank, 0:T]), "in_evac")

            def in_evacuation(l):
                if l:
                    wait(act, "fdn_evac", KD, 0)
                for n in range(IN_FIRST):
                    in_evac(n, n % 2)

            def value_copies(l):
                for i, (t, a, b) in enumerate(VGROUPS):
                    n = (P, P, TS)[t]
                    wait(act, "vtok_mm", i + 1)
                    post(copy(vtok[0:n, t, a:b, :], PS[0:n, 5 + i % 2, 0:(b - a) * P].rearrange("p (v d) -> p v d", d=P)),
                         "vtok_copied")

            def prompt_attention(l):
                s = 0
                for v in range(len(AUNITS) + 1):
                    if v < len(AUNITS):
                        A, B = wkA[v % 2], wkB[v % 2]
                        if AUNITS[v][0] == "sb":
                            wait(act, "at_s", v + 1)
                            post(softplus_rest(A[:, 0:512], B[:, 0:512]), "sb_soft")
                        else:
                            wait(act, "at_nm", v - 3)
                            w = A.rearrange("p (g t k) -> p t g k", g=3, t=2)[:, :, 0:len(AUNITS[v][2]), :]
                            for t in range(2):
                                ins = act.activation(w[:, t], w[:, t], ACT.Exp, bias=small[:, 6 * v + t:6 * v + t + 1],
                                                     accum_out=small[:, 6 * v + 2 + t:6 * v + 3 + t])
                            post(ins, "at_e")
                    if v >= 1:
                        u = v - 1
                        if AUNITS[u][0] == "sb":
                            wait(act, "sb_r", u + 1)
                            A = wkA[u % 2][:, 0:512]
                            post(act.activation(A, A, ACT.Exp), "sb_p")
                        for n in late_blocks(u):
                            in_evac(n, late_bank(n))
                        for _ in AUNITS[u][2]:
                            wait(act, "pt_mm", s + 1)
                            if s >= 2:
                                wait(act, "at_pv_sub", s - 1)
                            post(copy(pt[s % 2], PS[:, 5 + s % 2, 0:384]), "pt_copied")
                            s += 1

            def gate_evac(g, bank):
                wait(act, "gate_mm", g + 1)
                post(act.activation(gate(g), PS[:, bank, 0:T], ACT.Sigmoid), "gate_evac")

            def sample_attention(l, kind):
                A, B = sA, sB
                if kind == "sb":
                    wait(act, "ssb_s", 1)
                    post(softplus_rest(A, B), "ssb_soft")
                    wait(act, "ssb_r", 1)
                    post(act.activation(A, A, ACT.Exp), "ssb_p")
                    act.wait_ge(dma_sems["rows_stored"], 16 * 3 * (l + 1))
                    gate_evac(0, 0)
                    gate_evac(1, 7)
                else:
                    gate_evac(2, 0)
                    gate_evac(3, 7)
                    wait(act, "smo_nm", 1)
                    post(act.activation(A, A, ACT.Exp, bias=small[:, 60:61], accum_out=small[:, 61:62]), "smo_e")
                    gate_evac(4, 0)
                    gate_evac(5, 7)
                for i in range(2):
                    wait(act, f"s{kind}_pt", i + 1)
                    post(copy(spt[:, 4 * i:4 * i + 4, :], PS[:, 5 + i, :].rearrange("p (g n) -> p g n", g=4)),
                         f"s{kind}_ptcopied")
                wait(act, f"s{kind}_pt", 3)
                post(copy(spt[0:TS, NPG, :], PS[0:TS, 7, 0:P]), f"s{kind}_ptcopied")

            def convolution(l):
                wait(act, "conv_y", 1)
                post(act.activation(cT[:, :, :], cT[:, :, :], ACT.Silu), "conv_silu")
                wait(act, "ab_in", 1)
                post(act.activation(abT[32:36, :], projT[32:36, AB, :], ACT.Sigmoid), "beta_done")
                step(act.activation(negA[0:4, :], par[0:4, l, PALOG:PALOG + 1], ACT.Exp))
                post(softplus_rest(abw[0:4, :], abT[0:4, :]), "ab_soft")
                wait(act, "conv_ms", 1)
                rs = wk[:, 0, 4 * T:8 * T]
                post(act.activation(rs, rs, ACT.Sqrt), "conv_root")

            def dilated_sample(l):
                A = sA[0:64, 0:DW]
                wait(act, "sdi_nm", 1)
                post(act.activation(A, A, ACT.Exp, bias=small[0:64, 60:61], accum_out=small[0:64, 61:62]), "sdi_e")
                gate_evac(6, 0)
                gate_evac(7, 7)
                flat = spt.rearrange("p g n -> p (g n)")
                wait(act, "sdi_pt", 1)
                post(copy(flat[:, 0:448], PS[:, 5, 0:448]), "sdi_ptcopied")
                post(copy(flat[0:TS, 7 * P:7 * P + 192], PS[0:TS, 6, 0:192]), "sdi_ptcopied")

            def delta(l):
                for c in range(3):
                    n = gdn_rows(c)
                    wait(act, "gtok_mm", c + 1)
                    post(copy(gtok[0:n, c, 0:2, :], PS[0:n, 2 * c, :].rearrange("p (a n) -> p a n", a=2)), "gtok_copied")
                for c in range(3):
                    n = gdn_rows(c)
                    wait(act, "gbc_mm", c + 1)
                    G = PS[:, 2 * c, 0:4 * n]
                    post(act.activation(gwork[c][:, 5, 0:4 * n], G, ACT.Exp), "g_eg")
                    gv = G.rearrange("p (h n) -> p h n", h=4)
                    if c < 2:
                        ins = act.activation(glast[:, c, 0:4], gv[:, :, n - 1], ACT.Exp)
                    else:
                        ins = act.activation(glast[:, c, :].rearrange("p (h b) -> p h b", h=4), gv[:, :, TQ - 1::TQ], ACT.Exp)
                    post(ins, "g_last")
                    wait(act, "gsc_in", c + 1)
                    act.activation(gsc[0:n, c, 16:20], gsc[0:n, c, 8:12], ACT.Exp)
                    post(act.activation(gsc[0:n, c, 28:32], gsc[0:n, c, 24:28], ACT.Exp), "gsc_exp")
                    wait(act, "gam_in", c + 1)
                    post(act.activation(gwork[c][0:n, 0, 0:4 * n], gwork[c][0:n, 0, 0:4 * n], ACT.Exp), "gam")
                wait(act, "gtok_mm", 3)
                post(act.activation(cT[:, 4:6, :], projT[:, GZ:GZ + 2, :], ACT.Silu), "z_silu")
                for s in range(7):
                    if s < 6:
                        gate_evac(8 + s, 7 - s % 2)
                    for c in range(3):
                        n = gdn_rows(c)
                        if s < gdn_levels(c):
                            wait(act, f"g{c}_x", s + 1)
                            post(copy(gwork[c][0:n, 5, 0:4 * n], PS[0:n, 2 * c, 0:4 * n]), f"g{c}_xcopied")
                for c in range(3):
                    n = gdn_rows(c)
                    wait(act, "gw_mm", c + 1)
                    if c < 2:
                        post(copy(gtok[:, c, 4, :], PS[:, 2 * c, 0:2 * n], -1.0), "gnw")
                    else:
                        for a in range(2):
                            ins = copy(nwm[:, a, :].rearrange("p (b x) -> p b x", x=36)[:, :, 0:TQ],
                                       PS[:, 4, a * TS:(a + 1) * TS].rearrange("p (b q) -> p b q", q=TQ), -1.0)
                        post(ins, "gnw")
                for c in range(3):
                    n = gdn_rows(c)
                    wait(act, "gu_mm", c + 1)
                    new = gtok[0:n, c, 3, :].rearrange("p (a t d) -> p a t d", a=2, t=2)
                    for hf in range(2):
                        ins = copy(new[:, :, hf, :], PS[0:n, 2 * c + hf, 0:P].rearrange("p (a d) -> p a d", a=2))
                    post(ins, "gvnew")

            def gates(l):
                wait(act, "go_rs", 1)
                post(act.activation(gosq[:, 2:4, :], gosq[:, 2:4, :], ACT.Sqrt), "go_root")
                for g in range(14, EARLY):
                    gate_evac(g, 4 + g % 2)
                for g in range(EARLY, 4 * KD):
                    if (g - EARLY) % 4 == 0:
                        wait(act, "merged", (g - EARLY) // 4 + 1)
                    gate_evac(g, g % 2)

            def feed_forward(t, nblk):
                for i in range(nblk):
                    act.wait_ge(S.sem(t + "gu_mm"), 2 * i + 1)
                    if i >= 2:
                        act.wait_ge(S.sem(t + "act"), i - 1)
                    post(act.activation(wk[:, 1, (i % 2) * T:(i % 2 + 1) * T], PS[:, (2 * i) % 4, 0:T], ACT.Silu),
                         t + "silu")

            def gathered(q):
                for a in range(2):
                    act.wait_ge(S.sem("gather_mm"), q * 2 + (a + 1))
                    post(copy(hgT[:, 4 * a:4 * a + 4, :], PS[:, 2 + a, :].rearrange("p (k n) -> p k n", k=4)), "gathered")

            def transposed(q, c):
                act.wait_ge(S.sem("eactT_mm"), q * EC + (c + 1))
                post(copy(eactT[:, 4 * c:4 * c + 4, :], PS[:, 6, :].rearrange("p (k n) -> p k n", k=4)), "eactT_copied")

            def expert_pass(q):
                for c in range(EC):
                    act.wait_ge(S.sem("moe_unit"), q * EU + (SLOTS + 4 * c + 2))
                    if c != 1:
                        act.wait_ge(S.sem("eact"), q * EC + max(c - 1, 0))
                    post(act.activation(esilu[c % 2], PS[:, 2 * (c % 2), :], ACT.Silu), "esilu")
                    if c:
                        transposed(q, c - 1)
                gathered(q + 1)
                transposed(q, EC - 1)
                act.wait_ge(S.sem("back_mm"), q + 1)
                post(copy(backT, PS[:, 7, 0:T]), "back_copied")
                act.wait_ge(S.sem("moe_unit"), q * EU + (SLOTS + EU))
                post(copy(yg[:, 0:512], PS[:, 4, :]), "yg_low")

            act.wait_ge(dma_sems["const_loaded"], 16)
            act.wait_ge(dma_sems["x_loaded"], 48)
            for l in range(L):
                S.layer = l
                norm_root("mix")
                in_evacuation(l)
                value_copies(l)
                prompt_attention(l)
                sample_attention(l, "sb")
                sample_attention(l, "mo")
                convolution(l)
                dilated_sample(l)
                delta(l)
                gates(l)
                norm_root("ffn")
                if l == 0:
                    feed_forward("f", FB)
            for t in range(3):
                n = gdn_rows(t)
                act.wait_ge(S.sem("route_in"), t + 1)
                post(act.activation(toks[0:n, t, 5:6], toks[0:n, t, 4:5], ACT.Exp), "route_exp")
            for i in range(6):
                t, a = i // 2, i % 2
                n = gdn_rows(t)
                act.wait_ge(S.sem("htok_mm"), i + 1)
                post(copy(htok[0:n, t, 512 * a:512 * a + 512], PS[0:n, i, :]), "htok_copied")
            gathered(0)
            with act.Fori(0, NEXP) as e:
                expert_pass(e)
            act.wait_ge(S.sem("plan_made"), 1)
            extra = act.value_load(plani[0:1, EXTRA:EXTRA + 1], min_val=0, max_val=EXTRA)
            with act.Fori(0, EXTRA) as x:
                with act.If(x < extra):
                    expert_pass(x + NEXP)
            norm_root("fin")

        @block.vector
        def _(dve):
            chain = Chain(dve, steps["dve"])
            step = chain.step
            AUNITS = attention_units()

            def tt(out, a, b, op):
                return dve.tensor_tensor(out, a, b, op)

            def ts(out, a, s1, s2, op0, op1=ALU.bypass):
                if s2 is None:
                    return dve.tensor_scalar(out, a, s1, None, op0)
                return dve.tensor_scalar(out, a, s1, s2, op0, op1)

            def stt(out, a, s, b, op0, op1):
                return dve.scalar_tensor_tensor(out=out, in0=a, scalar=s, in1=b, op0=op0, op1=op1)

            def square(k):
                post(tt(hT[:, k, :], xT[:, k, :], xT[:, k, :], ALU.mult), "norm_squares")

            def norm(tag, col, l):
                if tag == "fin" or (tag == "mix" and l == 0):
                    for k in range(KD):
                        square(k)
                wait(dve, "norm_sum", NORM[tag])
                post(ts(rstd[:, :], PS[:, 7, 0:T], 1.0 / D, EPS, ALU.mult, ALU.add), "norm_mean")
                wait(dve, "norm_root", NORM[tag])
                step(dve.reciprocal(rstd[:, :], rstd[:, :]))
                for k in range(KD):
                    ins = stt(hT[:, k, :], xT[:, k, :], par[:, l, col + k:col + k + 1], rstd[:, :], ALU.mult, ALU.mult)
                    post(ins, "norm_h")

            def bias_tables():
                dve.wait_ge(dma_sems["const_loaded"], 16)
                dve.wait_ge(dma_sems["setup_loaded"], 16)
                wait(dve, "tables_mm", 1)

                def t(name, rows=P):
                    return setup[0:rows, sat[name][0]:sat[name][1]]
                masks = t("pr_mask").rearrange("p (m n) -> p m n", m=4)
                for h in range(10):
                    wait(dve, "table_mm", h + 1)
                    post(tt(prompt_bias[:, h, :], PS[:, (0, 1, 7)[h % 3], :], masks[:, 0 if h < 4 else 1 + (h - 4) // 2, :],
                            ALU.add), "table_sum")
                hot = PS[:, 2:5, :].rearrange("p a b -> p (a b)")
                dve.tensor_copy(mo_bias[:, 0:PAST], hot[:, 0:PAST])
                tt(mo_bias[:, PAST:SW], hot[:, PAST:SW], t("mo_new"), ALU.add)
                post(tt(di_bias[:, :], PS[0:64, 5:7, :].rearrange("p a b -> p (a b)")[:, 0:DW], t("di_sample", 64), ALU.add),
                     "tables_read")
                dve.wait_ge(S.sem("tables_read"), 1)

            def prompt_attention(l):
                dve.wait_ge(dma_sems["bias_loaded"], 32 * (l + 1))
                subs = 0
                done = []
                for u in AUNITS:
                    subs += len(u[2])
                    done.append(subs)

                def sc(u, c):
                    return small[:, 6 * u + c:6 * u + c + 2]

                def first(u):
                    kind, h, parts, _ = AUNITS[u]
                    A = wkA[u % 2]
                    n = len(parts)
                    if u >= 2:
                        wait(dve, "at_pv_sub", done[u - 2])
                    wait(dve, "at_qk", u + 1)
                    b0 = score_banks(u)[0]
                    if kind == "sb":
                        post(stt(A[:, 0:512], PS[:, b0, :], SCALE, cc("sb_prompt"), ALU.mult, ALU.add), "at_s")
                        return
                    bias = prompt_bias[:, h:h + 1, :] if kind == "mo" else prompt_bias[:, 4 + h:9 + h:2, :]
                    post(stt(A.rearrange("p (g n) -> p g n", g=3)[:, 0:n, :], PS[:, b0:b0 + n, :], SCALE, bias,
                             ALU.mult, ALU.add), "at_s")
                    wait(dve, "at_s", u + 1)
                    w = A.rearrange("p (g t k) -> p t g k", g=3, t=2)[:, :, 0:n, :]
                    step(dve.tensor_reduce(sc(u, 4), w, AX.XY, ALU.max))
                    post(ts(sc(u, 0), sc(u, 4), -1.0, None, ALU.mult), "at_nm")

                def second(u):
                    kind, h, parts, _ = AUNITS[u]
                    A, B, R = wkA[u % 2], wkB[u % 2], wkR[u % 2]
                    if kind == "sb":
                        wait(dve, "sb_soft", u + 1)
                        step(stt(B[:, 0:512], A[:, 0:512], 0.0, B[:, 0:512], ALU.max, ALU.add))
                        suffix_sums(R, B, ((0, TP), (TP, 2 * TP)), P)
                        post(tt(A[:, 0:512], A[:, 0:512], R[:, 0:512], ALU.subtract), "sb_r")
                        return
                    wait(dve, "at_e", u - 3)
                    step(dve.reciprocal(sc(u, 4), sc(u, 2)))
                    w = A.rearrange("p (g t k) -> p t g k", g=3, t=2)[:, :, 0:len(parts), :]
                    for t in range(2):
                        ins = ts(w[:, t], w[:, t], small[:, 6 * u + 4 + t:6 * u + 5 + t], None, ALU.mult)
                    post(ins, "md_p")

                def third(u):
                    _, h, parts, ob = AUNITS[u]
                    hf = half(parts[0][2])
                    wait(dve, "at_pv_sub", done[u])
                    post(dve.tensor_copy(oT[hf, ob, 0:TP], PS[hf, u % 2, 0:TP]), "at_o")

                n = len(AUNITS)
                for v in range(n + 2):
                    if v < n:
                        first(v)
                    if 1 <= v <= n:
                        second(v - 1)
                    if v >= 2:
                        third(v - 2)

            def suffix_sums(out, a, spans, rows):
                for lo, hi in spans:
                    o, x = (y[:, lo:hi][:, ::-1] for y in (out, a))
                    ins = dve.tensor_tensor_scan(o, cc("ones", rows, 1).to_broadcast([rows, hi - lo]), x, 0.0,
                                                 ALU.mult, ALU.add)
                step(ins)

            def sample_queries(l, kind):
                if kind == "sb":
                    wait(dve, "q_zeroed", 1)
                qb = {"sb": SBQ, "mo": MQ}[kind]
                for hp in range(2):
                    for hf in range(2):
                        q = projT[half(hf), qb + hp, TP:T].rearrange("p (b q) -> p b q", q=TQ)
                        dve.tensor_copy(qbd.rearrange("p (b x) -> p b x", x=272)[
                            half(hf), :, hp * 136 + hf * 4:hp * 136 + hf * 4 + TQ], q)
                        c = (2 * hp + hf) * 4
                        ins = dve.tensor_copy(qall[half(hf), hp, :].rearrange("p (b x) -> p b x", x=16)[:, :, c:c + TQ], q)
                post(ins, f"s{kind}_q")

            def sample_output(kind, ob):
                for j in range(4):
                    wait(dve, f"s{kind}_v", 2 * j + 2)
                    post(dve.tensor_copy(so[:, 512 * j:512 * j + 512], PS[0:16, 1 + j, :]), f"s{kind}_out")
                wait(dve, f"s{kind}_outT", 1)
                src = PS[:, 1, 0:256].rearrange("p (b a x) -> p b a x", b=NS, a=2)
                for a in range(2):
                    for hf in range(2):
                        col = (2 * a + hf) * TQ
                        step(dve.tensor_copy(oT[half(hf), ob + a, TP:T].rearrange("p (b q) -> p b q", q=TQ),
                                             src[half(hf), :, a, col:col + TQ]))

            def softmax(A, rows, kind):
                step(dve.tensor_reduce(small[0:rows, 62:63], A, AX.X, ALU.max))
                post(ts(small[0:rows, 60:61], small[0:rows, 62:63], -1.0, None, ALU.mult), f"s{kind}_nm")
                wait(dve, f"s{kind}_e", 1)
                step(dve.reciprocal(small[0:rows, 62:63], small[0:rows, 61:62]))
                post(ts(A, A, small[0:rows, 62:63], None, ALU.mult), f"s{kind}_p")

            def sample_attention(l, kind):
                if kind == "sb":
                    sample_queries(l, "sb")
                A, B, R = sA, sB, sR
                scores = PS[:, 2:5, :].rearrange("p a b -> p (a b)")[:, 0:SW]
                wait(dve, f"s{kind}_qk", 1)
                if kind == "sb":
                    ts(A[:, 0:PAST], scores[:, 0:PAST], SCALE, None, ALU.mult)
                    post(stt(A[:, PAST:SW], scores[:, PAST:SW], SCALE, cc("sb_new"), ALU.mult, ALU.add), "ssb_s")
                    wait(dve, "ssb_soft", 1)
                    step(stt(B, A, 0.0, B, ALU.max, ALU.add))
                    suffix_sums(R, B, ((0, SW),), P)
                    post(tt(A, A, R, ALU.subtract), "ssb_r")
                    sample_queries(l, "mo")
                    sample_output("sb", OSB)
                    return
                step(ts(A, scores, SCALE, None, ALU.mult))
                g = A[:, 0:PAST].rearrange("p (n k) -> p n k", n=4)
                step(dve.tensor_reduce(small[:, 0:4], g, AX.X, ALU.add))
                step(dve.tensor_reduce(small[:, 4:5], small[:, 0:4], AX.X, ALU.min))
                step(ts(small[:, 8:12], small[:, 0:4], small[:, 4:5], None, ALU.is_le))
                step(tt(small[:, 8:12], small[:, 8:12], cc("rank"), ALU.mult))
                step(dve.tensor_reduce(small[:, 5:6], small[:, 8:12], AX.X, ALU.max))
                step(ts(small[:, 8:12], small[:, 8:12], small[:, 5:6], NEG, ALU.is_equal, ALU.mult))
                step(tt(A, A, mo_bias[:, :], ALU.add))
                step(tt(g, g, small[:, 8:12].unsqueeze(2).to_broadcast([P, 4, 256]), ALU.add))
                softmax(A, P, "mo")
                convolution(l)
                sample_output("mo", OMO)

            def dilated_sample(l):
                wait(dve, "dq_zeroed", 1)
                for g in range(3):
                    for hf in range(2):
                        q = projT[half(hf), DQ + g, TP:T].rearrange("p (b q) -> p b q", q=TQ)
                        dve.tensor_copy(dqbd.rearrange("p (b x) -> p b x", x=200)[
                            half(hf), :, g * 64 + hf * 4:g * 64 + hf * 4 + TQ], q)
                        ins = dve.tensor_copy(dqall[half(hf), g, :].rearrange("p (b x) -> p b x", x=8)[:, :, hf * 4:hf * 4 + TQ], q)
                post(ins, "sdi_q")
                A = sA[0:64, 0:DW]
                norm_qk()
                wait(dve, "sdi_qk", 1)
                step(stt(A, PS[0:64, 2:4, :].rearrange("p a b -> p (a b)")[:, 0:DW], SCALE, di_bias[:, :], ALU.mult, ALU.add))
                softmax(A, 64, "di")
                wait(dve, "sdi_v", 1)
                post(dve.tensor_copy(so[0:8, 0:1024].rearrange("p (a n) -> p a n", a=2), PS[0:8, 1:3, :]), "sdi_out")
                wait(dve, "sdi_outT", 1)
                for hf in range(2):
                    src = PS[half(hf), 1, 0:64].rearrange("p (b x) -> p b x", b=NS)[:, :, hf * 4:hf * 4 + TQ]
                    post(dve.tensor_copy(oT[half(hf), ODI, TP:T].rearrange("p (b q) -> p b q", q=TQ), src), "sdi_read")
                wait(dve, "sdi_read", 2)

            def convolution(l):
                def w(f, i):
                    return par[:, l, PCONV + 4 * f + i:PCONV + 4 * f + i + 1]
                dve.wait_ge(dma_sems["state_loaded"], 32 * (l + 1))
                dve.wait_ge(dma_sems["rows_stored"], 16 * 3 * (l + 1))
                dve.tensor_copy(conv_out[:, :, 0:3], projT[:, GQ:GQ + 6, TP - 3:TP])
                step(dve.tensor_copy(sconv[:, :, :, 3:7], projT[:, GQ:GQ + 6, TP:T].rearrange("p f (b q) -> p f b q", q=TQ)))
                post(dve.tensor_copy(conv_out[:, :, 3:].rearrange("p f (b q) -> p f b q", q=3), sconv[:, :, :, 4:7]),
                     "conv_state")
                for i in (3, 2, 1, 0):
                    d = 3 - i
                    for f in range(6):
                        y, x = cT[:, f, 0:TP], projT[:, GQ + f, 0:TP]
                        ys = cT[:, f, TP:T].rearrange("p (b q) -> p b q", q=TQ)
                        xs = sconv[:, f, :, i:i + TQ]
                        if i == 3:
                            ts(y, x, w(f, i), None, ALU.mult)
                            ins = ts(ys, xs, w(f, i), None, ALU.mult)
                        else:
                            stt(y[:, d:], x[:, 0:TP - d], w(f, i), y[:, d:], ALU.mult, ALU.add)
                            ins = stt(ys, xs, w(f, i), ys, ALU.mult, ALU.add)
                    if i:
                        step(ins)
                    else:
                        post(ins, "conv_y")

                post(ts(abw[0:4, :], projT[0:4, AB, :], par[0:4, l, PDTB:PDTB + 1], None, ALU.add), "ab_in")
                wait(dve, "conv_silu", 1)
                sq = wk[:, 0, 0:4 * T].rearrange("p (a n) -> p a n", a=4)
                post(tt(sq, cT[:, 0:4, :], cT[:, 0:4, :], ALU.mult), "conv_sq")
                wait(dve, "ab_soft", 1)
                step(stt(abT[0:4, :], abw[0:4, :], 0.0, abT[0:4, :], ALU.max, ALU.add))
                post(ts(abT[0:4, :], abT[0:4, :], negA[0:4, :], -1.0, ALU.mult, ALU.mult), "ab_done")

            def norm_qk():
                rs = wk[:, 0, 4 * T:8 * T].rearrange("p (a n) -> p a n", a=4)
                wait(dve, "conv_sum", 1)
                post(ts(rs, PS[:, 4:8, 0:T], EPS, None, ALU.add), "conv_ms")
                wait(dve, "conv_root", 1)
                step(dve.reciprocal(rs, rs))
                stt(cT[:, 0:2, :], cT[:, 0:2, :], SCALE, rs[:, 0:2, :], ALU.mult, ALU.mult)
                post(tt(cT[:, 2:4, :], cT[:, 2:4, :], rs[:, 2:4, :], ALU.mult), "conv_done")

            def delta(l):
                for c in range(3):
                    n = gdn_rows(c)
                    wait(dve, "gtok_mm", c + 1)
                    dve.tensor_copy(gsc[0:n, c, 0:4], PS[0:n, 2 * c + 1, 0:4])
                    post(dve.tensor_copy(gsc[0:n, c, 4:8], PS[0:n, 2 * c + 1, 32:36]), "gsc_g")
                for c in range(3):
                    n = gdn_rows(c)
                    wait(dve, "gsc_g", c + 1)
                    for slot, table, col in ((0, "seq_upto" if c == 2 else "upto", 0), (1, "ident", 4)):
                        ins = tt(gwork[c][0:n, slot, 0:4 * n].rearrange("p (h n) -> p h n", h=4),
                                 cc(table, n, n).unsqueeze(1).to_broadcast([n, 4, n]),
                                 gsc[0:n, c, col:col + 4].unsqueeze(2).to_broadcast([n, 4, n]), ALU.mult)
                    post(ins, "gbc_rhs")
                for c in range(3):
                    n = gdn_rows(c)
                    wait(dve, "gcum_mm", 3)
                    dve.tensor_copy(gsc[0:n, c, 8:12], PS[0:n, 6, c * 32:c * 32 + 4])
                    step(dve.tensor_copy(gsc[0:n, c, 12:16], PS[0:n, 6, c * 32 + 8:c * 32 + 12]))
                    post(tt(gsc[0:n, c, 24:28], gsc[0:n, c, 12:16], gsc[0:n, c, 8:12], ALU.subtract), "gsc_in")
                for c in range(3):
                    n = gdn_rows(c)
                    wait(dve, "gbc_mm", c + 1)
                    wait(dve, "g_last", c + 1)
                    gam = gwork[c][0:n, 0, 0:4 * n].rearrange("p (h n) -> p h n", h=4)
                    step(tt(gam, PS[0:n, 2 * c, 0:4 * n].rearrange("p (h n) -> p h n", h=4),
                            gsc[0:n, c, 8:12].unsqueeze(2).to_broadcast([n, 4, n]), ALU.subtract))
                    post(tt(gam, gam, cc("seq_later" if c == 2 else "later", n, n).unsqueeze(1).to_broadcast([n, 4, n]),
                            ALU.add), "gam_in")
                    wait(dve, "g_eg", c + 1)
                    kq = gwork[c][:, 6, 0:4 * n].rearrange("p (a n) -> p a n", a=4)
                    for hf in range(2):
                        def pick(ap):
                            return ap.rearrange("p (a t n) -> p a t n", a=2, t=2)[half(hf), :, hf, :]
                        tt(kq[half(hf), 2:4], cT[half(hf), 0:2, c * P:c * P + n], pick(gwork[c][:, 5, 0:4 * n]), ALU.mult)
                        ins = tt(kq[half(hf), 0:2], cT[half(hf), 2:4, c * P:c * P + n], pick(PS[:, 2 * c + 1, 0:4 * n]), ALU.mult)
                    post(ins, "gkq")
                    wait(dve, "gsc_exp", c + 1)
                    step(tt(gsc[0:n, c, 20:24], gsc[0:n, c, 16:20], gsc[0:n, c, 4:8], ALU.mult))
                    wait(dve, "gtok_copied", c + 1)
                    for dst, src, col in ((1, 1, 4), (2, 0, 20), (0, 0, 28)):
                        ins = tt(gtok[0:n, c, dst, :].rearrange("p (h d) -> p h d", h=4),
                                 gtok[0:n, c, src, :].rearrange("p (h d) -> p h d", h=4),
                                 gsc[0:n, c, col:col + 4].unsqueeze(2).to_broadcast([n, 4, HD]), ALU.mult)
                    post(ins, "gscaled")
                for c in range(3):
                    n = gdn_rows(c)
                    wait(dve, "gm_mm", c + 1)
                    wait(dve, "gam", c + 1)
                    for hf in range(2):
                        def own(slot):
                            return gwork[c][0:n, slot, 0:4 * n].rearrange("p (a t n) -> p a t n", a=2, t=2)[:, :, hf, :]
                        ps = PS[0:n, 2 * c + hf, 0:4 * n].rearrange("p (w a n) -> p w a n", w=2, a=2)
                        tt(own(1), ps[:, 0], own(0), ALU.mult)
                        tt(own(2), ps[:, 1], own(0), ALU.mult)
                    for slot in (3, 4):
                        ins = dve.tensor_copy(gwork[c][0:n, slot, 0:4 * n].rearrange("p (h n) -> p h n", h=4),
                                              cc("ident", n, n).unsqueeze(1).to_broadcast([n, 4, n]))
                    step(ins)
                for s in range(7):
                    for c in range(3):
                        n = gdn_rows(c)
                        if s < gdn_levels(c):
                            if s:
                                wait(dve, f"g{c}_t", s)
                            post(tt(gwork[c][0:n, 0, 0:4 * n].rearrange("p (h n) -> p h n", h=4),
                                    gwork[c][0:n, 1, 0:4 * n].rearrange("p (h n) -> p h n", h=4),
                                    cc(f"lvl{s}", n, n).unsqueeze(1).to_broadcast([n, 4, n]), ALU.mult), f"g{c}_bt")
                    for c in range(3):
                        n = gdn_rows(c)
                        if s < gdn_levels(c):
                            wait(dve, f"g{c}_y", s + 1)
                            tt(gwork[c][0:n, 3, 0:4 * n], gwork[c][0:n, 3, 0:4 * n], PS[0:n, 2 * c, 0:4 * n], ALU.subtract)
                            post(tt(gwork[c][0:n, 4, 0:4 * n], gwork[c][0:n, 4, 0:4 * n], PS[0:n, 2 * c + 1, 0:4 * n],
                                    ALU.subtract), f"g{c}_t")
                for c in range(3):
                    n = gdn_rows(c)
                    wait(dve, "go_mm", c + 1)
                    step(dve.tensor_copy(oT[:, OGD:OGD + 2, c * P:c * P + n],
                                         PS[:, 2 * c, 0:2 * n].rearrange("p (a n) -> p a n", a=2)))
                    if c == 0:
                        wait(dve, "gs_mm", 1)
                        post(dve.tensor_copy(pS[:, :, :], PS[:, 6, 0:P].rearrange("p (a n) -> p a n", a=2)), "pstate")
                        wait(dve, "pstate", 1)
                    if c == 1:
                        wait(dve, "gs_mm", 2)
                        for h in range(4):
                            hf, hp = half(h % 2), h // 2
                            ins = stt(pS[hf, hp, :], pS[hf, hp, :], glast[hf, 1, h:h + 1], PS[hf, 7, hp * HD:(hp + 1) * HD],
                                      ALU.mult, ALU.add)
                        post(ins, "pstate")
                wait(dve, "gvnew", 3)
                dve.wait_ge(dma_sems["rows_stored"], 16 * 3 * (l + 1))
                vm = mergedT.rearrange("p a b -> p (a b)")
                for h in range(4):
                    ins = tt(vm[0:TS, h * 512:(h + 1) * 512].rearrange("p (b d) -> p b d", b=NS),
                             gtok[0:TS, 2, 3, h * HD:(h + 1) * HD].unsqueeze(1).to_broadcast([TS, NS, HD]),
                             cc("seq_of", TS).unsqueeze(2).to_broadcast([TS, NS, HD]), ALU.mult)
                post(ins, "gvm")
                for hf in range(2):
                    gl = glast[half(hf), 2, :].rearrange("p (a t b) -> p a t b", a=2, t=2)[:, :, hf, :]
                    ins = tt(sS[half(hf)], sS[half(hf)], gl.unsqueeze(3).to_broadcast([64, 2, NS, HD]), ALU.mult)
                step(ins)
                wait(dve, "gss_mm", 1)
                post(tt(sS[:, :, :, :], sS[:, :, :, :], PS[:, 6:8, :].rearrange("p a (b d) -> p a b d", b=NS), ALU.add),
                     "sstate")
                post(tt(gosq[:, 0:2, :], oT[:, OGD:OGD + 2, :], oT[:, OGD:OGD + 2, :], ALU.mult), "go_sq")
                wait(dve, "go_sum", 1)
                post(ts(gosq[:, 2:4, :], PS[:, 0:2, 0:T], 1.0 / HD, EPS, ALU.mult, ALU.add), "go_rs")
                wait(dve, "go_root", 1)
                step(dve.reciprocal(gosq[:, 2:4, :], gosq[:, 2:4, :]))
                step(stt(oT[:, OGD:OGD + 2, :], oT[:, OGD:OGD + 2, :], par[:, l, PGN:PGN + 1], gosq[:, 2:4, :],
                         ALU.mult, ALU.mult))
                wait(dve, "z_silu", 1)
                post(tt(oT[:, OGD:OGD + 2, :], oT[:, OGD:OGD + 2, :], cT[:, 4:6, :], ALU.mult), "o_done")
                wait(dve, "o_done", 1)

            def merge(l):
                for m in range(KD):
                    t = wk[:, m % 2, 0:4 * T].rearrange("p (b n) -> p b n", b=4)
                    for br in range(4):
                        n = 4 * m + br
                        wait(dve, "gate_evac", n + 1)
                        wait(dve, "br_mm", n + 1)
                        post(tt(t[:, br, :], PS[:, 2 + n % 4, 0:T], gate(n), ALU.mult), "br_evac")
                    wait(dve, "br_evac", 4 * m + 4)
                    step(tt(t[:, 0:2, :], t[:, 0:2, :], t[:, 2:4, :], ALU.add))
                    post(tt(mergedT[:, m, :], t[:, 0, :], t[:, 1, :], ALU.add), "merged")
                for m in range(KD):
                    wait(dve, "out_mm", m + 1)
                    post(tt(xT[:, m, :], xT[:, m, :], PS[:, m % 2, 0:T], ALU.add), "out_evac")
                    wait(dve, "out_evac", m + 1)
                    square(m)

            def feed_forward(t, nblk):
                for i in range(nblk):
                    dve.wait_ge(S.sem(t + "gu_mm"), 2 * i + 2)
                    dve.wait_ge(S.sem(t + "silu"), i + 1)
                    post(tt(actT[:, i, :], wk[:, 1, (i % 2) * T:(i % 2 + 1) * T], PS[:, (2 * i + 1) % 4, 0:T], ALU.mult),
                         t + "act")
                for m in range(KD):
                    dve.wait_ge(S.sem(t + "dn_mm"), m + 1)
                    post(tt(xT[:, m, :], xT[:, m, :], PS[:, 4 + m % 2, 0:T], ALU.add), t + "dn_evac")
                    dve.wait_ge(S.sem(t + "dn_evac"), m + 1)
                    square(m)

            def places(q):
                for t in range(3):
                    n = gdn_rows(t)
                    col = slot_of[0:n, t, q:q + 1] if isinstance(q, int) else slot_of[0:n, t, bass.ds(q, 1)]
                    ins = ts(perm[0:n, t, :], cc("slot_no", n), col, None, ALU.is_equal)
                post(ins, "perm_made")

            def expert_pass(q):
                for c in range(EC):
                    dve.wait_ge(S.sem("moe_unit"), q * EU + (SLOTS + 4 * c + 4))
                    dve.wait_ge(S.sem("esilu"), q * EC + (c + 1))
                    post(tt(eact[:, 512 * c:512 * c + 512], esilu[c % 2], PS[:, 2 * (c % 2) + 1, :], ALU.mult), "eact")
                    if c == EC - 3:
                        places(q + 1)
                    if c == EC - 2:
                        for t in range(3):
                            n = gdn_rows(t)
                            ins = ts(permw[0:n, t, :], cc("slot_no", n), slot_of[0:n, t, bass.ds(q, 1)],
                                     weight[0:n, t, bass.ds(q, 1)], ALU.is_equal, ALU.mult)
                        post(ins, "permw_made")
                dve.wait_ge(S.sem("moe_unit"), q * EU + (SLOTS + EU))
                post(dve.tensor_copy(yg[:, 512:1024], PS[:, 5, :]), "yg_high")
                dve.wait_ge(S.sem("moe_added"), q * KD)
                for m in range(KD):
                    dve.wait_ge(S.sem("back_sum"), q * KD + (m + 1))
                    post(tt(xT[:, m, :], xT[:, m, :], PS[:, 6 + m % 2, 0:T], ALU.add), "moe_added")

            def routing():
                wait(dve, "router_mm", 1)
                dve.wait_ge(S.sem("slots_zeroed"), 1)
                for t in range(3):
                    n = gdn_rows(t)
                    lg, one, two, c = (rlog[0:n, t, i, :] for i in range(4))

                    def col(i):
                        return toks[0:n, t, i:i + 1]
                    step(dve.tensor_copy(lg, PS[0:n, 6, t * 8:t * 8 + 8]))

                    def pick(out, top, rank):
                        step(dve.tensor_reduce(top, lg, AX.X, ALU.max))
                        step(ts(out, lg, top, None, ALU.is_ge))
                        step(tt(out, out, cc("down", n), ALU.mult))
                        step(dve.tensor_reduce(rank, out, AX.X, ALU.max))
                        step(ts(out, out, rank, None, ALU.is_equal))
                    pick(one, col(0), col(2))
                    step(stt(lg, one, NEG, lg, ALU.mult, ALU.add))
                    pick(two, col(1), col(3))
                    step(tt(lg, one, two, ALU.add))
                    post(tt(col(4), col(1), col(0), ALU.subtract), "route_in")
                    dve.wait_ge(S.sem("route_exp"), t + 1)
                    step(ts(col(6), col(5), 1.0, None, ALU.add))
                    step(dve.reciprocal(col(7), col(6)))
                    step(tt(col(8), col(7), col(5), ALU.mult))
                    step(ts(one, one, col(7), None, ALU.mult))
                    post(stt(c, two, col(8), one, ALU.mult, ALU.add), "chosen")
                dve.wait_ge(S.sem("counted"), 1)
                for t in range(3):
                    n = gdn_rows(t)
                    step(tt(slot_of[0:n, t, 0:NEXP], PS[0:n, 6, 32 + t * 8:40 + t * 8], rlog[0:n, t, 0, :], ALU.mult))
                step(ts(slot_of[:, :, 0:NEXP], slot_of[:, :, 0:NEXP], 1.0, None, ALU.subtract))
                places(0)
                dve.wait_ge(S.sem("chosen"), 3)
                step(dve.tensor_copy(weight[:, :, 0:NEXP], rlog[:, :, 3, :]))
                count, more, upto, before, a, b, hot, num = (tally[:, i, :] for i in range(8))
                step(dve.tensor_copy(count, PS[:, 6, 56:64]))
                step(ts(more, count, CAP + 0.5, None, ALU.is_ge))
                step(stt(more, count, 2 * CAP + 0.5, more, ALU.is_ge, ALU.add))
                step(dve.tensor_tensor_scan(upto, cc("ones", P, 1).to_broadcast([P, NEXP]), more, 0.0, ALU.mult, ALU.add))
                step(tt(before, upto, more, ALU.subtract))
                step(ts(num, cc("down"), -1.0, float(NEXP), ALU.mult, ALU.add))
                far = toks[:, :, 8:16]
                tmp = rlog[:, :, 1, :]
                step(stt(far, before.unsqueeze(1).to_broadcast([P, 3, NEXP]), float(CAP), slot_of[:, :, 0:NEXP],
                         ALU.mult, ALU.add))
                for x in range(EXTRA):
                    step(ts(a, upto, x + 0.5, None, ALU.is_ge))
                    step(ts(b, before, x + 0.5, None, ALU.is_ge))
                    step(tt(hot, a, b, ALU.subtract))
                    step(tt(a, hot, num, ALU.mult))
                    step(dve.tensor_reduce(planf[0:1, x:x + 1], a[0:1, :], AX.X, ALU.add))
                    for src, out in ((far, slot_of), (rlog[:, :, 3, :], weight)):
                        step(tt(tmp, src, hot.unsqueeze(1).to_broadcast([P, 3, NEXP]), ALU.mult))
                        step(dve.tensor_reduce(out[:, :, NEXP + x:NEXP + x + 1], tmp, AX.X, ALU.add))
                    step(ts(slot_of[:, :, NEXP + x:NEXP + x + 1], slot_of[:, :, NEXP + x:NEXP + x + 1],
                            float(CAP * (1 + x)), None, ALU.subtract))
                step(dve.tensor_copy(planf[0:1, EXTRA:EXTRA + 1], upto[0:1, NEXP - 1:NEXP]))
                post(dve.tensor_copy(plani[0:1, 0:EXTRA + 1], planf[0:1, 0:EXTRA + 1]), "plan_made")
                dve.wait_ge(S.sem("plan_made"), 1)

            dve.wait_ge(dma_sems["x_loaded"], 48)
            for l in range(L):
                S.layer = l
                norm("mix", PMIX, l)
                if l == 0:
                    bias_tables()
                prompt_attention(l)
                sample_attention(l, "sb")
                sample_attention(l, "mo")
                dilated_sample(l)
                delta(l)
                merge(l)
                norm("ffn", PFFN, l)
                if l == 0:
                    feed_forward("f", FB)
                    wait(dve, "fdn_evac", KD, 0)
            routing()
            with dve.Fori(0, NEXP) as e:
                expert_pass(e)
            extra = dve.value_load(plani[0:1, EXTRA:EXTRA + 1], min_val=0, max_val=EXTRA)
            with dve.Fori(0, EXTRA) as x:
                with dve.If(x < extra):
                    expert_pass(x + NEXP)
            dve.wait_ge(S.sem("moe_added"), extra * KD + NEXP * KD)
            norm("fin", PFIN, 0)

        @block.gpsimd
        def _(pool):
            step = Chain(pool, steps["pool"]).step
            S.layer = 0
            out = dma_sems["outputs_stored"]
            rows_out = dma_sems["rows_stored"]
            windows = dma_sems["windows_stored"]
            pool.memset(abT[:, :], 0.0)
            pool.memset(nwm[:, :, :], 0.0)
            pool.memset(qall[:, :, :], 0.0)
            pool.memset(dqall[:, :, :], 0.0)
            pool.memset(rlog[:, :, :, :], 0.0)
            post(pool.memset(slot_of[:, :, :], 0.0), "slots_zeroed")
            scratch = A["scratch"]
            wait(pool, "table_sum", 10)
            pool.dma_start(scratch, region[:, :]).then_inc(dma_sems["bias_stored"], 16)
            pool.wait_ge(dma_sems["bias_stored"], 16)
            pool.wait_ge(dma_sems["pages_loaded"], 16)

            def page_halves(l, kinds):
                for n, unit in enumerate(units):
                    if unit[0] in kinds and unit[1] == l:
                        page_half(pool, n, 1)

            for l in range(L):
                S.layer = l
                if l:
                    wait(pool, "o_done", 1, l - 1)
                    pool.wait_ge(out, stored_after(l - 1))
                for t in range(2):
                    pool.dma_start(prompt_bias[:, :, t * TP:(t + 1) * TP],
                                   bass.AP(scratch.tensor, TP - 1 - t * P, [[5120 - 1, P], [2 * TP, 10], [1, TP]])
                                   ).then_inc(dma_sems["bias_loaded"], 16)
                pool.dma_start(sconv[:, :, :, 0:3], A["conv"][l]).then_inc(dma_sems["state_loaded"], 16)
                wait(pool, "in_evac", NBLK)
                for i, (a, b) in enumerate(((SBK, GZ), (MK, DQ), (DK, AB))):
                    pool.dma_start(A["rows"][l, :, (0, 10, 14)[i]:(0, 10, 14)[i] + b - a, :], projT[:, a:b, :]
                                   ).then_inc(rows_out, 16)
                for name, keep in (("dk0", 128), ("dk1", 512)):
                    pool.dma_start(A[name + "_out"][l], A[name][l, :, :, TQ:keep]).then_inc(windows, 16)
                pool.dma_start(A["dk2a_out"][l], A["dk2"][l, :, :, 4:16, :]).then_inc(windows, 16)
                pool.dma_start(A["dk2b_out"][l], A["dk2"][l, :, :, 0:4, 1:64]).then_inc(windows, 16)
                for name, keep in (("dv0", 128), ("dv1", 512), ("dv2", 1024)):
                    pool.dma_start(A[name + "_out"][l].rearrange("t b d -> t (b d)"),
                                   A[name][l, TQ:keep].rearrange("t b d -> t (b d)")).then_inc(windows, 16)
                wait(pool, "at_o", 10)
                post(pool.memset(qbd, 0.0), "q_zeroed")
                pool.dma_start(sS, A["S"][l]).then_inc(dma_sems["state_loaded"], 16)
                page_halves(l, PAGED[0:3])
                wait(pool, "smo_qk", 1)
                post(pool.memset(dqbd, 0.0), "dq_zeroed")
                page_halves(l, PAGED[3:])
                wait(pool, "conv_state", 1)
                pool.dma_start(A["conv_out"][l], conv_out[:, :, :]).then_inc(out, 16)
                wait(pool, "pstate", 2)
                pool.dma_start(A["pS_out"][l], pS[:, :, :]).then_inc(out, 16)
                wait(pool, "sstate", 1)
                pool.dma_start(A["sS_out"][l], sS).then_inc(out, 16)
            wait(pool, "norm_h", KD * NORM["fin"])
            pool.dma_start(A["y_out"], hT[:, :, :]).then_inc(out, 16)
            pool.wait_ge(out, stored_after(L - 1) + 16)
            pool.wait_ge(rows_out, 16 * 3 * L)
            pool.wait_ge(windows, 16 * 7 * L)

        return {k: (v[0] if v[1] else 0) for k, v in S.count.items()}


def stored_after(l):
    return 16 * 3 * (l + 1)


def laid_out(x):
    f = {k: np.asarray(v) for k, v in x.items()}

    def tr(a, *axes):
        return np.ascontiguousarray(np.transpose(a, axes))

    def feature_blocks(v):
        return np.swapaxes(v.reshape(v.shape[:-1] + (-1, P)), -1, -2)

    o = {}
    tok = np.concatenate([f["x_prompt"].reshape(TP, D), f["x_sample"].reshape(TS, D)])
    o["x"] = tr(tok.reshape(T, KD, P), 2, 1, 0)
    w = f["w_in"]
    zero = np.zeros((L, D, 28), np.float32)
    cols = np.concatenate([w[:, :, 0:1536], w[:, :, 1536:1792], w[:, :, 1800:2568], w[:, :, 2568:3720],
                           w[:, :, 1792:1796], zero, w[:, :, 1796:1800], zero, np.zeros((L, D, 64), np.float32)], 2)
    o["in"] = tr(cols.reshape(L, KD, P, NBLK // 2, 2, P), 0, 3, 2, 4, 1, 5).reshape(L, NBLK // 2, P, SLOT)
    g = w[:, :, 3720:].reshape(L, KD, P, 2, 2, KD, P)
    o["gate"] = tr(g, 0, 5, 3, 2, 4, 1, 6).reshape(L, 2 * KD, P, SLOT)
    br = np.concatenate([f["w_br_sb"], f["w_br_gdn"], f["w_br_moba"], f["w_br_dil"]], 1)
    o["br"] = tr(br.reshape(L, 7, P, KD // 2, 2, P), 0, 3, 2, 4, 1, 5).reshape(L, KD // 2, P, 14 * P)
    o["out"] = tr(f["w_out"].reshape(L, KD, P, KD // 2, 2, P), 0, 3, 2, 4, 1, 5).reshape(L, KD // 2, P, SLOT)

    def gate_up(wg, wu):
        both = np.stack([wg, wu], -3).reshape((-1, 2, KD, P, wg.shape[-1] // P, P))
        return tr(both, 0, 4, 3, 1, 2, 5).reshape(-1, P, SLOT)

    def down(wd):
        nb = wd.shape[-2] // P
        blocks = wd.reshape(-1, nb, P, KD, P).transpose(0, 3, 1, 2, 4).reshape(-1, 16, P, P)
        return tr(blocks, 0, 2, 1, 3).reshape(-1, P, SLOT)
    o["fgu"], o["fdn"] = gate_up(f["ffn_w_gate"], f["ffn_w_up"]), down(f["ffn_w_down"])
    moe = np.empty((NEXP, EU, P, SLOT), np.float32)
    for i, name in enumerate(("moe_w_gate", "moe_w_up")):
        w = f[name][0].reshape(NEXP, 2, 4, P, EC, 512).transpose(0, 4, 1, 3, 2, 5)
        moe[:, 0:4 * EC].reshape(NEXP, EC, 2, 2, P, 4, 512)[:, :, i] = w
    moe[:, 4 * EC:] = f["moe_w_down"][0].reshape(NEXP, EB // 2, 2, P, D).transpose(0, 1, 3, 2, 4).reshape(
        NEXP, EB // 2, P, SLOT)
    o["moe"] = moe.reshape(-1, P, SLOT)
    o["router"] = tr(f["moe_router"][0].reshape(KD, P, NEXP), 1, 0, 2)
    for kind, name in (("sb", "cache_sb_kv"), ("mo", "cache_moba_kv")):
        c = f[name].reshape(-1, PAGE, 2, 256)
        o[kind + "k"] = tr(c[:, :, 0].reshape(-1, PAGE, 2, P), 0, 3, 2, 1).reshape(-1, P, 256)
        o[kind + "v"] = np.ascontiguousarray(c[:, :, 1])
    for g in range(3):
        c = f[f"cache_dil_kv_{g}"].reshape(L, NS, -1, 2, P)
        o[f"dk{g}"] = tr(c[:, :, :, 0], 0, 3, 1, 2)
        o[f"dv{g}"] = tr(c[:, :, :, 1], 0, 2, 1, 3)
    o["dk2"] = tr(o["dk2"].reshape(L, P, NS, 64, 16), 0, 1, 2, 4, 3)
    o["conv"] = tr(f["state_gdn_conv"].reshape(L, NS, 3, 6, P), 0, 4, 3, 1, 2)
    o["S"] = tr(f["state_gdn_S"].reshape(L, NS, 2, 2, HD, HD), 0, 3, 4, 2, 1, 5).reshape(L, P, 2, NS, HD)
    par = np.zeros((P, L, NPAR), np.float32)
    par[:, :, PMIX:PMIX + 8] = feature_blocks(f["norm_mix"]).transpose(1, 0, 2)
    par[:, :, PFFN:PFFN + 8] = feature_blocks(f["norm_ffn"]).transpose(1, 0, 2)
    par[:, :, PCONV:PCONV + 24] = f["gdn_conv_w"].reshape(L, 4, 6, P).transpose(3, 0, 2, 1).reshape(P, L, 24)
    par[:, :, PGN] = np.concatenate([f["gdn_norm_w"]] * 2, 1).T
    par[0:4, :, PALOG] = f["gdn_a_log"].T
    par[0:4, :, PDTB] = f["gdn_dt_bias"].T
    par[:, :, PFIN:PFIN + 8] = feature_blocks(f["final_norm"])[:, None, :]
    o["par"] = par
    rel = f["rel_bias"]
    mo = np.zeros((TQ, BUCKETS, NS, 4, TQ), np.float32)
    di = np.zeros((TQ, BUCKETS, 3, NS, 2, TQ), np.float32)
    for t in range(TQ):
        mo[t, :, :, :, t] = rel[:, None, 0:4]
        di[t, :, :, :, :, t] = rel[:, 4:10].reshape(BUCKETS, 3, 1, 2)
    o["pages"] = f["page_table"].astype(np.int32).reshape(1, NS * NPG)
    C = tables()
    o["const"] = np.concatenate([C[n] for n in RESIDENT], 1)
    o["setup"] = np.concatenate([C[n] for n in SETUP] + [np.pad(rel, ((0, P - BUCKETS), (0, 0))), mo.reshape(P, P),
                                                         di.reshape(P, 3 * 64)], 1)
    return o


OUTPUTS = {
    "y_out": (P, KD, T), "rows": (L, P, 20, T), "dk0_out": (L, P, NS, 124), "dk1_out": (L, P, NS, 508),
    "dk2a_out": (L, P, NS, 12, 64), "dk2b_out": (L, P, NS, 4, 63), "dv0_out": (L, 124, NS, P),
    "dv1_out": (L, 508, NS, P), "dv2_out": (L, 1020, NS, P), "conv_out": (L, P, 6, 27), "pS_out": (L, P, 2, HD),
    "sS_out": (L, P, 2, NS, HD),
}


def given_back(r):
    y = r["y_out"].transpose(2, 1, 0).reshape(T, D)
    rows = r["rows"].transpose(0, 3, 2, 1)

    def kv(first, n, heads):
        a = rows[:, :, first:first + 2 * n].reshape(L, T, 2, heads, HD)
        return a[:, None, :TP], a[:, TP:].reshape(L, NS, TQ, 2, heads, HD)
    p_sb, s_sb = kv(0, 2, 4)
    p_mo, s_mo = kv(10, 2, 4)
    dil = rows[:, :, 14:20].reshape(L, T, 2, 3, 2, HD)
    conv = r["conv_out"].transpose(0, 3, 2, 1).reshape(L, 27, 768)
    p_conv, s_conv = conv[:, None, 0:3], conv[:, 3:].reshape(L, NS, 3, 768)
    pS = r["pS_out"].reshape(L, 2, HD, 2, HD).transpose(0, 3, 1, 2, 4).reshape(L, 1, 4, HD, HD)
    sS = r["sS_out"].reshape(L, 2, HD, 2, NS, HD).transpose(0, 4, 3, 1, 2, 5).reshape(L, NS, 4, HD, HD)
    out = [y[:TP].reshape(1, TP, D), y[TP:].reshape(NS, TQ, D), p_sb, s_sb, p_mo, s_mo, p_conv, s_conv, pS, sS]
    k2 = np.zeros((L, P, NS, 64, 16), np.float32)
    k2[..., 0:12] = r["dk2a_out"].transpose(0, 1, 2, 4, 3)
    k2[:, :, :, 0:63, 12:16] = r["dk2b_out"].transpose(0, 1, 2, 4, 3)
    ks = [r["dk0_out"], r["dk1_out"], k2.reshape(L, P, NS, PAST)[..., 0:PAST - TQ]]
    for g in range(3):
        keep = min(DIL[g][0], TP)
        out.append(dil[:, None, TP - keep:TP, :, g])
        old = np.stack([ks[g].transpose(0, 2, 3, 1), r[f"dv{g}_out"].transpose(0, 2, 1, 3)], 3)
        old = old.reshape(L, NS, -1, 2, 2, HD)
        out.append(np.concatenate([old, dil[:, TP:, :, g].reshape(L, NS, TQ, 2, 2, HD)], 2))
    return tuple(np.ascontiguousarray(a) for a in out)


def declare(nc, arrays):
    A = {}
    for n, a in arrays.items():
        A[n] = nc.dram_tensor("in_" + n, a.shape, mybir.dt.from_np(a.dtype), kind="ExternalInput").ap()
    for n, shape in OUTPUTS.items():
        A[n] = nc.dram_tensor("out_" + n, shape, F32, kind="ExternalOutput").ap()
    A["scratch"] = nc.dram_tensor("bias_scratch", (P, 5120), F32, kind="Internal").ap()
    A["n_phys"] = arrays["sbk"].shape[0] // L
    return A


def kernel(**inputs):
    import concourse.bacc as bacc
    from concourse.bass_utils import run_bass_kernel_spmd as run

    arrays = laid_out(inputs)
    count = bacc.Bacc("TRN2", target_bir_lowering=False, num_devices=1)
    per = program(count, declare(count, arrays), {})
    nc = bacc.Bacc("TRN2", target_bir_lowering=False, num_devices=1)
    program(nc, declare(nc, arrays), per)
    r = run(nc, [{"in_" + n: a for n, a in arrays.items()}], core_ids=[0]).results[0]
    return given_back({n: np.asarray(r["out_" + n]) for n in OUTPUTS})
```
